# Optimizing a Trainium2 kernel written in Bass

```python
import jax, jax.numpy as jnp
from jax import lax
import numpy as np

D_MODEL = 1024
BATCH = 1
SEQ = 256
DEPTH = 1

CTX_LEN = 256
GRID_W = 64
D_MIX = 1024
HEAD_DIM = 64
N_Q_HEADS = 8
N_KV_HEADS = 2
Q_PER_KV = N_Q_HEADS // N_KV_HEADS
D_ATTN = N_Q_HEADS * HEAD_DIM
D_KV = N_KV_HEADS * HEAD_DIM
N_GM_GROUPS = 8
GM_GROUP_DIM = 64
D_GM = N_GM_GROUPS * GM_GROUP_DIM
CHUNK = 128
Q_BLOCK = 128
D_IN = D_ATTN + 2 * D_KV + 2 * D_GM
ROPE_THETA = 10000.0
N_EXPERTS = 16
CAPACITY_FACTOR = 2
EXPERT_FF = 2048
EPS = 1e-6


def rmsnorm(x, g):
    xf = x.astype(jnp.float32)
    y = xf * lax.rsqrt(jnp.mean(xf * xf, axis=-1, keepdims=True) + EPS)
    return (y * g.astype(jnp.float32)).astype(x.dtype)

def adaln(cvec, w_mod, b_mod):
    m = jax.nn.silu(cvec) @ w_mod + b_mod
    return jnp.split(m, 6, axis=-1)

def axial_rope(row, col):
    n_freq = HEAD_DIM // 4
    inv = ROPE_THETA ** (-jnp.arange(n_freq, dtype=jnp.float32) / n_freq)
    ang = jnp.concatenate([row[:, None].astype(jnp.float32) * inv,
                           col[:, None].astype(jnp.float32) * inv], axis=-1)
    return jnp.cos(ang), jnp.sin(ang)

def apply_rope(x, cos, sin):
    shape = (cos.shape[0],) + (1,) * (x.ndim - 3) + (cos.shape[-1],)
    cos = cos.reshape(shape).astype(x.dtype)
    sin = sin.reshape(shape).astype(x.dtype)
    x1, x2 = jnp.split(x, 2, axis=-1)
    return jnp.concatenate([x1 * cos - x2 * sin, x1 * sin + x2 * cos], axis=-1)

def modulate(x, g, shift, scale):
    return rmsnorm(x, g) * (1 + scale) + shift

def split_in_proj(w_in):
    return jnp.split(w_in, [D_ATTN, D_ATTN + 2 * D_KV], axis=1)

def queries(h, w_q, q_gain):
    b, n = h.shape[:2]
    return rmsnorm((h @ w_q).reshape(b, n, N_KV_HEADS, Q_PER_KV, HEAD_DIM), q_gain)

def keys_values(h, w_kv, k_gain):
    b, n = h.shape[:2]
    k, v = jnp.split(h @ w_kv, 2, axis=-1)
    k = rmsnorm(k.reshape(b, n, N_KV_HEADS, HEAD_DIM), k_gain)
    return k, v.reshape(b, n, N_KV_HEADS, HEAD_DIM)

def gqa_attend(q, k, v):
    b, nq = q.shape[:2]
    scale = HEAD_DIM ** -0.5

    def block(qb):
        s = jnp.einsum('bqkgd,bskd->bkgqs', qb, k).astype(jnp.float32) * scale
        p = jax.nn.softmax(s, axis=-1).astype(v.dtype)
        return jnp.einsum('bkgqs,bskd->bqkgd', p, v)

    nb = nq // Q_BLOCK
    qb = jnp.moveaxis(q.reshape(b, nb, Q_BLOCK, N_KV_HEADS, Q_PER_KV, HEAD_DIM), 1, 0)
    o = lax.map(block, qb)
    return jnp.moveaxis(o, 0, 1).reshape(b, nq, D_ATTN)

def spatial_gating(h, w_gm, v_gain, w_s, b_s):
    b, n = h.shape[:2]
    u, vv = jnp.split(jax.nn.gelu(h @ w_gm, approximate=False), 2, axis=-1)
    vv = rmsnorm(vv, v_gain).reshape(b, n // CHUNK, CHUNK, N_GM_GROUPS, GM_GROUP_DIM)
    mixed = jnp.einsum('gij,bcjgd->bcigd', w_s, vv) + b_s.T[:, :, None]
    return u * mixed.reshape(b, n, D_GM)

def expert_choice_ffn(h, w_router, w1, w3, w2):
    n, d = h.shape[1], h.shape[2]
    cap = CAPACITY_FACTOR * n // N_EXPERTS
    aff = jax.nn.softmax((h @ w_router).astype(jnp.float32), axis=-1)
    gate, idx = lax.top_k(jnp.swapaxes(aff, 1, 2), cap)
    xe = jax.vmap(lambda hb, ib: hb[ib])(h, idx)
    hid = jax.nn.silu(jnp.einsum('becd,edf->becf', xe, w1)) * jnp.einsum('becd,edf->becf', xe, w3)
    ye = jnp.einsum('becf,efd->becd', hid, w2) * gate[..., None].astype(h.dtype)

    def scatter(yb, ib):
        return jnp.zeros((n, d), h.dtype).at[ib.reshape(-1)].add(yb.reshape(-1, d))

    return jax.vmap(scatter)(ye, idx)

def hybrid_layer(xl, xc, c, c_ctx, cos, sin, w_mod, b_mod, g_mix, g_ffn, w_in, q_gain, k_gain,
                 v_gain, w_s, b_s, w_out, w_router, w1, w3, w2, update_ctx):
    sh1, sc1, gt1, sh2, sc2, gt2 = [m[:, None, :] for m in adaln(c, w_mod, b_mod)]
    csh1, csc1, cgt1, csh2, csc2, cgt2 = adaln(c_ctx, w_mod, b_mod)
    w_q, w_kv, w_gm = split_in_proj(w_in)

    hl = modulate(xl, g_mix, sh1, sc1)
    hc = modulate(xc, g_mix, csh1, csc1)
    kc, vc = keys_values(hc, w_kv, k_gain)
    ql = apply_rope(queries(hl, w_q, q_gain), cos, sin)
    kl, vl = keys_values(hl, w_kv, k_gain)
    kl = apply_rope(kl, cos, sin)
    k_all = jnp.concatenate([kl, kc], axis=1)
    v_all = jnp.concatenate([vl, vc], axis=1)
    mix_l = jnp.concatenate([gqa_attend(ql, k_all, v_all),
                             spatial_gating(hl, w_gm, v_gain, w_s, b_s)], axis=-1)
    xl_new = xl + gt1 * (mix_l @ w_out)

    xl_new = xl_new + gt2 * expert_choice_ffn(modulate(xl_new, g_ffn, sh2, sc2), w_router, w1, w3, w2)

    if update_ctx:
        qc = queries(hc, w_q, q_gain)
        mix_c = jnp.concatenate([gqa_attend(qc, kc, vc),
                                 spatial_gating(hc, w_gm, v_gain, w_s, b_s)], axis=-1)
        xc = xc + cgt1 * (mix_c @ w_out)
        xc = xc + cgt2 * expert_choice_ffn(modulate(xc, g_ffn, csh2, csc2), w_router, w1, w3, w2)
    return xl_new, xc

def first_inputs(seed: int = 0) -> dict:
    key = jax.random.key(seed)
    ks = jax.random.split(key, 21)
    f32 = jnp.float32
    L = DEPTH

    def nrm(k, shape, s):
        return jax.random.normal(k, shape, f32) * s

    return {
        "x": nrm(ks[0], (BATCH, SEQ, D_MODEL), 1.0),
        "c": nrm(ks[1], (BATCH, D_MODEL), 1.0),
        "ctx": nrm(ks[2], (BATCH, CTX_LEN, D_MODEL), 1.0),
        "c_ctx": nrm(ks[3], (D_MODEL,), 1.0),
        "w_mod": nrm(ks[4], (L, D_MODEL, 6 * D_MODEL), D_MODEL ** -0.5),
        "b_mod": nrm(ks[5], (L, 6 * D_MODEL), 0.02),
        "g_mix": 1.0 + nrm(ks[6], (L, D_MODEL), 0.02),
        "g_ffn": 1.0 + nrm(ks[7], (L, D_MODEL), 0.02),
        "w_in": nrm(ks[8], (L, D_MODEL, D_IN), D_MODEL ** -0.5),
        "q_gain": 1.0 + nrm(ks[9], (L, HEAD_DIM), 0.02),
        "k_gain": 1.0 + nrm(ks[10], (L, HEAD_DIM), 0.02),
        "v_gain": 1.0 + nrm(ks[11], (L, D_GM), 0.02),
        "w_s": nrm(ks[12], (L, N_GM_GROUPS, CHUNK, CHUNK), CHUNK ** -0.5),
        "b_s": 1.0 + nrm(ks[13], (L, N_GM_GROUPS, CHUNK), 0.02),
        "w_out": nrm(ks[14], (L, D_MIX, D_MODEL), D_MIX ** -0.5),
        "w_router": nrm(ks[15], (L, D_MODEL, N_EXPERTS), D_MODEL ** -0.5),
        "w1": nrm(ks[16], (L, N_EXPERTS, D_MODEL, EXPERT_FF), D_MODEL ** -0.5),
        "w3": nrm(ks[17], (L, N_EXPERTS, D_MODEL, EXPERT_FF), D_MODEL ** -0.5),
        "w2": nrm(ks[18], (L, N_EXPERTS, EXPERT_FF, D_MODEL), EXPERT_FF ** -0.5),
        "g_final": 1.0 + nrm(ks[19], (D_MODEL,), 0.02),
    }

def first_block(x, c, ctx, c_ctx, w_mod, b_mod, g_mix, g_ffn, w_in, q_gain, k_gain, v_gain,
              w_s, b_s, w_out, w_router, w1, w3, w2, g_final):
    n_lat = x.shape[1]
    rows = n_lat // GRID_W
    row = jnp.repeat(jnp.arange(rows), GRID_W)
    col = jnp.tile(jnp.arange(GRID_W), rows)
    cos, sin = axial_rope(row, col)
    xl, xc = x, ctx
    for layer in range(DEPTH):
        xl, xc = hybrid_layer(xl, xc, c, c_ctx, cos, sin, w_mod[layer], b_mod[layer], g_mix[layer],
                              g_ffn[layer], w_in[layer], q_gain[layer], k_gain[layer], v_gain[layer],
                              w_s[layer], b_s[layer], w_out[layer], w_router[layer], w1[layer],
                              w3[layer], w2[layer], update_ctx=layer + 1 < DEPTH)
    return rmsnorm(xl, g_final)


DEPTH_2 = 2

QBLOCK = 128
WINDOW = 128
MLA_HEADS = D_MODEL // 128
MLA_Q_RANK = D_MODEL // 4
MLA_KV_RANK = D_MODEL // 8
MLA_NOPE = 64
MLA_ROPE = 32
MLA_V = 64
SWA_HEADS = D_MODEL // 128
SWA_KV_HEADS = SWA_HEADS // 4
SWA_HEAD_DIM = 64
FOX_HEADS = D_MODEL // 64
FOX_HEAD_DIM = 64
FOX_WIDTH = FOX_HEADS * FOX_HEAD_DIM
FORGET_BIAS_INIT = 2.0

EVEN_WIDTH = MLA_HEADS * MLA_V + SWA_HEADS * SWA_HEAD_DIM
EVEN_SPLITS = (MLA_Q_RANK, MLA_KV_RANK, MLA_ROPE, SWA_HEADS * SWA_HEAD_DIM,
               SWA_KV_HEADS * SWA_HEAD_DIM, SWA_KV_HEADS * SWA_HEAD_DIM, EVEN_WIDTH)
ODD_SPLITS = (FOX_WIDTH, FOX_WIDTH, FOX_WIDTH, FOX_HEADS, FOX_WIDTH)
N_EVEN = (DEPTH_2 + 1) // 2
N_ODD = DEPTH_2 // 2


def rms_norm(x, g):
    xf = x.astype(jnp.float32)
    y = xf * lax.rsqrt(jnp.mean(xf * xf, axis=-1, keepdims=True) + EPS)
    return (y * g.astype(jnp.float32)).astype(x.dtype)

def split_cols(z, sizes):
    idx = [int(v) for v in np.cumsum(sizes)[:-1]]
    return jnp.split(z, idx, axis=-1)

def rope_angles(positions, dim):
    inv_freq = 1.0 / (ROPE_THETA ** (jnp.arange(0, dim, 2, dtype=jnp.float32) / dim))
    return positions.astype(jnp.float32)[..., None] * inv_freq

def apply_rope_2(x, ang):
    cos, sin = jnp.cos(ang), jnp.sin(ang)
    xf = x.astype(jnp.float32)
    x1, x2 = jnp.split(xf, 2, axis=-1)
    return jnp.concatenate([x1 * cos - x2 * sin, x2 * cos + x1 * sin], axis=-1).astype(x.dtype)

def alibi_slopes(n):
    return 2.0 ** (-8.0 * (jnp.arange(n, dtype=jnp.float32) + 1.0) / n)

def causal_block_attention(q, k, v, log_cum=None):
    B, S, H, Dk = q.shape
    Dv = v.shape[-1]
    nb = S // QBLOCK
    scale = Dk ** -0.5
    kpos = jnp.arange(S)
    lc_t = None if log_cum is None else jnp.transpose(log_cum, (0, 2, 1))

    def one_block(i):
        start = i * QBLOCK
        qi = lax.dynamic_slice_in_dim(q, start, QBLOCK, axis=1)
        s = jnp.einsum('bqhd,bkhd->bhqk', qi, k, preferred_element_type=jnp.float32) * scale
        if lc_t is not None:
            ci = lax.dynamic_slice_in_dim(lc_t, start, QBLOCK, axis=2)
            s = s + ci[..., :, None] - lc_t[..., None, :]
        qpos = start + jnp.arange(QBLOCK)
        mask = kpos[None, :] <= qpos[:, None]
        s = jnp.where(mask, s, -jnp.inf)
        p = jax.nn.softmax(s, axis=-1)
        return jnp.einsum('bhqk,bkhd->bqhd', p.astype(v.dtype), v)

    out = lax.map(one_block, jnp.arange(nb))
    return jnp.transpose(out, (1, 0, 2, 3, 4)).reshape(B, S, H, Dv)

def sliding_window_sink_attention(q, k, v, sinks, slopes):
    B, S, H, D = q.shape
    KV = k.shape[2]
    G = H // KV
    W = WINDOW
    nb = S // W
    qb = q.reshape(B, nb, W, KV, G, D)
    pad = ((0, 0), (W, 0), (0, 0), (0, 0))
    kp = jnp.pad(k, pad).reshape(B, nb + 1, W, KV, D)
    vp = jnp.pad(v, pad).reshape(B, nb + 1, W, KV, D)
    kb = jnp.concatenate([kp[:, :-1], kp[:, 1:]], axis=2)
    vb = jnp.concatenate([vp[:, :-1], vp[:, 1:]], axis=2)
    s = jnp.einsum('bnqkgd,bnckd->bnkgqc', qb, kb, preferred_element_type=jnp.float32) * (D ** -0.5)
    a = jnp.arange(W)[:, None]
    c = jnp.arange(2 * W)[None, :]
    dist = (W + a - c).astype(jnp.float32)
    blk = jnp.arange(nb)[:, None, None]
    valid = (dist >= 0) & (dist < W) & (blk * W + c[None] - W >= 0)
    s = s - slopes.reshape(KV, G)[:, :, None, None] * dist
    s = jnp.where(valid[None, :, None, None], s, -jnp.inf)
    sink = sinks.astype(jnp.float32).reshape(KV, G)[:, :, None, None]
    m = jnp.maximum(jnp.max(s, axis=-1, keepdims=True), sink)
    p = jnp.exp(s - m)
    p = p / (jnp.sum(p, axis=-1, keepdims=True) + jnp.exp(sink - m))
    o = jnp.einsum('bnkgqc,bnckd->bnqkgd', p.astype(v.dtype), vb)
    return o.reshape(B, S, H, D)

def mla_swa_layer(x, positions, g_in, w_in, g_q_a, w_q_up, g_kv_a, w_kv_up, sinks, w_out):
    B, S, _ = x.shape
    h = rms_norm(x, g_in)
    z = h @ w_in
    cq, ckv, kpe, q_s, k_s, v_s, gate = split_cols(z, EVEN_SPLITS)
    q = (rms_norm(cq, g_q_a) @ w_q_up).reshape(B, S, MLA_HEADS, MLA_NOPE + MLA_ROPE)
    q_nope, q_pe = q[..., :MLA_NOPE], q[..., MLA_NOPE:]
    kv = (rms_norm(ckv, g_kv_a) @ w_kv_up).reshape(B, S, MLA_HEADS, MLA_NOPE + MLA_V)
    k_nope, v_m = kv[..., :MLA_NOPE], kv[..., MLA_NOPE:]
    ang = rope_angles(positions, MLA_ROPE)
    q_pe = apply_rope_2(q_pe, ang[:, :, None, :])
    k_pe = apply_rope_2(kpe, ang)[:, :, None, :]
    qm = jnp.concatenate([q_nope, q_pe], axis=-1)
    km = jnp.concatenate([k_nope, jnp.broadcast_to(k_pe, (B, S, MLA_HEADS, MLA_ROPE))], axis=-1)
    o_mla = causal_block_attention(qm, km, v_m)
    o_swa = sliding_window_sink_attention(
        q_s.reshape(B, S, SWA_HEADS, SWA_HEAD_DIM),
        k_s.reshape(B, S, SWA_KV_HEADS, SWA_HEAD_DIM),
        v_s.reshape(B, S, SWA_KV_HEADS, SWA_HEAD_DIM),
        sinks, alibi_slopes(SWA_HEADS))
    o = jnp.concatenate([o_mla.reshape(B, S, -1), o_swa.reshape(B, S, -1)], axis=-1)
    return x + (o * jax.nn.silu(gate)) @ w_out

def fox_layer(x, g_in, w_in, b_f, w_out):
    B, S, _ = x.shape
    h = rms_norm(x, g_in)
    z = h @ w_in
    q, k, v, f_logit, gate = split_cols(z, ODD_SPLITS)
    log_f = jax.nn.log_sigmoid(f_logit.astype(jnp.float32) + b_f.astype(jnp.float32))
    log_cum = jnp.cumsum(log_f, axis=1)
    o = causal_block_attention(q.reshape(B, S, FOX_HEADS, FOX_HEAD_DIM),
                               k.reshape(B, S, FOX_HEADS, FOX_HEAD_DIM),
                               v.reshape(B, S, FOX_HEADS, FOX_HEAD_DIM), log_cum=log_cum)
    return x + (o.reshape(B, S, FOX_WIDTH) * jax.nn.silu(gate)) @ w_out

def second_inputs(seed: int = 0) -> dict:
    key = jax.random.key(seed)
    ks = jax.random.split(key, 16)
    f32 = jnp.float32

    def w(k, shape, fan_in):
        return jax.random.normal(k, shape, f32) * (fan_in ** -0.5)

    def gain(k, shape):
        return 1.0 + 0.05 * jax.random.normal(k, shape, f32)

    x = jax.random.normal(ks[0], (BATCH, SEQ, D_MODEL), f32)
    positions = jnp.broadcast_to(jnp.arange(SEQ, dtype=jnp.int32), (BATCH, SEQ))
    return {
        "x": x,
        "positions": positions,
        "e_g_in": gain(ks[1], (N_EVEN, D_MODEL)),
        "e_w_in": w(ks[2], (N_EVEN, D_MODEL, sum(EVEN_SPLITS)), D_MODEL),
        "e_g_q_a": gain(ks[3], (N_EVEN, MLA_Q_RANK)),
        "e_w_q_up": w(ks[4], (N_EVEN, MLA_Q_RANK, MLA_HEADS * (MLA_NOPE + MLA_ROPE)), MLA_Q_RANK),
        "e_g_kv_a": gain(ks[5], (N_EVEN, MLA_KV_RANK)),
        "e_w_kv_up": w(ks[6], (N_EVEN, MLA_KV_RANK, MLA_HEADS * (MLA_NOPE + MLA_V)), MLA_KV_RANK),
        "e_sinks": jax.random.normal(ks[7], (N_EVEN, SWA_HEADS), f32),
        "e_w_out": w(ks[8], (N_EVEN, EVEN_WIDTH, D_MODEL), EVEN_WIDTH),
        "o_g_in": gain(ks[9], (N_ODD, D_MODEL)),
        "o_w_in": w(ks[10], (N_ODD, D_MODEL, sum(ODD_SPLITS)), D_MODEL),
        "o_b_f": FORGET_BIAS_INIT + 0.5 * jax.random.normal(ks[11], (N_ODD, FOX_HEADS), f32),
        "o_w_out": w(ks[12], (N_ODD, FOX_WIDTH, D_MODEL), FOX_WIDTH),
        "g_final": gain(ks[13], (D_MODEL,)),
    }

def second_block(x, positions, e_g_in, e_w_in, e_g_q_a, e_w_q_up, e_g_kv_a, e_w_kv_up, e_sinks,
              e_w_out, o_g_in, o_w_in, o_b_f, o_w_out, g_final):
    for layer in range(DEPTH_2):
        j = layer // 2
        if layer % 2 == 0:
            x = mla_swa_layer(x, positions, e_g_in[j], e_w_in[j], e_g_q_a[j], e_w_q_up[j],
                              e_g_kv_a[j], e_w_kv_up[j], e_sinks[j], e_w_out[j])
        else:
            x = fox_layer(x, o_g_in[j], o_w_in[j], o_b_f[j], o_w_out[j])
    return rms_norm(x, g_final)


def setup_inputs(seed=0):
    out = dict(first_inputs(seed))
    for name, value in second_inputs(seed + 1).items():
        if name != "x":
            out[name + "_2"] = value
    return out


def reference(
    x, c, ctx, c_ctx, w_mod, b_mod, g_mix, g_ffn, w_in, q_gain, k_gain, v_gain, w_s, b_s, w_out,
    w_router, w1, w3, w2, g_final, positions_2, e_g_in_2, e_w_in_2, e_g_q_a_2, e_w_q_up_2,
    e_g_kv_a_2, e_w_kv_up_2, e_sinks_2, e_w_out_2, o_g_in_2, o_w_in_2, o_b_f_2, o_w_out_2,
    g_final_2,
):
    x = first_block(
        x, c, ctx, c_ctx, w_mod, b_mod, g_mix, g_ffn, w_in, q_gain, k_gain, v_gain, w_s, b_s,
        w_out, w_router, w1, w3, w2, g_final,
    )
    return second_block(
        x, positions_2, e_g_in_2, e_w_in_2, e_g_q_a_2, e_w_q_up_2, e_g_kv_a_2, e_w_kv_up_2,
        e_sinks_2, e_w_out_2, o_g_in_2, o_w_in_2, o_b_f_2, o_w_out_2, g_final_2,
    )


_drawn_inputs = setup_inputs


def setup_inputs(seed=0):
    import zlib

    import numpy as np

    out = dict(_drawn_inputs(seed))
    spreads = {}
    factors = {'q_gain': 8.0,
     'k_gain': 8.0,
     'v_gain': 3.978,
     'b_s': 4.162,
     'e_g_in_2': 3.283,
     'e_g_q_a_2': 8.0,
     'e_g_kv_a_2': 5.902,
     'e_sinks_2': 16.164,
     'o_g_in_2': 8.0,
     'o_b_f_2': 8.0}
    for name, (base, spread) in spreads.items():
        noise = np.random.default_rng([zlib.crc32(name.encode()), seed]).standard_normal(out[name].shape)
        drawn = base * np.exp(spread * noise) if base else spread * noise
        out[name] = __import__('jax').numpy.asarray(drawn.astype(out[name].dtype))
    for name, factor in factors.items():
        out[name] = (out[name] * factor).astype(out[name].dtype)
    return out
```

```python
from contextlib import ExitStack

import numpy as np

import concourse.bass as bass
from concourse import mybir

F32 = mybir.dt.float32
I32 = mybir.dt.int32
ACT = mybir.ActivationFunctionType
ALU = mybir.AluOpType
AX = mybir.AxisListType

P = 128
D = 1024
T = 256
E = 16
SLOT = 4096
NSLOT = 7
EPS = 1e-6
NEG = -1.0e30

INS = ["x", "c", "ctx", "c_ctx", "w_mod", "b_mod", "g_mix", "g_ffn", "w_in", "q_gain", "k_gain", "v_gain",
       "w_s", "b_s", "w_out", "w_router", "w1", "w3", "w2", "g_final", "positions_2", "e_g_in_2", "e_w_in_2",
       "e_g_q_a_2", "e_w_q_up_2", "e_g_kv_a_2", "e_w_kv_up_2", "e_sinks_2", "e_w_out_2", "o_g_in_2",
       "o_w_in_2", "o_b_f_2", "o_w_out_2", "g_final_2"]

K_ID, K_TRI, K_CM, K_DIST, K_ONE, K_COS, K_SIN, K_IOTA, K_SLOT, K_INV, K_HALF, K_END = np.cumsum(
    [0, 128, 128, 256, 256, 128, 64, 64, 32, 1, 16, 16]).tolist()


def constants():
    k = np.zeros((P, K_END), np.float32)
    r = np.arange(P)
    k[:, K_ID:K_ID + 128] = np.eye(P)
    k[:, K_TRI:K_TRI + 128] = r[:, None] <= r[None, :]
    k[:, K_CM + 128:K_CM + 256] = np.where(r[None, :] <= r[:, None], 0.0, NEG)
    dist = 128 + r[:, None] - np.arange(256)[None, :]
    k[:, K_DIST:K_DIST + 256] = np.where((dist >= 0) & (dist < 128), dist, -NEG)
    k[:, K_ONE:K_ONE + 128] = 1.0
    f = np.float32
    inv = (f(10000.0) ** (-np.arange(16, dtype=f) / f(16))).astype(f)
    tok = np.arange(T)
    ang = np.concatenate([(tok // 64).astype(f)[:, None] * inv, (tok % 64).astype(f)[:, None] * inv], axis=1)
    k[:, K_COS:K_COS + 64] = np.cos(ang).astype(f).reshape(2, P, 32).transpose(1, 0, 2).reshape(P, 64)
    k[:, K_SIN:K_SIN + 64] = np.sin(ang).astype(f).reshape(2, P, 32).transpose(1, 0, 2).reshape(P, 64)
    k[:, K_IOTA:K_IOTA + 32] = np.arange(32)[None, :]
    k[:, K_SLOT] = r % 32
    k[:, K_INV:K_INV + 16] = (f(1.0) / (f(10000.0) ** (np.arange(0, 32, 2, dtype=f) / f(32)))).astype(f)[None, :]
    k[:, K_HALF:K_HALF + 16] = -0.5
    return k


class Queue:

    def __init__(self, name, sem):
        self.name, self.sem, self.ops, self.count, self.seen = name, sem, [], 0, {}

    def wait(self, *tokens):
        for t in tokens:
            if t is None:
                continue
            if isinstance(t, list):
                self.wait(*t)
                continue
            sem, value = t
            if self.seen.get(id(sem), 0) < value:
                self.seen[id(sem)] = value
                self.ops.append(lambda e, s=sem, v=value: e.wait_ge(s, v))

    def do(self, fn, *after, mark=True):
        self.wait(*after)
        if mark:
            self.count += 1
            self.ops.append(lambda e: fn(e).then_inc(self.sem, 1))
            return (self.sem, self.count)
        self.ops.append(fn)

    def dma(self, sem, level, fn, *after):
        self.wait(*after)
        self.ops.append(lambda e: fn(e).then_inc(sem, 16))
        return (sem, level)

    def emit(self, eng):
        for op in self.ops:
            op(eng)


def program(nc, ins, kin, out):
    with ExitStack() as ctx:
        body(ctx, nc, ins, kin, out)


def body(ctx, nc, A, kin, out):
    nsem = [0]

    def sem(name):
        nsem[0] += 1
        return ctx.enter_context(nc.semaphore(name))

    pe = Queue("pe", sem("s_pe"))
    dve = Queue("dve", sem("s_dve"))
    act = Queue("act", sem("s_act"))
    pool = Queue("pool", sem("s_pool"))
    sp = Queue("sp", sem("s_sp"))

    ring = ctx.enter_context(nc.sbuf_tensor("ring", [P, NSLOT, SLOT], F32))
    PS = ctx.enter_context(nc.psum_tensor("PS", [P, 8, 512], F32))

    def sb(name, *shape, dt=F32):
        return ctx.enter_context(nc.sbuf_tensor(name, [P, *shape], dt))

    KC = sb("KC", K_END)
    ident = KC[:, K_ID:K_ID + 128]
    tri = KC[:, K_TRI:K_TRI + 128]
    cmask = KC[:, K_CM:K_CM + 256]
    dist = KC[:, K_DIST:K_DIST + 256]
    ones = KC[:, K_ONE:K_ONE + 128]
    iota = KC[:, K_IOTA:K_IOTA + 32]
    slotc = KC[:, K_SLOT:K_SLOT + 1]
    invf = KC[:, K_INV:K_INV + 16]

    X = sb("X", 2, D)
    qgb = sb("qgb", 64)
    kgb = sb("kgb", 64)
    SG = sb("SG", 2, D)
    vgb = SG[:, 0, 0:512]
    sinkb = sb("sinkb", 8)
    bfb = sb("bfb", 16)
    gfb = SG[:, 0, :]
    gtb = SG[:, 1, :]

    RT = sb("RT", 59)
    bm = sb("bm", 3, 512)
    mrow = bm
    mcol = sb("mcol", 3, 4, 4, 2)
    ab = sb("ab", 6, 8)
    cvec = sb("cvec", 8, 32)
    wr = sb("wr", 8, E)
    wf = sb("wf", 8, 16)
    rcs = sb("rcs", 2, 2, 16)
    st = sb("st", 486)
    SC = 16384
    S = sb("S", SC)

    def reg(off, *shape):
        n = int(np.prod(shape))
        assert off + n <= SC, (off, n)
        v = S[:, off:off + n]
        if len(shape) > 1:
            names = "abcd"[:len(shape)]
            v = v.rearrange("p (" + " ".join(names) + ") -> p " + " ".join(names),
                            **{k: s for k, s in zip(names, shape)})
        return v

    R = reg(12288, 128)
    stn = [0]

    def col(n=1):
        stn[0] += n
        assert stn[0] <= 486
        return st[:, stn[0] - n:stn[0]]

    def bc(ap, shape, *axes):
        for a in axes:
            ap = ap.unsqueeze(a)
        return ap.to_broadcast(shape)

    free = {b: [] for b in range(8)}
    turn = {}

    def bank(group):
        i = turn.get(group, 0)
        turn[group] = i + 1
        b = group[i % len(group)]
        assert free[b] is not None, f"bank {b} still held"
        t, free[b] = free[b], None
        return b, t

    ALL6 = (0, 1, 2, 3, 4, 5)
    OB = (6, 7)
    B4 = (0, 1, 2, 3)

    def load(q, dst, src, *after):
        s = sem(f"s_l{nsem[0]}")
        return q.dma(s, 16, lambda e: e.dma_start(dst, src), *after)

    t_k = load(sp, KC[:], kin)
    t_r = [load(sp, R[8 * i:8 * i + 8, :], A[n].rearrange("(j p) -> j p", p=P))
           for i, n in enumerate(["c", "c_ctx", "g_mix", "g_ffn", "e_g_in_2", "o_g_in_2"])]
    t_r.append(load(sp, R[48:56, :], A["b_s"]))
    t_r.append(load(sp, R[56:58, :], A["e_g_q_a_2"].rearrange("(j p) -> j p", p=P)))
    t_r.append(load(sp, R[58:59, :], A["e_g_kv_a_2"].rearrange("(j p) -> j p", p=P)))

    ring_sem = [sem(f"s_w{i}") for i in range(NSLOT)]
    units = []
    t_used = {}

    def unit(key, src, k, w):
        units.append(key)
        u = len(units) - 1
        slot = u % NSLOT
        dst = ring[:, slot, 0:k * w].rearrange("p (k w) -> p k w", k=k)
        before = []
        if u >= NSLOT:
            before = [("used", units[u - NSLOT])]
        place[key] = (dst, (ring_sem[slot], 16 * (u // NSLOT + 1)))
        pending.append((dst, src, ring_sem[slot], before))

    place, pending = {}, []

    def weight(key):
        dst, tok = place[key]
        pe.wait(tok)
        return dst

    def kview(ap):
        return ap.rearrange("(k p) n -> p k n", p=P)

    wm = kview(A["w_mod"])
    for G in range(1):
        for k in range(4):
            unit(("mod", G, k), wm[:, 2 * k:2 * k + 2, 2048 * G:2048 * G + 2048], 2, 2048)
    wi = kview(A["w_in"])
    IN1 = [("kv", 512, 256), ("q", 0, 512), ("vv", 1280, 512), ("u", 768, 512)]
    for n, o, w in IN1:
        unit(("in", n), wi[:, :, o:o + w], 8, w)
    for G in range(1, 3):
        for k in range(4):
            unit(("mod", G, k), wm[:, 2 * k:2 * k + 2, 2048 * G:2048 * G + 2048], 2, 2048)
    for h in range(2):
        unit(("out1", h), kview(A["w_out"])[:, :, 512 * h:512 * h + 512], 8, 512)
    for e in range(E):
        for n in ("w1", "w3"):
            for k in range(4):
                unit((n, e, k), kview(A[n][e])[:, 2 * k:2 * k + 2, :], 2, 2048)
        for j in range(4):
            unit(("w2", e, j), kview(A["w2"][e])[:, 4 * j:4 * j + 4, :], 4, 1024)
    we = kview(A["e_w_in_2"])
    for n, o, w in [("a", 0, 416), ("qs", 416, 512), ("kvs", 928, 256), ("g0", 1184, 512), ("g1", 1696, 512)]:
        unit(("e", n), we[:, :, o:o + w], 8, w)
        if n == "a":
            unit(("qup",), kview(A["e_w_q_up_2"]), 2, 768)
            unit(("kvup",), kview(A["e_w_kv_up_2"]), 1, 1024)
    for h in range(2):
        unit(("out2", h), kview(A["e_w_out_2"])[:, :, 512 * h:512 * h + 512], 8, 512)
    wo = kview(A["o_w_in_2"])
    for n, o in [("q0", 0), ("q1", 512), ("k0", 1024), ("k1", 1536), ("v0", 2048), ("v1", 2560),
                 ("g0", 3088), ("g1", 3600)]:
        unit(("o", n), wo[:, :, o:o + 512], 8, 512)
    for h in range(2):
        unit(("out3", h), kview(A["o_w_out_2"])[:, :, 512 * h:512 * h + 512], 8, 512)

    small = {}

    def ring_loads():
        for n, (dst, src, s, before) in enumerate(pending):
            sp.wait(*[t_used[key] for _, key in before])
            sp.ops.append(lambda e, dst=dst, src=src, s=s: e.dma_start(dst, src).then_inc(s, 16))

    XC = reg(6144, 2, D)
    t_x = load(act, X[:], A["x"].rearrange("(t p) d -> p t d", p=P))
    t_c = load(act, XC, A["ctx"].rearrange("(t p) d -> p t d", p=P))
    t_qg = load(act, qgb[:], A["q_gain"].partition_broadcast(P))
    t_kg = load(act, kgb[:], A["k_gain"].partition_broadcast(P))
    t_vg = load(act, vgb, A["v_gain"].partition_broadcast(P))
    WS = reg(14336, 8, 128)
    t_ws = load(act, WS, A["w_s"].rearrange("g i j -> i g j"))
    t_bm0 = dve.do(lambda e: e.memset(bm[:], 0.0))
    t_bm = []
    for r in range(2):
        for j in range(4):
            t_bm.append(load(act, bm[32 * j + r:32 * j + r + 1, :, :],
                             A["b_mod"].rearrange("(g j n) -> j g n", j=4, n=512)[j:j + 1], t_bm0))
    t_wr = load(act, wr[:], kview(A["w_router"]))
    t_sk = load(act, sinkb[:], A["e_sinks_2"].partition_broadcast(P))
    t_bf = load(act, bfb[:], A["o_b_f_2"].partition_broadcast(P))
    t_wf = load(act, wf[:], kview(A["o_w_in_2"])[:, :, 3072:3088])

    def rstd(outc, ssq, *after):
        n = ssq.shape[-1]
        t = pool.do(lambda e: e.tensor_scalar(outc, ssq, EPS, None, ALU.add), *after)
        return pool.do(lambda e: e.tensor_tensor(outc, outc, KC[:, K_HALF:K_HALF + n], ALU.pow), t)

    def square_sum(in_, outc, junk, width, *after):
        return act.do(lambda e: e.activation(junk, in_, ACT.Square, scale=float(width) ** -0.5, accum_out=outc),
                      *after)

    def transposes(group, pieces, after, parts=P):
        b, fr = bank(group)
        pe.wait(fr, after)
        for i, in_ in enumerate(pieces):
            tok = pe.do(lambda e, i=i, in_=in_, b=b: e.transpose(PS[0:parts, b, 128 * i:128 * i + 128], in_, ident),
                        mark=i == len(pieces) - 1)
        return b, tok

    ev = [0]

    def evac(dst, src, *after):
        ev[0] += 1
        if ev[0] % 2:
            return dve.do(lambda e: e.tensor_copy(dst, src), *after)
        return act.do(lambda e: e.activation(dst, src, ACT.Copy), *after)

    pe.wait(t_k)
    b, fr = bank(ALL6)
    tok = pe.do(lambda e: e.transpose(PS[:, 0, 0:59], R[0:59, :], ident[0:59, 0:59]), t_r)
    t_rt = dve.do(lambda e: e.tensor_copy(RT[:], PS[:, 0, 0:59]), tok)
    free[b] = [t_rt]
    t_cz = pool.do(lambda e: e.memset(cvec[:], 0.0))
    act.wait(t_rt, t_cz)
    t_cv = [act.do(lambda e, r=r: e.activation(cvec[:, :, r], RT[:, 8 * r:8 * r + 8], ACT.Silu)) for r in range(2)]

    c_gmix, c_gffn, c_ge, c_go = [RT[:, 8 * i:8 * i + 8] for i in (2, 3, 4, 5)]
    c_bs, c_qa, c_kva = RT[:, 48:56], RT[:, 56:58], RT[:, 58:59]

    t_mcol = {}
    t_mrow = {}

    def modulation(G):
        b, fr = bank(ALL6)
        pe.wait(fr, t_cv)
        for k in range(4):
            w = weight(("mod", G, k))
            for kk in range(2):
                for j in range(4):
                    tok = pe.do(lambda e, w=w, k=k, kk=kk, j=j, b=b: e.matmul(
                        PS[32 * j:32 * j + 32, b, :], cvec[:, 2 * k + kk, :], w[:, kk, 512 * j:512 * j + 512],
                        start=(k == 0 and kk == 0), stop=(k == 3 and kk == 1)), mark=(kk == 1 and j == 3))
            t_used[("mod", G, k)] = tok
        t = dve.do(lambda e: e.tensor_tensor(mrow[:, G, :], PS[:, b, :], bm[:, G, :], ALU.add), tok, t_bm, t_bm0)
        free[b] = [t]
        t_mrow[G] = t

    def modulation_cols(G):
        b, tok = transposes(ALL6, [mrow[:, G, 128 * s:128 * s + 128] for s in range(4)], t_mrow[G])
        t_mcol[G] = dve.do(lambda e: e.tensor_copy(
            mcol[:, G, :, :, :], PS[:, b, :].rearrange("p (s j r) -> p s j r", s=4, r=32)[:, :, :, 0:2]),
                           tok)
        free[b] = [t_mcol[G]]

    def mvec(G, unit0, r):
        return mcol[:, G, :, unit0:unit0 + 2, r].rearrange("p s j -> p j s")

    def ab8(i):
        return ab[:, i, :].rearrange("p (j s) -> p j s", j=2)

    modulation(0)
    modulation_cols(0)
    t_ab = []
    for r in range(2):
        t_ab.append(dve.do(lambda e, r=r: e.scalar_tensor_tensor(
            out=ab8(2 * r), in0=mvec(0, 2, r), scalar=1.0, in1=c_gmix.rearrange("p (j s) -> p j s", j=2),
            op0=ALU.add, op1=ALU.mult), t_mcol[0]))
        t_ab.append(dve.do(lambda e, r=r: e.tensor_copy(ab8(2 * r + 1), mvec(0, 0, r))))

    XN = reg(4096, 2, D)
    junk = reg(12288, D)
    ss1 = col(4)
    rs1 = col(4)
    tok = t_cv[-1]
    t_sq = []
    for i in range(4):
        src = X[:, i, :] if i < 2 else XC[:, i - 2, :]
        tok = square_sum(src, ss1[:, i:i + 1], junk, D, t_x, t_c, tok)
    t_rs1 = rstd(rs1, ss1, tok)
    t_xn = []
    for i in range(4):
        src = X[:, i, :] if i < 2 else XC[:, i - 2, :]
        dst = XN[:, i, :] if i < 2 else XC[:, i - 2, :]
        t_xn.append(dve.do(lambda e, src=src, dst=dst, i=i: e.tensor_scalar(dst, src, rs1[:, i:i + 1], None, ALU.mult),
                           t_rs1))
    hT = reg(0, 8, 512)
    t_hT = []
    for k in range(8):
        b, tok = transposes(ALL6, [(XN if i < 2 else XC)[:, i % 2, 128 * k:128 * k + 128] for i in range(4)], t_xn)
        for r, eng in ((0, dve), (1, act)):
            dst, src = hT[:, k, 256 * r:256 * r + 256], PS[:, b, 256 * r:256 * r + 256]
            a_, b_ = ab[:, 2 * r, k:k + 1], ab[:, 2 * r + 1, k:k + 1]
            if eng is dve:
                tok = dve.do(lambda e, dst=dst, src=src, a_=a_, b_=b_: e.tensor_scalar(
                    dst, src, a_, b_, ALU.mult, ALU.add), tok, t_ab)
            else:
                tok = act.do(lambda e, dst=dst, src=src, a_=a_, b_=b_: e.activation(
                    dst, src, ACT.Identity, bias=b_, scale=a_), tok, t_ab)
            t_hT.append(tok)
        free[b] = [tok]

    def project(key, h, tile, width, group, k8=8, o=0, after=()):
        b, fr = bank(group)
        pe.wait(fr, *after)
        w = weight(key)
        for k in range(k8):
            tok = pe.do(lambda e, k=k: e.matmul(PS[:, b, 0:width], h[:, k, 128 * tile:128 * tile + 128],
                                                w[:, k, o:o + width], start=(k == 0), stop=(k == k8 - 1)),
                        mark=k == k8 - 1)
        t_used[key] = tok
        return b, tok

    KV = reg(9216, 4, 256)
    KR = reg(10240, 4, 128)
    sqk = reg(10752, 4, 128)
    ssk, rsk = col(8), col(8)
    b_kv, t_kvp = [], []
    for i in range(4):
        b, tok = project(("in", "kv"), hT, i, 256, ALL6, after=[t_hT])
        tok = act.do(lambda e, b=b, i=i: e.activation(KV[:, i, :], PS[:, b, 0:256], ACT.Copy), tok)
        t_kvp.append(tok)
        free[b] = [tok]
    t_kvev = t_kvp[-1]
    tabq = reg(11264, 4, 2, 32)
    tabk = reg(11520, 4, 2, 32)
    cosT = KC[:, K_COS:K_COS + 64].rearrange("p (t f) -> p t f", t=2)
    sinT = KC[:, K_SIN:K_SIN + 64].rearrange("p (t f) -> p t f", t=2)
    t_tab = []
    for tab, g in ((tabq, qgb), (tabk, kgb)):
        for i, (tr, half) in enumerate(((cosT, 0), (sinT, 1), (sinT, 0), (cosT, 1))):
            t_tab.append(pool.do(lambda e, tab=tab, i=i, tr=tr, half=half, g=g: e.tensor_tensor(
                tab[:, i, :, :], tr, bc(g[:, 32 * half:32 * half + 32], [P, 2, 32], 1), ALU.mult), t_qg, t_kg, t_k))
    kh = KV[:, :, 0:128].rearrange("p t (g d) -> p t g d", g=2)
    t1 = dve.do(lambda e: e.tensor_tensor(sqk, KV[:, :, 0:128], KV[:, :, 0:128], ALU.mult), t_kvev)
    t1 = dve.do(lambda e: e.tensor_reduce(ssk, sqk.rearrange("p t (g d) -> p (t g) d", g=2), AX.X, ALU.add), t1)
    t1 = dve.do(lambda e: e.tensor_scalar(ssk, ssk, 1.0 / 64, None, ALU.mult), t1)
    t1 = rstd(rsk, ssk, t1)
    t_kn = dve.do(lambda e: e.tensor_tensor(kh, kh, bc(rsk.rearrange("p (t g) -> p t g", g=2), [P, 4, 2, 64], 3),
                                            ALU.mult), t1)
    rt = reg(11776, 2, 2, 2, 32)

    def rope(dst1, dst2, x1, x2, c1, s2, s1, c2, tmp, *after):
        ta = dve.do(lambda e: e.tensor_tensor(dst1, x1, c1, ALU.mult), *after)
        tb = dve.do(lambda e: e.tensor_tensor(tmp[0], x2, s2, ALU.mult))
        tc = dve.do(lambda e: e.tensor_tensor(dst2, x1, s1, ALU.mult))
        td = dve.do(lambda e: e.tensor_tensor(tmp[1], x2, c2, ALU.mult))
        te = dve.do(lambda e: e.tensor_tensor(dst1, dst1, tmp[0], ALU.subtract), tb)
        return [te, dve.do(lambda e: e.tensor_tensor(dst2, dst2, tmp[1], ALU.add), td)]

    krh = KR.rearrange("p t (g d) -> p t g d", g=2)

    def kt_(i):
        return bc(tabk[:, i, :, :], [P, 2, 2, 32], 2)

    t_kr = rope(krh[:, 0:2, :, 0:32], krh[:, 0:2, :, 32:64], kh[:, 0:2, :, 0:32], kh[:, 0:2, :, 32:64],
                kt_(0), kt_(1), kt_(2), kt_(3), (rt[:, 0], rt[:, 1]), t_kn, t_tab)
    t_kr.append(dve.do(lambda e: e.tensor_tensor(krh[:, 2:4, :, :], kh[:, 2:4, :, :],
                                                 bc(kgb[:], [P, 2, 2, 64], 1, 1), ALU.mult), t_kn))
    KT = reg(8192, 512)
    b, tok = transposes(ALL6, [KR[:, i, :] for i in range(4)], t_kr)
    t_KT = evac(KT, PS[:, b, :], tok)
    free[b] = [t_KT]

    QN = reg(6144, 2, 512)
    QR = reg(7168, 2, 512)
    sqq = reg(12288, 2, 512)
    ssq, rsq = col(16), col(16)
    t_qr = []
    for i in range(2):
        b, tok = project(("in", "q"), hT, i, 512, ALL6)
        qv = QN[:, i, :].rearrange("p (h d) -> p h d", h=8)
        t1 = act.do(lambda e, b=b, i=i: e.activation(sqq[:, i, :], PS[:, b, :], ACT.Square, scale=0.125), tok)
        t1 = dve.do(lambda e, i=i: e.tensor_reduce(ssq[:, 8 * i:8 * i + 8],
                                                   sqq[:, i, :].rearrange("p (h d) -> p h d", h=8), AX.X, ALU.add), t1)
        t1 = rstd(rsq[:, 8 * i:8 * i + 8], ssq[:, 8 * i:8 * i + 8], t1)
        t1 = dve.do(lambda e, b=b, i=i, qv=qv: e.tensor_tensor(
            qv, PS[:, b, :].rearrange("p (h d) -> p h d", h=8), bc(rsq[:, 8 * i:8 * i + 8], [P, 8, 64], 2), ALU.mult), t1)
        free[b] = [t1]
        src = QN[:, i, :].rearrange("p (g n d) -> p g n d", g=2, n=4)
        dst = QR[:, i, :].rearrange("p (n g d) -> p g n d", g=2, n=4)

        tmpv = S[:, 13312:13312 + 512].rearrange("p (a g n d) -> p a g n d", a=2, g=2, n=4)

        def qt_(n, i=i):
            return bc(tabq[:, n, i, :], [P, 2, 4, 32], 1, 1)

        t_qr += rope(dst[:, :, :, 0:32], dst[:, :, :, 32:64], src[:, :, :, 0:32], src[:, :, :, 32:64],
                     qt_(0), qt_(1), qt_(2), qt_(3), (tmpv[:, 0], tmpv[:, 1]), t1, t_tab, t_qr)
    QT = reg(9216 + 2048 + 1024, 2, 512)

    VV = reg(4096, 2, 512)
    U = reg(5120, 2, 512)
    t_vv, t_u = [], []
    for n, dst, lst in (("vv", VV, t_vv), ("u", U, t_u)):
        for i in range(2):
            b, tok = project(("in", n), hT, i, 512, ALL6)
            tok = act.do(lambda e, b=b, i=i, dst=dst: e.activation(dst[:, i, :], PS[:, b, :], ACT.Gelu), tok, t_hT)
            free[b] = [tok]
            lst.append(tok)
    t_hfree = tok_in = t_used[("in", "u")]
    t_QT = []
    for i in range(2):
        b, tok = transposes(ALL6, [QR[:, i, 128 * n:128 * n + 128] for n in range(4)], t_qr)
        t = evac(QT[:, i, :], PS[:, b, :], tok)
        free[b] = [t]
        t_QT.append(t)

    ssv, rsv = col(2), col(2)
    jv = reg(0, 512)
    tok = None
    for i in range(2):
        tok = act.do(lambda e, i=i: e.activation(jv, VV[:, i, :], ACT.Square, scale=512.0 ** -0.5,
                                                 accum_out=ssv[:, i:i + 1]), t_vv, t_hfree, tok)
    t1 = rstd(rsv, ssv, tok)
    t_vn = []
    for i in range(2):
        t_vn.append(dve.do(lambda e, i=i: e.scalar_tensor_tensor(
            out=VV[:, i, :], in0=VV[:, i, :], scalar=rsv[:, i:i + 1], in1=vgb, op0=ALU.mult, op1=ALU.mult),
            t1, t_vg))

    MIX = reg(0, 2, D)
    PB = [reg(2048 + 512 * i, 512) for i in range(3)]
    PT = [reg(7168 - 1024 + 512 * i, 512) for i in range(2)]
    t_PT_free = [None, None]
    t_P_free = [None, None, None]

    class Attention:

        def __init__(self, pbuf, ptbuf, before):
            self.pbuf, self.ptbuf, self.before = pbuf, ptbuf, before
            self.pfree = [before for _ in pbuf]
            self.ptfree = [before for _ in ptbuf]
            self.n = 0

        def run(self, heads, lag=2):
            live = {}
            for n in range(len(heads) + lag + 1):
                if n < len(heads):
                    h = heads[n]
                    m = (self.n + n) % len(self.pbuf)
                    b, fr = bank(ALL6)
                    pe.wait(fr)
                    tok = h["scores"](b)
                    p = self.pbuf[m][:, 0:h["nk"]]
                    t_e, t_fr = h["soft"](b, p, tok, self.pfree[m])
                    free[b] = [t_fr]
                    live[n] = [p, t_e, m]
                if 0 <= n - lag < len(heads):
                    h = heads[n - lag]
                    p, t_e, m = live[n - lag]
                    m2 = (self.n + n - lag) % len(self.ptbuf)
                    nt = h["nk"] // 128
                    b, tok = transposes(ALL6, [p[:, 128 * i:128 * i + 128] for i in range(nt)], t_e)
                    self.pfree[m] = tok
                    t = evac(self.ptbuf[m2][:, 0:128 * nt], PS[:, b, 0:128 * nt], tok, self.ptfree[m2])
                    free[b] = [t]
                    live[n - lag] += [m2, t]
                if 0 <= n - lag - 1 < len(heads):
                    h = heads[n - lag - 1]
                    p, t_e, m, m2, t = live.pop(n - lag - 1)
                    pe.wait(t, *[w() if callable(w) else w for w in h["wait"]])
                    nt = h["nk"] // 128
                    for i in range(nt):
                        tok = pe.do(lambda e, h=h, i=i, m2=m2, nt=nt: e.matmul(
                            h["o"], self.ptbuf[m2][:, 128 * i:128 * i + 128], h["values"][i],
                            start=(i == 0), stop=(i == nt - 1)), mark=i == nt - 1)
                    self.ptfree[m2] = tok
                    if "done" in h:
                        h["done"](tok)
            self.n += len(heads)

    mx1, nm1, sm1, ri1 = col(16), col(16), col(16), col(16)
    at1 = Attention(PB, PT, [t_hfree, tok, *t_qr])
    heads = []
    t_mixa = []
    for i in range(2):
        for n in range(4):
            for g in range(2):
                idx = 8 * i + 4 * g + n

                def scores(b, i=i, n=n, g=g):
                    pe.wait(t_QT, t_KT)
                    return pe.do(lambda e: e.matmul(PS[:, b, :], QT[64 * g:64 * g + 64, i, 128 * n:128 * n + 128],
                                                    KT[64 * g:64 * g + 64, :], start=True, stop=True))

                def soft(b, p, tok, pfree, idx=idx):
                    c = slice(idx, idx + 1)
                    t1 = dve.do(lambda e: e.tensor_reduce(mx1[:, c], PS[:, b, :], AX.X, ALU.max), tok)
                    t1 = dve.do(lambda e: e.tensor_scalar(nm1[:, c], mx1[:, c], -0.125, None, ALU.mult), t1)
                    t1 = act.do(lambda e: e.activation(p, PS[:, b, :], ACT.Exp, bias=nm1[:, c], scale=0.125,
                                                       accum_out=sm1[:, c]), t1, pfree)
                    return t1, t1

                h = dict(scores=scores, soft=soft, nk=512, o=PS[:, OB[i], 64 * (4 * g + n):64 * (4 * g + n) + 64],
                         values=[KV[:, s, 128 + 64 * g:192 + 64 * g] for s in range(4)], wait=[])
                if n == 0 and g == 0:
                    h["wait"] = [free[OB[i]]]
                if n == 3 and g == 1:
                    def done(tok, i=i):
                        t1 = dve.do(lambda e: e.reciprocal(ri1[:, 8 * i:8 * i + 8], sm1[:, 8 * i:8 * i + 8]), tok)
                        t1 = dve.do(lambda e: e.tensor_tensor(
                            MIX[:, i, 0:512].rearrange("p (h d) -> p h d", h=8),
                            PS[:, OB[i], :].rearrange("p (h d) -> p h d", h=8),
                            bc(ri1[:, 8 * i:8 * i + 8], [P, 8, 64], 2), ALU.mult), t1, t_hfree, t_vn)
                        free[OB[i]] = [t1]
                        t_mixa.append(t1)
                    h["done"] = done
                heads.append(h)
    at1.run(heads)

    t_gf = load(pool, gfb, A["g_final"].partition_broadcast(P), t_vn)

    WST = reg(15360, 8, 128)
    t_wst = []
    for hlf in range(2):
        b, tok = transposes(ALL6, [WS[:, 4 * hlf + i, :] for i in range(4)], t_ws)
        t = evac(WST[:, 4 * hlf:4 * hlf + 4, :], PS[:, b, :].rearrange("p (g i) -> p g i", g=4), tok)
        free[b] = [t]
        t_wst.append(t)
    t_mixg = []
    for i in range(2):
        b, fr = bank(ALL6)
        pe.wait(fr, t_wst, t_vn)
        for g in range(8):
            tok = pe.do(lambda e, b=b, g=g, i=i: e.matmul(PS[:, b, 64 * g:64 * g + 64], WST[:, g, :],
                                                          VV[:, i, 64 * g:64 * g + 64], start=True, stop=True),
                        mark=g == 7)
        mg = MIX[:, i, 512:1024].rearrange("p (g d) -> p g d", g=8)
        t1 = dve.do(lambda e, b=b, mg=mg: e.tensor_tensor(mg, PS[:, b, :].rearrange("p (g d) -> p g d", g=8),
                                                          bc(c_bs, [P, 8, 64], 2), ALU.add), tok, t_hfree, t_vn)
        free[b] = [t1]
        t_mixg.append(dve.do(lambda e, i=i: e.tensor_tensor(MIX[:, i, 512:1024], MIX[:, i, 512:1024], U[:, i, :],
                                                            ALU.mult), t1, t_u))

    modulation(1)
    modulation(2)
    modulation_cols(1)
    modulation_cols(2)
    t_ab2 = [dve.do(lambda e: e.scalar_tensor_tensor(
        out=ab8(4), in0=mvec(2, 0, 0), scalar=1.0, in1=c_gffn.rearrange("p (j s) -> p j s", j=2),
        op0=ALU.add, op1=ALU.mult), t_mcol[2]),
        dve.do(lambda e: e.tensor_copy(ab8(5), mvec(1, 2, 0)), t_mcol[1])]

    def gate_rows(G, u0, group, *after):
        toks = []
        for j in range(2):
            b, fr = bank(group)
            r = 32 * (u0 + j)
            tok = pe.do(lambda e, b=b, r=r: e.matmul(PS[:, b, :], ident[:, r:r + 1].to_broadcast([P, 128]),
                                                     mrow[:, G, :], start=True, stop=True), fr, t_mrow[G])
            t = act.do(lambda e, b=b, j=j: e.activation(gtb[:, 512 * j:512 * j + 512], PS[:, b, :], ACT.Copy),
                       tok, *after)
            free[b] = [t]
            toks.append(t)
        return toks

    t_gt1 = gate_rows(1, 0, ALL6)

    def back(off, src, after):
        dst = reg(off, 8, 256)
        toks = []
        for m in range(4):
            b, tok = transposes(ALL6, [src[:, i, 128 * (2 * m + kk):128 * (2 * m + kk) + 128]
                                       for kk in range(2) for i in range(2)], after)
            t = evac(dst[:, 2 * m:2 * m + 2, :], PS[:, b, :].rearrange("p (k t) -> p k t", k=2), tok)
            free[b] = [t]
            toks.append(t)
        return dst, toks

    t_mix = t_mixa + t_mixg
    MT, t_MT = back(2048 + 2048, MIX, t_mix)
    YT = reg(2048, 2, D)
    t_x1 = []
    for h in range(2):
        for i in range(2):
            b, tok = project(("out1", h), MT, i, 512, ALL6, after=[t_MT])
            c = slice(512 * h, 512 * h + 512)
            t1 = dve.do(lambda e, b=b, i=i, c=c: e.tensor_tensor(YT[:, i, c], PS[:, b, :], gtb[:, c], ALU.mult),
                        tok, t_gt1)
            free[b] = [t1]
            t_x1.append(dve.do(lambda e, i=i, c=c: e.tensor_tensor(X[:, i, c], X[:, i, c], YT[:, i, c], ALU.add), t1))
    t_mt_used = t_used[("out1", 1)]

    def normalise(dst, src, after, junk_off, jafter):
        ss_, rs_ = col(2), col(2)
        tok = None
        for i in range(2):
            tok = square_sum(src[:, i, :], ss_[:, i:i + 1], reg(junk_off, D), D, after, jafter, tok)
        t1 = rstd(rs_, ss_, tok)
        return [dve.do(lambda e, i=i: e.tensor_scalar(dst[:, i, :], src[:, i, :], rs_[:, i:i + 1], None, ALU.mult), t1)
                for i in range(2)]

    XN2 = reg(6144, 2, D)
    t_xn2 = normalise(XN2, X, t_x1, 8192, [t_mt_used])
    H2T = reg(4096, 8, 256)

    def turned(dst, src, a_col, b_col, after):
        toks = []
        for m in range(4):
            b, tok = transposes(ALL6, [src[:, i, 128 * (2 * m + kk):128 * (2 * m + kk) + 128]
                                       for kk in range(2) for i in range(2)], after)
            for kk in range(2):
                k = 2 * m + kk
                s_, d_ = PS[:, b, 256 * kk:256 * kk + 256], dst[:, k, :]
                eng = dve if m % 2 else act
                if eng is dve:
                    if b_col is None:
                        t = dve.do(lambda e, s_=s_, d_=d_, k=k: e.tensor_scalar(d_, s_, a_col[:, k:k + 1], None,
                                                                                ALU.mult), tok)
                    else:
                        t = dve.do(lambda e, s_=s_, d_=d_, k=k: e.tensor_scalar(
                            d_, s_, a_col[:, k:k + 1], b_col[:, k:k + 1], ALU.mult, ALU.add), tok)
                else:
                    bias = 0.0 if b_col is None else b_col[:, k:k + 1]
                    t = act.do(lambda e, s_=s_, d_=d_, k=k, bias=bias: e.activation(
                        d_, s_, ACT.Identity, bias=bias, scale=a_col[:, k:k + 1]), tok)
                toks.append(t)
            free[b] = [t]
        return toks

    act.wait(t_ab2)
    dve.wait(t_ab2)
    t_h2 = turned(H2T, XN2, ab[:, 4, :], ab[:, 5, :], t_xn2 + [t_mt_used])

    b, fr = bank(ALL6)
    pe.wait(fr, t_h2, t_wr)
    for i in range(2):
        for k in range(8):
            tok = pe.do(lambda e, b=b, i=i, k=k: e.matmul(PS[:, b, 16 * i:16 * i + 16], H2T[:, k, 128 * i:128 * i + 128],
                                                          wr[:, k, :], start=(k == 0), stop=(k == 7)),
                        mark=(i == 1 and k == 7))
    mxr, smr, rir = col(2), col(2), col(2)
    aff = col(32).rearrange("p (t e) -> p t e", t=2)
    lg = PS[:, b, 0:32].rearrange("p (t e) -> p t e", t=2)
    t1 = dve.do(lambda e: e.tensor_reduce(mxr, lg, AX.X, ALU.max), tok)
    t1 = dve.do(lambda e: e.tensor_scalar(mxr, mxr, -1.0, None, ALU.mult), t1)
    for i in range(2):
        t1 = act.do(lambda e, i=i, b=b: e.activation(aff[:, i, :], PS[:, b, 16 * i:16 * i + 16], ACT.Exp,
                                                bias=mxr[:, i:i + 1], accum_out=smr[:, i:i + 1]), t1)
    free[b] = [t1]
    t1 = dve.do(lambda e: e.reciprocal(rir, smr), t1)
    t_aff = dve.do(lambda e: e.tensor_tensor(aff, aff, bc(rir, [P, 2, 16], 2), ALU.mult), t1)
    b, fr = bank(ALL6)
    pe.wait(fr, t_aff)
    for i in range(2):
        tok = pe.do(lambda e, i=i, b=b: e.transpose(PS[0:16, b, 128 * i:128 * i + 128], aff[:, i, :], ident), mark=i == 1)
    o0 = 9216
    affT = reg(o0, 256)[0:16]
    wk = [reg(o0 + 256 + 256 * i, 256)[0:16] for i in range(2)]
    cum = reg(o0 + 768, 256)[0:16]
    pg = reg(o0 + 1024, 2, 256)[0:16]
    m8 = reg(o0 + 1536, 8)[0:16]
    t1 = dve.do(lambda e, b=b: e.tensor_copy(affT, PS[0:16, b, 0:256]), tok, t_mixa, t_mixg)
    free[b] = [t1]
    cur = affT
    for r in range(4):
        t1 = dve.do(lambda e, cur=cur: e.max(m8, cur), t1)
        t1 = dve.do(lambda e, cur=cur, r=r: e.match_replace(wk[r % 2], m8, cur, -1.0), t1)
        cur = wk[r % 2]
    sel = wk[0]
    t1 = dve.do(lambda e: e.tensor_scalar(sel, wk[1], -1.0, None, ALU.is_equal), t1)
    t_pgg = dve.do(lambda e: e.tensor_tensor(pg[:, 1, :], affT, sel, ALU.mult), t1)
    t1 = dve.do(lambda e: e.tensor_tensor_scan(cum, sel, sel, 0.0, ALU.add, ALU.bypass), t1)
    t1 = dve.do(lambda e: e.tensor_tensor(pg[:, 0, :], cum, sel, ALU.mult), t1)
    t_pg = dve.do(lambda e: e.tensor_scalar(pg[:, 0, :], pg[:, 0, :], -1.0, None, ALU.add), t1)
    b, fr = bank(ALL6)
    pe.wait(fr, t_pg)
    for i in range(2):
        tok = pe.do(lambda e, i=i, b=b: e.transpose(PS[:, b, 16 * i:16 * i + 16], pg[:, 0, 128 * i:128 * i + 128],
                                                    ident[0:16, 0:16]), mark=i == 1)
    SEL = reg(11264, 2, E, 32)
    post = col(32).rearrange("p (t e) -> p t e", t=2)
    t1 = dve.do(lambda e, b=b: e.tensor_copy(post, PS[:, b, 0:32].rearrange("p (t e) -> p t e", t=2)), tok)
    free[b] = [t1]
    t_sel = []
    for i in range(2):
        t_sel.append(dve.do(lambda e, i=i: e.tensor_tensor(
            SEL[:, i, :, :], bc(post[:, i, :], [P, E, 32], 2), bc(iota, [P, E, 32], 1), ALU.is_equal), t1))

    XE = reg(0, 8, 512)
    t_xe = []
    for k in range(8):
        b, fr = bank(ALL6)
        pe.wait(fr, t_sel)
        for i in range(2):
            tok = pe.do(lambda e, b=b, i=i, k=k: e.matmul(
                PS[:, b, :], XN2[:, i, 128 * k:128 * k + 128], SEL[:, i, :, :].rearrange("p e s -> p (e s)"),
                start=(i == 0), stop=(i == 1)), mark=i == 1)
        if k % 2:
            t = dve.do(lambda e, b=b, k=k: e.tensor_scalar(XE[:, k, :], PS[:, b, :], ab[:, 4, k:k + 1], ab[:, 5, k:k + 1],
                                                           ALU.mult, ALU.add), tok)
        else:
            t = act.do(lambda e, b=b, k=k: e.activation(XE[:, k, :], PS[:, b, :], ACT.Identity, bias=ab[:, 5, k:k + 1],
                                                        scale=ab[:, 4, k:k + 1]), tok)
        free[b] = [t]
        t_xe.append(t)

    BIA = reg(14336, 8, 256)

    def tables():
        t_bia = []
        for h in range(8):
            t_bia.append(pool.do(lambda e, h=h: e.tensor_scalar(BIA[:, h, :], dist, -8.0 * 2.0 ** -(h + 1), None, ALU.mult),
                                 t_wst, t_xe, t_mixg))
        posf = col(2)
        ang = col(32).rearrange("p (t f) -> p t f", t=2)
        nrd = col(32).rearrange("p (t f) -> p t f", t=2)
        C1 = 6.28125
        C2 = float(np.float32(np.float32((2 * np.pi - C1) * 2 ** 20).round() / 2 ** 20))
        C3 = float(np.float32(2 * np.pi - C1 - C2))
        MAG = 12582912.0
        prow = reg(13824, 128)[0:2]
        pflt = reg(13952, 128)[0:2]
        t_pos = load(pool, prow.bitcast(I32), A["positions_2"].rearrange("(t p) -> t p", p=P), t_xe)
        t1 = dve.do(lambda e: e.tensor_copy(pflt, prow.bitcast(I32)), t_pos)
        bp, fr = bank(B4)
        tok = pe.do(lambda e: e.transpose(PS[:, bp, 0:2], pflt, ident[0:2, 0:2]), fr, t1)
        t1 = dve.do(lambda e: e.tensor_copy(posf, PS[:, bp, 0:2]), tok)
        free[bp] = [t1]
        t_ang = None
        for i in range(2):
            t_ang = dve.do(lambda e, i=i: e.tensor_scalar(ang[:, i, :], invf, posf[:, i:i + 1], None, ALU.mult), t1)
        PI_ = 3.1415925
        t_rcs = []
        for n, (quarter, shift) in enumerate(((0.25, float(np.pi / 2)), (0.0, 0.0))):
            r_ = rcs[:, n, :, :]
            t1 = dve.do(lambda e, quarter=quarter: e.tensor_scalar(nrd, ang, float(1 / (2 * np.pi)), quarter,
                                                                   ALU.mult, ALU.add), t_ang, t_rcs)
            t1 = dve.do(lambda e: e.tensor_scalar(nrd, nrd, MAG, None, ALU.add), t1)
            t1 = dve.do(lambda e: e.tensor_scalar(nrd, nrd, MAG, None, ALU.subtract), t1)
            t1 = dve.do(lambda e, r_=r_: e.scalar_tensor_tensor(out=r_, in0=nrd, scalar=-C1, in1=ang,
                                                                op0=ALU.mult, op1=ALU.add), t1)
            for cc in (C2, C3):
                t1 = dve.do(lambda e, r_=r_, cc=cc: e.scalar_tensor_tensor(out=r_, in0=nrd, scalar=-cc, in1=r_,
                                                                           op0=ALU.mult, op1=ALU.add), t1)
            if shift:
                t1 = dve.do(lambda e, r_=r_, shift=shift: e.tensor_scalar(r_, r_, shift, None, ALU.add), t1)
            t1 = dve.do(lambda e, r_=r_: e.tensor_scalar(r_, r_, PI_, -PI_, ALU.min, ALU.max), t1)
            t_rcs.append(act.do(lambda e, r_=r_: e.activation(r_, r_, ACT.Sin), t1))

        return t_bia, t_rcs

    HB = [reg(4096 + 512 * i, 512) for i in range(2)]
    HT = [reg(5120 + 512 * i, 512) for i in range(2)]
    YE = [reg(6144 + 512 * i, 512) for i in range(2)]
    EQ = [reg(7168 + 256 * i, 256) for i in range(2)]
    GT = [reg(7680 + 256 * i, 256) for i in range(2)]
    t_hb, t_ht, t_ye, t_gt = [t_xe] * 2, [t_xe] * 2, [t_xe] * 2, [t_xe] * 2
    t_eq = [t_xe] * 2
    acc_free = [free[b] for b in (4, 5, 6, 7)]
    for b in (4, 5, 6, 7):
        free[b] = None
    gt_tok, ye_tok = {}, {}

    def scatter(e_):
        m = e_ % 2
        pe.wait(gt_tok[e_], ye_tok[e_])
        if e_ == 0:
            pe.wait(acc_free)
        for i in range(2):
            for dh in range(2):
                tok = pe.do(lambda e, i=i, dh=dh, m=m: e.matmul(
                    PS[:, 4 + 2 * i + dh, :], GT[m][64 * dh:64 * dh + 64, 128 * i:128 * i + 128],
                    YE[m][64 * dh:64 * dh + 64, :], start=(e_ == 0), stop=(e_ == E - 1)), mark=(i == 1 and dh == 1))
        t_ye[m] = t_gt[m] = tok
        return tok

    def up(name, e_, b):
        for k in range(4):
            w = weight((name, e_, k))
            for kk in range(2):
                for j in range(4):
                    tok = pe.do(lambda e, w=w, k=k, kk=kk, j=j: e.matmul(
                        PS[32 * j:32 * j + 32, b, :], XE[:, 2 * k + kk, 32 * e_:32 * e_ + 32],
                        w[:, kk, 512 * j:512 * j + 512],
                        start=(k == 0 and kk == 0), stop=(k == 3 and kk == 1)), mark=(kk == 1 and j == 3))
            t_used[(name, e_, k)] = tok
        return tok

    pe.wait(t_xe)
    for e_ in range(E):
        m = e_ % 2
        b, fr = bank(B4)
        tok = pe.do(lambda e, b=b, e_=e_: e.matmul(PS[:, b, :], ident[0:16, e_:e_ + 1].to_broadcast([16, 128]),
                                                   pg.rearrange("p a t -> p (a t)"), start=True, stop=True),
                    fr, t_pg, t_pgg)
        t1 = dve.do(lambda e, b=b, m=m: e.tensor_scalar(EQ[m], PS[:, b, 0:256], slotc, None, ALU.is_equal), tok, t_eq[m])
        t1 = dve.do(lambda e, b=b, m=m: e.tensor_tensor(GT[m], PS[:, b, 256:512], EQ[m], ALU.mult), t1, t_gt[m])
        t_eq[m] = gt_tok[e_] = t1
        free[b] = [t1]
        if e_ == 1:
            t_bia, t_rcs = tables()
        b1, fr = bank(B4)
        pe.wait(fr)
        tok = up("w1", e_, b1)
        t_s = act.do(lambda e, b1=b1, m=m: e.activation(HB[m], PS[:, b1, :], ACT.Silu), tok, t_hb[m])
        free[b1] = [t_s]
        b3, fr = bank(B4)
        pe.wait(fr)
        if e_:
            scatter(e_ - 1)
        tok = up("w3", e_, b3)
        t_h = dve.do(lambda e, b3=b3, m=m: e.tensor_tensor(HB[m], PS[:, b3, :], HB[m], ALU.mult), tok, t_s)
        free[b3] = [t_h]
        b, tok = transposes(B4, [HB[m][:, 128 * s:128 * s + 128] for s in range(4)], t_h)
        t_hb[m] = tok
        t_t = act.do(lambda e, b=b, m=m: e.activation(HT[m], PS[:, b, :], ACT.Copy), tok, t_ht[m])
        free[b] = [t_t]
        b, fr = bank(B4)
        pe.wait(fr, t_t)
        for j in range(4):
            w = weight(("w2", e_, j))
            for s in range(4):
                for dh in range(2):
                    q = 64 * dh + 32 * (s % 2)
                    tok = pe.do(lambda e, b=b, w=w, j=j, s=s, dh=dh, q=q, m=m: e.matmul(
                        PS[q:q + 32, b, :], HT[m][:, 128 * s + 32 * j:128 * s + 32 * j + 32],
                        w[:, s, 512 * dh:512 * dh + 512], start=(j == 0 and s < 2), stop=(j == 3 and s >= 2)),
                        mark=(s == 3 and dh == 1))
            t_used[("w2", e_, j)] = tok
        t_ht[m] = tok
        ye_tok[e_] = dve.do(lambda e, b=b, m=m: e.tensor_copy(YE[m], PS[:, b, :]), tok, t_ye[m])
        free[b] = [ye_tok[e_]]

    t_acc = scatter(E - 1)

    t_gt2 = gate_rows(2, 2, B4, t_x1)
    tmp = reg(8192, 2, D)
    t_x2 = []
    for i in range(2):
        for dh in range(2):
            c = slice(512 * dh, 512 * dh + 512)
            t1 = dve.do(lambda e, i=i, dh=dh, c=c: e.tensor_tensor(tmp[:, i, c], PS[:, 4 + 2 * i + dh, :], gtb[:, c],
                                                                   ALU.mult), t_acc, t_gt2)
            free[4 + 2 * i + dh] = [t1]
            t_x2.append(dve.do(lambda e, i=i, c=c: e.tensor_tensor(X[:, i, c], X[:, i, c], tmp[:, i, c], ALU.add), t1))
    XN3 = reg(2048, 2, D)
    ss_, rs_ = col(2), col(2)
    tok = None
    for i in range(2):
        tok = square_sum(X[:, i, :], ss_[:, i:i + 1], reg(0, D), D, t_x2, t_acc, tok)
    t1 = rstd(rs_, ss_, tok)
    t_xf = [dve.do(lambda e, i=i: e.scalar_tensor_tensor(out=X[:, i, :], in0=X[:, i, :], scalar=rs_[:, i:i + 1],
                                                         in1=gfb, op0=ALU.mult, op1=ALU.mult), t1, t_gf)
            for i in range(2)]

    t_n = normalise(XN3, X, t_xf, 0, [t_acc])
    HE = reg(4096, 8, 256)
    t_HE = turned(HE, XN3, c_ge, None, t_n + [t_acc])

    ZA = reg(0, 2, 416)
    t_za = []
    ssa, rsa = col(4), col(4)
    jk = reg(1024, 256)
    tj = None
    for i in range(2):
        b, tok = project(("e", "a"), HE, i, 416, ALL6, after=[t_HE])
        tz = dve.do(lambda e, b=b, i=i: e.tensor_copy(ZA[:, i, :], PS[:, b, 0:416]), tok, t_n)
        free[b] = [tz]
        tj = act.do(lambda e, i=i: e.activation(jk, ZA[:, i, 0:256], ACT.Square, scale=1.0 / 16,
                                                accum_out=ssa[:, 2 * i:2 * i + 1]), tz, tj, t_n)
        tj = act.do(lambda e, i=i: e.activation(jk[:, 0:128], ZA[:, i, 256:384], ACT.Square, scale=128.0 ** -0.5,
                                                accum_out=ssa[:, 2 * i + 1:2 * i + 2]), tj)
    t1 = rstd(rsa, ssa, tj)
    for i in range(2):
        t_za.append(dve.do(lambda e, i=i: e.tensor_scalar(ZA[:, i, 0:256], ZA[:, i, 0:256], rsa[:, 2 * i:2 * i + 1],
                                                          None, ALU.mult), t1))
        t_za.append(dve.do(lambda e, i=i: e.tensor_scalar(ZA[:, i, 256:384], ZA[:, i, 256:384],
                                                          rsa[:, 2 * i + 1:2 * i + 2], None, ALU.mult), t1))
    CT = reg(1024 + 256, 3, 256)
    t_ct = []
    for kk in range(3):
        b, tok = transposes(ALL6, [ZA[:, i, 128 * kk:128 * kk + 128] for i in range(2)], t_za)
        g_ = c_qa[:, kk:kk + 1] if kk < 2 else c_kva
        t_ct.append(dve.do(lambda e, b=b, kk=kk, g_=g_: e.tensor_scalar(CT[:, kk, :], PS[:, b, 0:256], g_, None,
                                                                        ALU.mult), tok, t_n))
        free[b] = [t_ct[-1]]
    KP = col(64).rearrange("p (t f) -> p t f", t=2)
    rtmp = reg(13824, 2, 8, 16)
    kt2 = [rtmp[:, a, 0:2, :] for a in range(2)]
    cs, sn = rcs[:, 0, :, :], rcs[:, 1, :, :]
    t_kp = rope(KP[:, :, 0:16], KP[:, :, 16:32], ZA[:, :, 384:400], ZA[:, :, 400:416], cs, sn, sn, cs, kt2,
                t_rcs, t_za, t_acc)
    QK = reg(2048, 2, 8, 96)
    KM = reg(8192, 2, 8, 96)
    VM = reg(9728, 2, 8, 64)
    QMT = reg(10752, 8, 256)
    t_qk, t_km, t_vm = [], [], []
    for i in range(2):
        for o, w, h0, hn in ((0, 480, 0, 5), (480, 288, 5, 3)):
            b, tok = project(("qup",), CT, i, w, ALL6, k8=2, o=o, after=[t_ct])
            v = PS[:, b, 0:w].rearrange("p (h d) -> p h d", d=96)
            ta = act.do(lambda e, v=v, i=i, h0=h0, hn=hn: e.activation(QK[:, i, h0:h0 + hn, 0:64], v[:, :, 0:64], ACT.Copy),
                        tok, t_HE)
            tm = [rtmp[:, a, 0:hn, :] for a in range(2)]
            tr_ = rope(QK[:, i, h0:h0 + hn, 64:80], QK[:, i, h0:h0 + hn, 80:96], v[:, :, 64:80], v[:, :, 80:96],
                       bc(cs[:, i, :], [P, hn, 16], 1), bc(sn[:, i, :], [P, hn, 16], 1),
                       bc(sn[:, i, :], [P, hn, 16], 1), bc(cs[:, i, :], [P, hn, 16], 1), tm, ta, t_kp)
            free[b] = tr_
            t_qk += [ta] + tr_
            t_kp = tr_ + t_kp
    for i in range(2):
        for o in range(2):
            b, tok = project(("kvup",), CT[:, 2:3, :], i, 512, ALL6, k8=1, o=512 * o)
            v = PS[:, b, :].rearrange("p (h d) -> p h d", d=128)
            ta = act.do(lambda e, v=v, i=i, o=o: e.activation(KM[:, i, 4 * o:4 * o + 4, 0:64], v[:, :, 0:64], ACT.Copy),
                        tok, t_x2)
            tb = act.do(lambda e, v=v, i=i, o=o: e.activation(VM[:, i, 4 * o:4 * o + 4, :], v[:, :, 64:128], ACT.Copy))
            free[b] = [tb]
            t_km.append(ta)
            t_vm.append(tb)
        t_km.append(dve.do(lambda e, i=i: e.tensor_copy(KM[:, i, :, 64:96], bc(KP[:, i, :], [P, 8, 32], 1)),
                           t_kp, t_x2))
    QST = reg(12800, 4, 256)
    KST = reg(3584, 2, 256)
    w = weight(("e", "qs"))
    t_qst = []
    for n2 in range(2):
        b, fr = bank(ALL6)
        pe.wait(fr)
        for nn in range(2):
            n = 2 * n2 + nn
            for k in range(8):
                tok = pe.do(lambda e, b=b, n=n, nn=nn, k=k, w=w: e.matmul(
                    PS[:, b, 256 * nn:256 * nn + 256],
                    w[:, k, 128 * n:128 * n + 128], HE[:, k, :],
                    start=(k == 0), stop=(k == 7)), mark=(nn == 1 and k == 7))
        t = evac(QST[:, 2 * n2:2 * n2 + 2, :], PS[:, b, :].rearrange("p (n t) -> p n t", n=2), tok, t_xe)
        free[b] = [t]
        t_qst.append(t)
    t_used[("e", "qs")] = tok
    w = weight(("e", "kvs"))
    b, fr = bank(ALL6)
    pe.wait(fr)
    for k in range(8):
        tok = pe.do(lambda e, b=b, k=k, w=w: e.matmul(PS[:, b, 0:256], w[:, k, 0:128], HE[:, k, :],
                                                      start=(k == 0), stop=(k == 7)), mark=k == 7)
    t_kst = None
    for g in range(2):
        for r in range(2):
            t_kst = dve.do(lambda e, b=b, g=g, r=r: e.tensor_copy(KST[64 * r:64 * r + 64, g, :],
                                                                  PS[64 * g:64 * g + 64, b, 0:256]), tok, t_HE)
    free[b] = [t_kst]
    VS = reg(0 + 896, 2, 128)
    t_vs = []
    for i in range(2):
        b, tok = project(("e", "kvs"), HE, i, 128, ALL6, o=128)
        t_vs.append(act.do(lambda e, b=b, i=i: e.activation(VS[:, i, :], PS[:, b, 0:128], ACT.Copy), tok, t_ct))
        free[b] = [t_vs[-1]]
    t_sg = []
    for h in range(2):
        for i in range(2):
            b, tok = project(("e", f"g{h}"), HE, i, 512, ALL6)
            t_sg.append(act.do(lambda e, b=b, i=i, h=h: e.activation(SG[:, i, 512 * h:512 * h + 512], PS[:, b, :],
                                                                     ACT.Silu), tok))
            free[b] = [t_sg[-1]]
    t_he_used = tok
    KMT = reg(4096, 8, 256)
    t_qmt, t_kmt = [], []
    for src, dst, lst, aft in ((QK, QMT, t_qmt, t_qk), (KM, KMT, t_kmt, t_km)):
        for hp in range(4):
            b, tok = transposes(ALL6, [src[:, i, 2 * hp + hh, :] for hh in range(2) for i in range(2)], aft, parts=96)
            t = evac(dst[0:96, 2 * hp:2 * hp + 2, :], PS[0:96, b, :].rearrange("p (h t) -> p h t", h=2), tok, t_he_used,
                     t_acc)
            free[b] = [t]
            lst.append(t)
    t_qkm_used = tok

    O2 = reg(6144, 2, D)
    Zb = [reg(2048 + 256 * i, 256) for i in range(3)]
    PB2 = [reg(2816 + 256 * i, 256) for i in range(3)]
    PT2 = [reg(8192 + 256 * i, 256) for i in range(2)]
    mx2, nm2, sm2, ri2 = mx1, nm1, sm1, ri1
    at2 = Attention(PB2, PT2, [t_qkm_used])
    zfree = [None] * 3
    znum = [0]

    def masked_soft(b, p, tok, pfree, bias, scale, mxc, nmc, smc, shift=None, floor=None, first=None):
        z = znum[0] % 3
        znum[0] += 1
        nk = bias.shape[-1]
        zz = Zb[z][:, 0:nk]
        t1 = dve.do(lambda e: e.tensor_tensor_reduce(zz, PS[:, b, 0:nk], bias, scale, -3.0e38, ALU.add, ALU.max, mxc),
                    tok, zfree[z], first)
        t_fr = t1
        if floor is not None:
            t1 = dve.do(lambda e: e.tensor_scalar(nmc, mxc, floor, -1.0, ALU.max, ALU.mult), t1)
        elif shift is not None:
            t1 = dve.do(lambda e: e.tensor_scalar(nmc, mxc, shift, -1.0, ALU.add, ALU.mult), t1)
            t1 = dve.do(lambda e: e.tensor_scalar(nmc, nmc, shift, None, ALU.add), t1)
        else:
            t1 = dve.do(lambda e: e.tensor_scalar(nmc, mxc, -1.0, None, ALU.mult), t1)
        t1 = act.do(lambda e: e.activation(p, zz, ACT.Exp, bias=nmc, accum_out=smc), t1, pfree)
        zfree[z] = t1
        return t1, t_fr

    heads = []
    t_o2 = []
    esk = col(16)
    for i in range(2):
        nk = 128 * (i + 1)
        for h in range(8):
            idx = 8 * i + h

            def scores(b, i=i, h=h, nk=nk):
                pe.wait(t_qmt, t_kmt)
                return pe.do(lambda e: e.matmul(PS[:, b, 0:nk], QMT[0:96, h, 128 * i:128 * i + 128], KMT[0:96, h, 0:nk],
                                                start=True, stop=True))

            def soft(b, p, tok, pfree, idx=idx, nk=nk):
                c = slice(idx, idx + 1)
                return masked_soft(b, p, tok, pfree, cmask[:, 256 - nk:256], 96.0 ** -0.5, mx2[:, c], nm2[:, c],
                                   sm2[:, c], first=t_qkm_used)

            hd = dict(scores=scores, soft=soft, nk=nk, o=PS[:, OB[i], 64 * h:64 * h + 64],
                      values=[VM[:, s, h, :] for s in range(i + 1)], wait=[t_vm])
            if h == 0:
                hd["wait"] = [t_vm, free[OB[i]]]
            if h == 7:
                def done(tok, i=i):
                    t1 = dve.do(lambda e: e.reciprocal(ri2[:, 8 * i:8 * i + 8], sm2[:, 8 * i:8 * i + 8]), tok)
                    t1 = dve.do(lambda e: e.tensor_tensor(
                        O2[:, i, 0:512].rearrange("p (h d) -> p h d", h=8),
                        PS[:, OB[i], :].rearrange("p (h d) -> p h d", h=8),
                        bc(ri2[:, 8 * i:8 * i + 8], [P, 8, 64], 2), ALU.mult), t1, t_he_used, t_qkm_used)
                    free[OB[i]] = [t1]
                    t_o2.append(dve.do(lambda e: e.tensor_tensor(O2[:, i, 0:512], O2[:, i, 0:512], SG[:, i, 0:512],
                                                                 ALU.mult), t1, t_sg))
                hd["done"] = done
            heads.append(hd)
    at2.run(heads)

    mx3, nm3, sm3, ri3 = mx2, nm2, col(16), ri2
    heads = []
    for i in range(2):
        nk = 128 * (i + 1)
        for n in range(4):
            for g in range(2):
                h = 4 * g + n
                idx = 8 * i + h

                def scores(b, i=i, h=h, r=64 * (h % 2), g=g, nk=nk):
                    pe.wait(t_qst, t_kst)
                    return pe.do(lambda e: e.matmul(PS[:, b, 0:nk], QST[r:r + 64, h // 2, 128 * i:128 * i + 128],
                                                    KST[r:r + 64, g, 0:nk], start=True, stop=True))

                def soft(b, p, tok, pfree, idx=idx, nk=nk, h=h):
                    c = slice(idx, idx + 1)
                    t1, t_fr = masked_soft(b, p, tok, pfree, BIA[:, h, 256 - nk:256], 0.125, mx3[:, c], nm3[:, c],
                                           sm3[:, c], floor=sinkb[:, h:h + 1], first=[t_bia, t_sk])
                    t2 = act.do(lambda e: e.activation(esk[:, c], sinkb[:, h:h + 1], ACT.Exp, bias=nm3[:, c]))
                    return [t1, t2], t_fr

                hd = dict(scores=scores, soft=soft, nk=nk, o=PS[:, OB[i], 64 * h:64 * h + 64],
                          values=[VS[:, s, 64 * g:64 * g + 64] for s in range(i + 1)], wait=[t_vs])
                if n == 0 and g == 0:
                    hd["wait"] = [t_vs, ("o", i)]
                if n == 3 and g == 1:
                    def done(tok, i=i):
                        c = slice(8 * i, 8 * i + 8)
                        t1 = dve.do(lambda e: e.tensor_tensor(sm3[:, c], sm3[:, c], esk[:, c], ALU.add), tok)
                        t1 = dve.do(lambda e: e.reciprocal(ri3[:, c], sm3[:, c]), t1)
                        t1 = dve.do(lambda e: e.tensor_tensor(
                            O2[:, i, 512:1024].rearrange("p (h d) -> p h d", h=8),
                            PS[:, OB[i], :].rearrange("p (h d) -> p h d", h=8),
                            bc(ri3[:, c], [P, 8, 64], 2), ALU.mult), t1)
                        free[OB[i]] = [t1]
                        t_o2.append(dve.do(lambda e: e.tensor_tensor(O2[:, i, 512:1024], O2[:, i, 512:1024],
                                                                     SG[:, i, 512:1024], ALU.mult), t1))
                    hd["done"] = done
                if hd["wait"][-1] == ("o", i):
                    hd["wait"] = [t_vs, free[OB[i]]]
                heads.append(hd)
    at2.run(heads)

    OT, t_OT = back(10752, O2, t_o2)

    def residual(name, src_t, after):
        toks = []
        for h in range(2):
            for i in range(2):
                b, tok = project((name, h), src_t, i, 512, ALL6, after=[after])
                c = slice(512 * h, 512 * h + 512)
                t1 = dve.do(lambda e, b=b, i=i, c=c: e.tensor_tensor(X[:, i, c], PS[:, b, :], X[:, i, c], ALU.add), tok)
                free[b] = [t1]
                toks.append(t1)
        return toks

    t_x3 = residual("out2", OT, t_OT)
    t_ot_used = t_used[("out2", 1)]

    XN4 = reg(8192, 2, D)
    t_n = normalise(XN4, X, t_x3, 12800, [t_ot_used, t_o2])
    HO = reg(0, 8, 256)
    t_HO = turned(HO, XN4, c_go, None, t_n + [t_x3[-1]])
    fl = col(32).rearrange("p (t h) -> p t h", t=2)
    fe, fu, fd = [mx1[:, 0:16], nm1[:, 0:16], sm1[:, 0:16]], None, None
    F1 = reg(14336, 2, 16)
    F2 = reg(14368, 2, 16)
    F3 = reg(14400, 2, 16)
    F4 = reg(14432, 2, 16)
    F5 = reg(14464, 2, 16)
    b, fr = bank(ALL6)
    pe.wait(fr, t_HO, t_wf)
    for i in range(2):
        for k in range(8):
            tok = pe.do(lambda e, b=b, i=i, k=k: e.matmul(PS[:, b, 16 * i:16 * i + 16], HO[:, k, 128 * i:128 * i + 128],
                                                          wf[:, k, :], start=(k == 0), stop=(k == 7)),
                        mark=(i == 1 and k == 7))
    t1 = dve.do(lambda e, b=b: e.tensor_tensor(F1, PS[:, b, 0:32].rearrange("p (t h) -> p t h", t=2),
                                          bc(bfb[:], [P, 2, 16], 1), ALU.add), tok, t_bf, t_x3, t_bia)
    free[b] = [t1]
    t1 = dve.do(lambda e: e.tensor_scalar(F2, F1, -1.0, None, ALU.mult), t1)
    t1 = dve.do(lambda e: e.tensor_tensor(F2, F1, F2, ALU.min), t1)
    t1 = act.do(lambda e: e.activation(F2, F2, ACT.Exp), t1)
    t_u1 = dve.do(lambda e: e.tensor_scalar(F3, F2, 1.0, None, ALU.add), t1)
    t_ln = act.do(lambda e: e.activation(F4, F3, ACT.Ln), t_u1)
    t1 = dve.do(lambda e: e.tensor_scalar(F3, F3, -1.0, None, ALU.add), t_ln)
    t1 = dve.do(lambda e: e.tensor_scalar(F5, F3, 0.0, None, ALU.is_equal), t1)
    t1 = dve.do(lambda e: e.tensor_tensor(F3, F3, F5, ALU.add), t1)
    t1 = dve.do(lambda e: e.tensor_tensor(F4, F4, F5, ALU.add), t1)
    t1 = dve.do(lambda e: e.reciprocal(F3, F3), t1)
    t1 = dve.do(lambda e: e.tensor_tensor(F4, F4, F3, ALU.mult), t1)
    t1 = dve.do(lambda e: e.tensor_tensor(F4, F4, F2, ALU.mult), t1)
    t1 = dve.do(lambda e: e.tensor_scalar(F1, F1, 0.0, None, ALU.min), t1)
    t_lf = dve.do(lambda e: e.tensor_tensor(F1, F1, F4, ALU.subtract), t1)

    def straight(names, dst, after):
        toks = []
        for hf, nm in enumerate(names):
            w = weight(("o", nm))
            for n2 in range(2):
                b, fr = bank(ALL6)
                pe.wait(fr)
                for nn in range(2):
                    n = 2 * n2 + nn
                    for k in range(8):
                        tok = pe.do(lambda e, b=b, n=n, nn=nn, k=k, w=w: e.matmul(
                            PS[:, b, 256 * nn:256 * nn + 256], w[:, k, 128 * n:128 * n + 128], HO[:, k, :],
                            start=(k == 0), stop=(k == 7)), mark=(nn == 1 and k == 7))
                t = evac(dst[:, 4 * hf + 2 * n2:4 * hf + 2 * n2 + 2, :],
                         PS[:, b, :].rearrange("p (n t) -> p n t", n=2), tok, after)
                free[b] = [t]
                toks.append(t)
            t_used[("o", nm)] = tok
        return toks

    QF = reg(2048, 8, 256)
    t_qf = straight(("q0", "q1"), QF, t_x3)
    b, fr = bank(ALL6)
    pe.wait(fr, t_lf)
    pe.do(lambda e, b=b: e.matmul(PS[:, b, 0:16], tri, F1[:, 0, :], start=True, stop=True), mark=False)
    pe.do(lambda e, b=b: e.matmul(PS[:, b, 16:32], tri, F1[:, 1, :], start=True, stop=False), mark=False)
    tok = pe.do(lambda e, b=b: e.matmul(PS[:, b, 16:32], ones, F1[:, 0, :], start=False, stop=True))
    t_cs = dve.do(lambda e, b=b: e.tensor_copy(fl, PS[:, b, 0:32].rearrange("p (t h) -> p t h", t=2)), tok)
    free[b] = [t_cs]
    b, fr = bank(ALL6)
    pe.wait(fr, t_cs)
    for i in range(2):
        tok = pe.do(lambda e, i=i, b=b: e.transpose(PS[0:16, b, 128 * i:128 * i + 128], fl[:, i, :], ident), mark=i == 1)
    NC_ = reg(14592, 256)[0:16]
    t_nc = dve.do(lambda e, b=b: e.tensor_scalar(NC_, PS[0:16, b, 0:256], -8.0, None, ALU.mult), tok, t_bia, t_o2)
    free[b] = [t_nc]
    KF = reg(4096, 8, 256)
    t_kf = straight(("k0", "k1"), KF, t_x3)
    VF = reg(6144, 2, D)
    t_vf = []
    for h in range(2):
        for i in range(2):
            b, tok = project(("o", f"v{h}"), HO, i, 512, ALL6)
            t_vf.append(evac(VF[:, i, 512 * h:512 * h + 512], PS[:, b, :], tok, t_x3, t_OT))
            free[b] = [t_vf[-1]]
    t_sg2 = []
    for h in range(2):
        for i in range(2):
            b, tok = project(("o", f"g{h}"), HO, i, 512, ALL6)
            t_sg2.append(act.do(lambda e, b=b, i=i, h=h: e.activation(SG[:, i, 512 * h:512 * h + 512], PS[:, b, :],
                                                                      ACT.Silu), tok, t_o2))
            free[b] = [t_sg2[-1]]
    t_ho_used = tok
    O3 = reg(10752, 2, D)
    Zb[:] = [reg(12800 + 256 * i, 256) for i in range(3)]
    PB3 = [reg(13568 + 256 * i, 256) for i in range(3)]
    PT3 = [reg(14848 + 256 * i, 256) for i in range(2)]
    at3 = Attention(PB3, PT3, [t_ho_used, t_bia, t_x3])
    mx4, nm4, sm4, ri4 = [reg(15360 + 32 * i, 32) for i in range(4)]
    heads = []
    t_o3 = []
    for i in range(2):
        nk = 128 * (i + 1)
        for h in range(16):
            idx = 16 * i + h

            def scores(b, i=i, h=h, nk=nk):
                pe.wait(t_qf, t_kf, t_nc)
                r = 64 * (h % 2)
                pe.do(lambda e: e.matmul(PS[:, b, 0:nk], QF[r:r + 64, h // 2, 128 * i:128 * i + 128],
                                         KF[r:r + 64, h // 2, 0:nk], start=True, stop=False), mark=False)
                return pe.do(lambda e: e.matmul(PS[:, b, 0:nk], ident[0:16, h:h + 1].to_broadcast([16, 128]),
                                                NC_[:, 0:nk], start=False, stop=True))

            def soft(b, p, tok, pfree, idx=idx, nk=nk, i=i, h=h):
                c = slice(idx, idx + 1)
                return masked_soft(b, p, tok, pfree, cmask[:, 256 - nk:256], 0.125, mx4[:, c], nm4[:, c], sm4[:, c],
                                   shift=fl[:, i, h:h + 1], first=[t_ho_used, t_n])

            hd = dict(scores=scores, soft=soft, nk=nk, o=PS[:, OB[h // 8], 64 * (h % 8):64 * (h % 8) + 64],
                      values=[VF[:, s, 64 * h:64 * h + 64] for s in range(i + 1)], wait=[t_vf])
            if h % 8 == 0:
                hd["wait"] = [t_vf, lambda h=h: free[OB[h // 8]]]
            if h % 8 == 7:
                def done(tok, i=i, hf=h // 8):
                    c = slice(16 * i + 8 * hf, 16 * i + 8 * hf + 8)
                    oc = slice(512 * hf, 512 * hf + 512)
                    t1 = dve.do(lambda e: e.reciprocal(ri4[:, c], sm4[:, c]), tok)
                    t1 = dve.do(lambda e: e.tensor_tensor(
                        O3[:, i, oc].rearrange("p (h d) -> p h d", h=8),
                        PS[:, OB[hf], :].rearrange("p (h d) -> p h d", h=8),
                        bc(ri4[:, c], [P, 8, 64], 2), ALU.mult), t1, t_x3)
                    free[OB[hf]] = [t1]
                    t_o3.append(dve.do(lambda e: e.tensor_tensor(O3[:, i, oc], O3[:, i, oc], SG[:, i, oc],
                                                                 ALU.mult), t1, t_sg2))
                hd["done"] = done
            heads.append(hd)
    at3.run(heads)
    g2b = reg(4096, D)
    t_gf2 = load(pool, g2b, A["g_final_2"].partition_broadcast(P), t_o3)
    OT3, t_OT3 = back(2048, O3, t_o3)
    t_x4 = residual("out3", OT3, t_OT3)
    ssf, rsf = col(2), col(2)
    tok = None
    for i in range(2):
        tok = square_sum(X[:, i, :], ssf[:, i:i + 1], reg(8192, D), D, t_x4, tok)
    t1 = rstd(rsf, ssf, tok)
    s_out = sem("s_out")
    for i in range(2):
        t = dve.do(lambda e, i=i: e.scalar_tensor_tensor(out=X[:, i, :], in0=X[:, i, :], scalar=rsf[:, i:i + 1],
                                                         in1=g2b, op0=ALU.mult, op1=ALU.mult), t1, t_gf2)
        act.dma(s_out, 0, lambda e, i=i: e.dma_start(out.rearrange("(t p) d -> p t d", p=P)[:, i, :], X[:, i, :]), t)
    act.wait((s_out, 32))

    ring_loads()

    block = ctx.enter_context(nc.Block())

    @block.sync
    def _(eng):
        sp.emit(eng)

    @block.tensor
    def _(eng):
        pe.emit(eng)

    @block.vector
    def _(eng):
        dve.emit(eng)

    @block.scalar
    def _(eng):
        act.emit(eng)

    @block.gpsimd
    def _(eng):
        pool.emit(eng)


DROP = {"c": 1, "b_mod": 1, "g_mix": 1, "g_ffn": 1, "w_mod": 1, "w_in": 1, "q_gain": 1, "k_gain": 1, "v_gain": 1,
        "w_s": 1, "b_s": 1, "w_out": 1, "w_router": 1, "w1": 1, "w3": 1, "w2": 1, "x": 1, "ctx": 1, "positions_2": 1,
        "e_g_in_2": 1, "e_w_in_2": 1, "e_g_q_a_2": 1, "e_w_q_up_2": 1, "e_g_kv_a_2": 1, "e_w_kv_up_2": 1,
        "e_sinks_2": 1, "e_w_out_2": 1, "o_g_in_2": 1, "o_w_in_2": 1, "o_b_f_2": 1, "o_w_out_2": 1}


def kernel(**inputs):
    import concourse.bacc as bacc
    from concourse.bass_utils import run_bass_kernel_spmd as run

    nc = bacc.Bacc("TRN2", target_bir_lowering=False, num_devices=1)
    arrays, aps = {}, {}
    for name in INS:
        a = np.ascontiguousarray(inputs[name])
        arrays["in_" + name] = a
        ap = nc.dram_tensor("in_" + name, a.shape, mybir.dt.from_np(a.dtype), kind="ExternalInput").ap()
        aps[name] = ap[0] if name in DROP else ap
    k = constants()
    arrays["in_consts"] = k
    kin = nc.dram_tensor("in_consts", k.shape, F32, kind="ExternalInput").ap()
    o = nc.dram_tensor("out_0", (1, T, D), F32, kind="ExternalOutput").ap()
    program(nc, aps, kin, o[0])
    r = run(nc, [arrays], core_ids=[0])
    return r.results[0]["out_0"]
```

```python
from contextlib import ExitStack

import numpy as np

import concourse.bass as bass
from concourse import mybir

F32 = mybir.dt.float32
I32 = mybir.dt.int32
ACT = mybir.ActivationFunctionType
ALU = mybir.AluOpType
AX = mybir.AxisListType

P = 128
D = 1024
T = 256
E = 16
SLOT = 4096
NSLOT = 7
EPS = 1e-6
NEG = -1.0e30

INS = ["x", "c", "ctx", "c_ctx", "w_mod", "b_mod", "g_mix", "g_ffn", "w_in", "q_gain", "k_gain", "v_gain",
       "w_s", "b_s", "w_out", "w_router", "w1", "w3", "w2", "g_final", "positions_2", "e_g_in_2", "e_w_in_2",
       "e_g_q_a_2", "e_w_q_up_2", "e_g_kv_a_2", "e_w_kv_up_2", "e_sinks_2", "e_w_out_2", "o_g_in_2",
       "o_w_in_2", "o_b_f_2", "o_w_out_2", "g_final_2"]

K_ID, K_TRI, K_CM, K_DIST, K_ONE, K_COS, K_SIN, K_IOTA, K_SLOT, K_INV, K_HALF, K_END = np.cumsum(
    [0, 128, 128, 256, 256, 128, 64, 64, 32, 1, 16, 16]).tolist()


def constants():
    k = np.zeros((P, K_END), np.float32)
    r = np.arange(P)
    k[:, K_ID:K_ID + 128] = np.eye(P)
    k[:, K_TRI:K_TRI + 128] = r[:, None] <= r[None, :]
    k[:, K_CM + 128:K_CM + 256] = np.where(r[None, :] <= r[:, None], 0.0, NEG)
    dist = 128 + r[:, None] - np.arange(256)[None, :]
    k[:, K_DIST:K_DIST + 256] = np.where((dist >= 0) & (dist < 128), dist, -NEG)
    k[:, K_ONE:K_ONE + 128] = 1.0
    f = np.float32
    inv = (f(10000.0) ** (-np.arange(16, dtype=f) / f(16))).astype(f)
    tok = np.arange(T)
    ang = np.concatenate([(tok // 64).astype(f)[:, None] * inv, (tok % 64).astype(f)[:, None] * inv], axis=1)
    k[:, K_COS:K_COS + 64] = np.cos(ang).astype(f).reshape(2, P, 32).transpose(1, 0, 2).reshape(P, 64)
    k[:, K_SIN:K_SIN + 64] = np.sin(ang).astype(f).reshape(2, P, 32).transpose(1, 0, 2).reshape(P, 64)
    k[:, K_IOTA:K_IOTA + 32] = np.arange(32)[None, :]
    k[:, K_SLOT] = r % 32
    k[:, K_INV:K_INV + 16] = (f(1.0) / (f(10000.0) ** (np.arange(0, 32, 2, dtype=f) / f(32)))).astype(f)[None, :]
    k[:, K_HALF:K_HALF + 16] = -0.5
    return k


class Queue:

    def __init__(self, name, sem):
        self.name, self.sem, self.ops, self.count, self.seen = name, sem, [], 0, {}

    def wait(self, *tokens):
        for t in tokens:
            if t is None:
                continue
            if isinstance(t, list):
                self.wait(*t)
                continue
            sem, value = t
            if self.seen.get(id(sem), 0) < value:
                self.seen[id(sem)] = value
                self.ops.append(lambda e, s=sem, v=value: e.wait_ge(s, v))

    def do(self, fn, *after, mark=True):
        self.wait(*after)
        if mark:
            self.count += 1
            self.ops.append(lambda e: fn(e).then_inc(self.sem, 1))
            return (self.sem, self.count)
        self.ops.append(fn)

    def dma(self, sem, level, fn, *after):
        self.wait(*after)
        self.ops.append(lambda e: fn(e).then_inc(sem, 16))
        return (sem, level)

    def emit(self, eng):
        for op in self.ops:
            op(eng)


def program(nc, ins, kin, out):
    with ExitStack() as ctx:
        body(ctx, nc, ins, kin, out)


def body(ctx, nc, A, kin, out):
    nsem = [0]

    def sem(name):
        nsem[0] += 1
        return ctx.enter_context(nc.semaphore(name))

    pe = Queue("pe", sem("s_pe"))
    dve = Queue("dve", sem("s_dve"))
    act = Queue("act", sem("s_act"))
    pool = Queue("pool", sem("s_pool"))
    sp = Queue("sp", sem("s_sp"))

    ring = ctx.enter_context(nc.sbuf_tensor("ring", [P, NSLOT, SLOT], F32))
    PS = ctx.enter_context(nc.psum_tensor("PS", [P, 8, 512], F32))

    def sb(name, *shape, dt=F32):
        return ctx.enter_context(nc.sbuf_tensor(name, [P, *shape], dt))

    KC = sb("KC", K_END)
    ident = KC[:, K_ID:K_ID + 128]
    tri = KC[:, K_TRI:K_TRI + 128]
    cmask = KC[:, K_CM:K_CM + 256]
    dist = KC[:, K_DIST:K_DIST + 256]
    ones = KC[:, K_ONE:K_ONE + 128]
    iota = KC[:, K_IOTA:K_IOTA + 32]
    slotc = KC[:, K_SLOT:K_SLOT + 1]
    invf = KC[:, K_INV:K_INV + 16]

    X = sb("X", 2, D)
    qgb = sb("qgb", 64)
    kgb = sb("kgb", 64)
    SG = sb("SG", 2, D)
    vgb = SG[:, 0, 0:512]
    sinkb = sb("sinkb", 8)
    bfb = sb("bfb", 16)
    gfb = SG[:, 0, :]
    gtb = SG[:, 1, :]

    RT = sb("RT", 59)
    bm = sb("bm", 3, 512)
    mrow = bm
    mcol = sb("mcol", 3, 4, 4, 2)
    ab = sb("ab", 6, 8)
    cvec = sb("cvec", 8, 32)
    wr = sb("wr", 8, E)
    wf = sb("wf", 8, 16)
    rcs = sb("rcs", 2, 2, 16)
    st = sb("st", 486)
    SC = 16384
    S = sb("S", SC)

    def reg(off, *shape):
        n = int(np.prod(shape))
        assert off + n <= SC, (off, n)
        v = S[:, off:off + n]
        if len(shape) > 1:
            names = "abcd"[:len(shape)]
            v = v.rearrange("p (" + " ".join(names) + ") -> p " + " ".join(names),
                            **{k: s for k, s in zip(names, shape)})
        return v

    R = reg(12288, 128)
    stn = [0]

    def col(n=1):
        stn[0] += n
        assert stn[0] <= 486
        return st[:, stn[0] - n:stn[0]]

    def bc(ap, shape, *axes):
        for a in axes:
            ap = ap.unsqueeze(a)
        return ap.to_broadcast(shape)

    free = {b: [] for b in range(8)}
    turn = {}

    def bank(group):
        i = turn.get(group, 0)
        while free[group[i % len(group)]] is None and i < turn.get(group, 0) + len(group):
            i += 1
        turn[group] = i + 1
        b = group[i % len(group)]
        assert free[b] is not None, f"bank {b} still held"
        t, free[b] = free[b], None
        return b, t

    ALL6 = (0, 1, 2, 3, 4, 5)
    OB = (6, 7)
    B4 = (0, 1, 2, 3)

    def load(q, dst, src, *after):
        s = sem(f"s_l{nsem[0]}")
        return q.dma(s, 16, lambda e: e.dma_start(dst, src), *after)

    t_r = [load(sp, R[8 * i:8 * i + 8, :], A[n].rearrange("(j p) -> j p", p=P))
           for i, n in enumerate(["c", "c_ctx", "g_mix", "g_ffn", "e_g_in_2", "o_g_in_2"])]
    t_r.append(load(sp, R[48:56, :], A["b_s"]))
    t_r.append(load(sp, R[56:58, :], A["e_g_q_a_2"].rearrange("(j p) -> j p", p=P)))
    t_r.append(load(sp, R[58:59, :], A["e_g_kv_a_2"].rearrange("(j p) -> j p", p=P)))
    t_k = load(act, KC[:], kin)

    ring_sem = [sem(f"s_w{i}") for i in range(NSLOT)]
    units = []
    t_used = {}

    def unit(key, src, k, w):
        units.append(key)
        u = len(units) - 1
        slot = u % NSLOT
        dst = ring[:, slot, 0:k * w].rearrange("p (k w) -> p k w", k=k)
        before = []
        if u >= NSLOT:
            before = [("used", units[u - NSLOT])]
        place[key] = (dst, (ring_sem[slot], 16 * (u // NSLOT + 1)))
        pending.append((dst, src, ring_sem[slot], before))

    place, pending = {}, []

    def weight(key):
        dst, tok = place[key]
        pe.wait(tok)
        return dst

    def kview(ap):
        return ap.rearrange("(k p) n -> p k n", p=P)

    wm = kview(A["w_mod"])
    for G in range(1):
        for k in range(4):
            unit(("mod", G, k), wm[:, 2 * k:2 * k + 2, 2048 * G:2048 * G + 2048], 2, 2048)
    wi = kview(A["w_in"])
    IN1 = [("kv", 512, 256), ("q", 0, 512), ("vv", 1280, 512), ("u", 768, 512)]
    for n, o, w in IN1:
        unit(("in", n), wi[:, :, o:o + w], 8, w)
    for G in range(1, 3):
        for k in range(4):
            unit(("mod", G, k), wm[:, 2 * k:2 * k + 2, 2048 * G:2048 * G + 2048], 2, 2048)
    for h in range(2):
        unit(("out1", h), kview(A["w_out"])[:, :, 512 * h:512 * h + 512], 8, 512)
    for e in range(E):
        for n in ("w1", "w3"):
            for k in range(4):
                unit((n, e, k), kview(A[n][e])[:, 2 * k:2 * k + 2, :], 2, 2048)
        for j in range(4):
            unit(("w2", e, j), kview(A["w2"][e])[:, 4 * j:4 * j + 4, :], 4, 1024)
    we = kview(A["e_w_in_2"])
    for n, o, w in [("a", 0, 416), ("qs", 416, 512), ("kvs", 928, 256), ("g1", 1696, 512), ("g0", 1184, 512)]:
        unit(("e", n), we[:, :, o:o + w], 8, w)
        if n == "kvs":
            unit(("qup",), kview(A["e_w_q_up_2"]), 2, 768)
            unit(("kvup",), kview(A["e_w_kv_up_2"]), 1, 1024)
    for h in range(2):
        unit(("out2", h), kview(A["e_w_out_2"])[:, :, 512 * h:512 * h + 512], 8, 512)
    wo = kview(A["o_w_in_2"])
    for n, o in [("q0", 0), ("q1", 512), ("k0", 1024), ("k1", 1536), ("v0", 2048), ("v1", 2560),
                 ("g0", 3088), ("g1", 3600)]:
        unit(("o", n), wo[:, :, o:o + 512], 8, 512)
    for h in range(2):
        unit(("out3", h), kview(A["o_w_out_2"])[:, :, 512 * h:512 * h + 512], 8, 512)

    small = {}

    def ring_loads():
        for n, (dst, src, s, before) in enumerate(pending):
            sp.wait(*[t_used[key] for _, key in before])
            sp.ops.append(lambda e, dst=dst, src=src, s=s: e.dma_start(dst, src).then_inc(s, 16))

    XC = reg(6144, 2, D)
    t_x = load(act, X[:], A["x"].rearrange("(t p) d -> p t d", p=P))
    t_c = load(act, XC, A["ctx"].rearrange("(t p) d -> p t d", p=P))
    t_qg = load(act, qgb[:], A["q_gain"].partition_broadcast(P))
    t_kg = load(act, kgb[:], A["k_gain"].partition_broadcast(P))
    t_vg = load(act, vgb, A["v_gain"].partition_broadcast(P))
    WS = reg(14336, 8, 128)
    t_ws = load(act, WS, A["w_s"].rearrange("g i j -> i g j"))
    t_bm0 = dve.do(lambda e: e.memset(bm[:], 0.0))
    t_bm = []
    for r in range(2):
        for j in range(4):
            t_bm.append(load(act, bm[32 * j + r:32 * j + r + 1, :, :],
                             A["b_mod"].rearrange("(g j n) -> j g n", j=4, n=512)[j:j + 1], t_bm0))
    t_wr = load(act, wr[:], kview(A["w_router"]))
    t_sk = load(act, sinkb[:], A["e_sinks_2"].partition_broadcast(P))
    t_bf = load(act, bfb[:], A["o_b_f_2"].partition_broadcast(P))
    t_wf = load(act, wf[:], kview(A["o_w_in_2"])[:, :, 3072:3088])

    def rstd(outc, ssq, *after):
        n = ssq.shape[-1]
        t = pool.do(lambda e: e.tensor_scalar(outc, ssq, EPS, None, ALU.add), *after)
        return pool.do(lambda e: e.tensor_tensor(outc, outc, KC[:, K_HALF:K_HALF + n], ALU.pow), t)

    def square_sum(in_, outc, junk, width, *after):
        return act.do(lambda e: e.activation(junk, in_, ACT.Square, scale=float(width) ** -0.5, accum_out=outc),
                      *after)

    def transposes(group, pieces, after, parts=P):
        b, fr = bank(group)
        pe.wait(fr, after)
        for i, in_ in enumerate(pieces):
            tok = pe.do(lambda e, i=i, in_=in_, b=b: e.transpose(PS[0:parts, b, 128 * i:128 * i + 128], in_, ident),
                        mark=i == len(pieces) - 1)
        return b, tok

    ev = [0]

    def evac(dst, src, *after):
        ev[0] += 1
        if ev[0] % 2:
            return dve.do(lambda e: e.tensor_copy(dst, src), *after)
        return act.do(lambda e: e.activation(dst, src, ACT.Copy), *after)

    pe.wait(t_k)
    b, fr = bank(ALL6)
    tok = pe.do(lambda e: e.transpose(PS[:, 0, 0:59], R[0:59, :], ident[0:59, 0:59]), t_r)
    t_rt = dve.do(lambda e: e.tensor_copy(RT[:], PS[:, 0, 0:59]), tok)
    free[b] = [t_rt]
    t_cz = pool.do(lambda e: e.memset(cvec[:], 0.0))
    act.wait(t_rt, t_cz)
    t_cv = [act.do(lambda e, r=r: e.activation(cvec[:, :, r], RT[:, 8 * r:8 * r + 8], ACT.Silu)) for r in range(2)]

    c_gmix, c_gffn, c_ge, c_go = [RT[:, 8 * i:8 * i + 8] for i in (2, 3, 4, 5)]
    c_bs, c_qa, c_kva = RT[:, 48:56], RT[:, 56:58], RT[:, 58:59]

    t_mcol = {}
    t_mrow = {}

    def modulation_steps(G):
        held = []

        def step(k):
            if k == 0:
                b, fr = bank(ALL6)
                held.append(b)
                pe.wait(fr, t_cv)
            b = held[0]
            w = weight(("mod", G, k))
            for kk in range(2):
                for j in range(4):
                    tok = pe.do(lambda e, w=w, k=k, kk=kk, j=j, b=b: e.matmul(
                        PS[32 * j:32 * j + 32, b, :], cvec[:, 2 * k + kk, :], w[:, kk, 512 * j:512 * j + 512],
                        start=(k == 0 and kk == 0), stop=(k == 3 and kk == 1)), mark=(kk == 1 and j == 3))
            t_used[("mod", G, k)] = tok
            if k == 3:
                t = dve.do(lambda e: e.tensor_tensor(mrow[:, G, :], PS[:, b, :], bm[:, G, :], ALU.add), tok, t_bm, t_bm0)
                free[b] = [t]
                t_mrow[G] = t

        return [lambda k=k: step(k) for k in range(4)]

    def modulation(G):
        for step in modulation_steps(G):
            step()

    def modulation_cols(G):
        b, tok = transposes(ALL6, [mrow[:, G, 128 * s:128 * s + 128] for s in range(4)], t_mrow[G])
        t_mcol[G] = dve.do(lambda e: e.tensor_copy(
            mcol[:, G, :, :, :], PS[:, b, :].rearrange("p (s j r) -> p s j r", s=4, r=32)[:, :, :, 0:2]),
                           tok)
        free[b] = [t_mcol[G]]

    def mvec(G, unit0, r):
        return mcol[:, G, :, unit0:unit0 + 2, r].rearrange("p s j -> p j s")

    def ab8(i):
        return ab[:, i, :].rearrange("p (j s) -> p j s", j=2)

    XN = reg(4096, 2, D)
    junk = reg(12288, D)
    junk2 = reg(8192 + 2048, D)
    ss1 = col(4)
    rs1 = col(4)
    tok = t_cv[-1]
    tok2 = None
    for i in (0, 2):
        src, src2 = (X if i < 2 else XC)[:, 0, :], (X if i < 2 else XC)[:, 1, :]
        tok = square_sum(src, ss1[:, i:i + 1], junk, D, t_x if i < 2 else t_c, tok)
        tok2 = dve.do(lambda e, src2=src2, i=i: e.tensor_tensor_reduce(
            junk2, src2, src2, 1.0 / D, 0.0, ALU.mult, ALU.add, ss1[:, i + 1:i + 2]), t_x if i < 2 else t_c, tok2)
    t_rs1 = rstd(rs1, ss1, tok, tok2)
    t_xn = []
    for i in range(4):
        src = X[:, i, :] if i < 2 else XC[:, i - 2, :]
        dst = XN[:, i, :] if i < 2 else XC[:, i - 2, :]
        t_xn.append(dve.do(lambda e, src=src, dst=dst, i=i: e.tensor_scalar(dst, src, rs1[:, i:i + 1], None, ALU.mult),
                           t_rs1))
    hT = reg(0, 8, 512)
    t_raw = []
    for k in range(8):
        b, tok = transposes(ALL6, [(XN if i < 2 else XC)[:, i % 2, 128 * k:128 * k + 128] for i in range(4)], t_xn)
        t_raw.append(evac(hT[:, k, :], PS[:, b, :], tok))
        free[b] = [t_raw[-1]]
    modulation(0)
    modulation_cols(0)
    t_ab = []
    for r in range(2):
        t_ab.append(dve.do(lambda e, r=r: e.scalar_tensor_tensor(
            out=ab8(2 * r), in0=mvec(0, 2, r), scalar=1.0, in1=c_gmix.rearrange("p (j s) -> p j s", j=2),
            op0=ALU.add, op1=ALU.mult), t_mcol[0]))
        t_ab.append(dve.do(lambda e, r=r: e.tensor_copy(ab8(2 * r + 1), mvec(0, 0, r))))
    t_hT = []
    for k in range(8):
        for r in range(2):
            v = hT[:, k, 256 * r:256 * r + 256]
            a_, b_ = ab[:, 2 * r, k:k + 1], ab[:, 2 * r + 1, k:k + 1]
            if r == 0:
                t_hT.append(dve.do(lambda e, v=v, a_=a_, b_=b_: e.tensor_scalar(v, v, a_, b_, ALU.mult, ALU.add),
                                   t_raw, t_ab))
            else:
                t_hT.append(act.do(lambda e, v=v, a_=a_, b_=b_: e.activation(v, v, ACT.Identity, bias=b_, scale=a_),
                                   t_raw, t_ab))

    def project(key, h, tile, width, group, k8=8, o=0, after=()):
        b, fr = bank(group)
        pe.wait(fr, *after)
        w = weight(key)
        for k in range(k8):
            tok = pe.do(lambda e, k=k: e.matmul(PS[:, b, 0:width], h[:, k, 128 * tile:128 * tile + 128],
                                                w[:, k, o:o + width], start=(k == 0), stop=(k == k8 - 1)),
                        mark=k == k8 - 1)
        t_used[key] = tok
        return b, tok

    KV = reg(9216, 4, 256)
    KR = reg(10240, 4, 128)
    sqk = reg(10752, 4, 128)
    ssk, rsk = col(8), col(8)
    b_kv, t_kvp = [], []
    for i in range(4):
        b, tok = project(("in", "kv"), hT, i, 256, ALL6, after=[t_hT])
        tok = act.do(lambda e, b=b, i=i: e.activation(KV[:, i, :], PS[:, b, 0:256], ACT.Copy), tok)
        t_kvp.append(tok)
        free[b] = [tok]
    t_kvev = t_kvp[-1]
    tabq = reg(11264, 4, 2, 32)
    tabk = reg(11520, 4, 2, 32)
    cosT = KC[:, K_COS:K_COS + 64].rearrange("p (t f) -> p t f", t=2)
    sinT = KC[:, K_SIN:K_SIN + 64].rearrange("p (t f) -> p t f", t=2)
    t_tab = []
    for tab, g in ((tabq, qgb), (tabk, kgb)):
        for i, (tr, half) in enumerate(((cosT, 0), (sinT, 1), (sinT, 0), (cosT, 1))):
            t_tab.append(pool.do(lambda e, tab=tab, i=i, tr=tr, half=half, g=g: e.tensor_tensor(
                tab[:, i, :, :], tr, bc(g[:, 32 * half:32 * half + 32], [P, 2, 32], 1), ALU.mult), t_qg, t_kg, t_k))
    kh = KV[:, :, 0:128].rearrange("p t (g d) -> p t g d", g=2)
    t1 = dve.do(lambda e: e.tensor_tensor(sqk, KV[:, :, 0:128], KV[:, :, 0:128], ALU.mult), t_kvev)
    t1 = dve.do(lambda e: e.tensor_reduce(ssk, sqk.rearrange("p t (g d) -> p (t g) d", g=2), AX.X, ALU.add), t1)
    t1 = dve.do(lambda e: e.tensor_scalar(ssk, ssk, 1.0 / 64, None, ALU.mult), t1)
    t1 = rstd(rsk, ssk, t1)
    t_kn = dve.do(lambda e: e.tensor_tensor(kh, kh, bc(rsk.rearrange("p (t g) -> p t g", g=2), [P, 4, 2, 64], 3),
                                            ALU.mult), t1)
    rt = reg(11776, 2, 2, 2, 32)

    def rope(dst1, dst2, x1, x2, c1, s2, s1, c2, tmp, *after):
        ta = dve.do(lambda e: e.tensor_tensor(dst1, x1, c1, ALU.mult), *after)
        tb = dve.do(lambda e: e.tensor_tensor(tmp[0], x2, s2, ALU.mult))
        tc = dve.do(lambda e: e.tensor_tensor(dst2, x1, s1, ALU.mult))
        td = dve.do(lambda e: e.tensor_tensor(tmp[1], x2, c2, ALU.mult))
        te = dve.do(lambda e: e.tensor_tensor(dst1, dst1, tmp[0], ALU.subtract), tb)
        return [te, dve.do(lambda e: e.tensor_tensor(dst2, dst2, tmp[1], ALU.add), td)]

    krh = KR.rearrange("p t (g d) -> p t g d", g=2)

    def kt_(i):
        return bc(tabk[:, i, :, :], [P, 2, 2, 32], 2)

    t_kr = rope(krh[:, 0:2, :, 0:32], krh[:, 0:2, :, 32:64], kh[:, 0:2, :, 0:32], kh[:, 0:2, :, 32:64],
                kt_(0), kt_(1), kt_(2), kt_(3), (rt[:, 0], rt[:, 1]), t_kn, t_tab)
    t_kr.append(dve.do(lambda e: e.tensor_tensor(krh[:, 2:4, :, :], kh[:, 2:4, :, :],
                                                 bc(kgb[:], [P, 2, 2, 64], 1, 1), ALU.mult), t_kn))
    QN = reg(6144, 2, 512)
    QR = reg(7168, 2, 512)
    sqq = reg(12288, 2, 512)
    ssq, rsq = col(16), col(16)
    t_qr = []
    for i in range(2):
        b, tok = project(("in", "q"), hT, i, 512, ALL6)
        qv = QN[:, i, :].rearrange("p (h d) -> p h d", h=8)
        t1 = act.do(lambda e, b=b, i=i: e.activation(sqq[:, i, :], PS[:, b, :], ACT.Square, scale=0.125), tok)
        t1 = dve.do(lambda e, i=i: e.tensor_reduce(ssq[:, 8 * i:8 * i + 8],
                                                   sqq[:, i, :].rearrange("p (h d) -> p h d", h=8), AX.X, ALU.add), t1)
        t1 = rstd(rsq[:, 8 * i:8 * i + 8], ssq[:, 8 * i:8 * i + 8], t1)
        t1 = dve.do(lambda e, b=b, i=i, qv=qv: e.tensor_tensor(
            qv, PS[:, b, :].rearrange("p (h d) -> p h d", h=8), bc(rsq[:, 8 * i:8 * i + 8], [P, 8, 64], 2), ALU.mult), t1)
        free[b] = [t1]
        src = QN[:, i, :].rearrange("p (g n d) -> p g n d", g=2, n=4)
        dst = QR[:, i, :].rearrange("p (n g d) -> p g n d", g=2, n=4)

        tmpv = S[:, 13312:13312 + 512].rearrange("p (a g n d) -> p a g n d", a=2, g=2, n=4)

        def qt_(n, i=i):
            return bc(tabq[:, n, i, :], [P, 2, 4, 32], 1, 1)

        t_qr += rope(dst[:, :, :, 0:32], dst[:, :, :, 32:64], src[:, :, :, 0:32], src[:, :, :, 32:64],
                     qt_(0), qt_(1), qt_(2), qt_(3), (tmpv[:, 0], tmpv[:, 1]), t1, t_tab, t_qr)
    VV = reg(4096, 2, 512)
    U = reg(5120, 2, 512)
    t_vv, t_u = [], []

    def gelu_part(n, dst, lst, i):
        b, tok = project(("in", n), hT, i, 512, ALL6)
        tok = act.do(lambda e, b=b, i=i, dst=dst: e.activation(dst[:, i, :], PS[:, b, :], ACT.Gelu), tok, t_hT, t_raw)
        free[b] = [tok]
        lst.append(tok)

    for i in range(2):
        gelu_part("vv", VV, t_vv, i)
    KT = reg(8192, 512)
    b, tok = transposes(ALL6, [KR[:, i, :] for i in range(4)], t_kr)
    t_KT = evac(KT, PS[:, b, :], tok)
    free[b] = [t_KT]

    QT = reg(12288, 2, 512)
    t_QT = []
    for i in range(2):
        b, tok = transposes(ALL6, [QR[:, i, 128 * n:128 * n + 128] for n in range(4)], t_qr)
        t = evac(QT[:, i, :], PS[:, b, :], tok)
        free[b] = [t]
        t_QT.append(t)

    ssv, rsv = col(2), col(2)
    jv = reg(10752, 512)
    tok = None
    for i in range(2):
        tok = act.do(lambda e, i=i: e.activation(jv, VV[:, i, :], ACT.Square, scale=512.0 ** -0.5,
                                                 accum_out=ssv[:, i:i + 1]), t_vv, t_kn, tok)
    t1 = rstd(rsv, ssv, tok)
    t_vn = []
    for i in range(2):
        t_vn.append(dve.do(lambda e, i=i: e.scalar_tensor_tensor(
            out=VV[:, i, :], in0=VV[:, i, :], scalar=rsv[:, i:i + 1], in1=vgb, op0=ALU.mult, op1=ALU.mult),
            t1, t_vg))

    def interleaved(a, b_):
        return [h for two in zip(a, b_) for h in two]

    def attention(pairs, pbuf, ptbuf, before, fillers=()):
        fillers = list(fillers)
        pfree = [[before] for _ in pbuf]
        ptfree = [[before] for _ in ptbuf]
        n_p = n_pt = 0
        live = []

        def fill():
            if fillers:
                fillers.pop(0)()

        for n in range(len(pairs) + 1):
            now = []
            if n < len(pairs):
                two = pairs[n]
                for ld in two:
                    b, fr = bank(ALL6)
                    pe.wait(fr)
                    now.append([ld, b, None])
                for hh in range(len(two[0]["heads"])):
                    for it in now:
                        it[2] = it[0]["heads"][hh][0](it[1], hh * it[0]["nk"])
                for it in now:
                    ld, b, tok = it
                    m = n_p % len(pbuf)
                    n_p += 1
                    t_e, t_fr = ld["soft"](b, pbuf[m], tok, pfree[m])
                    free[b] = [t_fr]
                    it[1:] = [m, t_e]
            fill()
            stage = []
            for ld, m, t_e in live:
                m2 = n_pt % len(ptbuf)
                n_pt += 1
                b, tok = transposes(ALL6, [pbuf[m][:, 128 * i:128 * i + 128] for i in range(4)], t_e)
                pfree[m] = [tok]
                t = evac(ptbuf[m2], PS[:, b, :], tok, ptfree[m2])
                free[b] = [t]
                stage.append((ld, m2, t))
            fill()
            for ld, m2, t in stage:
                pe.wait(t, *[w() if callable(w) else w for w in ld["wait"]])
                nt = ld["nk"] // 128
                for hh, (_, values, o) in enumerate(ld["heads"]):
                    for i in range(nt):
                        c = 128 * (nt * hh + i)
                        last = hh == len(ld["heads"]) - 1 and i == nt - 1
                        tok = pe.do(lambda e, c=c, o=o, v=values[i], m2=m2, i=i, nt=nt: e.matmul(
                            o, ptbuf[m2][:, c:c + 128], v, start=(i == 0), stop=(i == nt - 1)), mark=last)
                ptfree[m2] = [tok]
                if "done" in ld:
                    ld["done"](tok)
            live = now
        while fillers:
            fill()

    MIX = reg(10240, 2, D)
    PB = [reg(6144 + 512 * i, 512) for i in range(4)]
    PT = [reg(13312, 512), reg(13824, 512), reg(8704, 512)]
    mx1, nm1, sm1, ri1 = col(16), col(16), col(16), col(16)
    t_mixa = []
    pairs = []
    for i in range(2):
        for n in range(4):
            two = []
            for g in range(2):
                idx = 8 * i + 4 * g + n

                def score(b, c, i=i, n=n, g=g):
                    pe.wait(t_QT, t_KT)
                    return pe.do(lambda e: e.matmul(PS[:, b, :], QT[64 * g:64 * g + 64, i, 128 * n:128 * n + 128],
                                                    KT[64 * g:64 * g + 64, :], start=True, stop=True))

                def soft(b, p, tok, before, c=slice(idx, idx + 1)):
                    t1 = dve.do(lambda e: e.tensor_reduce(mx1[:, c], PS[:, b, :], AX.X, ALU.max), tok)
                    t1 = dve.do(lambda e: e.tensor_scalar(nm1[:, c], mx1[:, c], -0.125, None, ALU.mult), t1)
                    t1 = act.do(lambda e: e.activation(p, PS[:, b, :], ACT.Exp, bias=nm1[:, c], scale=0.125,
                                                       accum_out=sm1[:, c]), t1, before)
                    return t1, t1

                ld = dict(nk=512, soft=soft, wait=[t_kvp] + ([free[OB[i]]] if n == 0 and g == 0 else []),
                          heads=[(score, [KV[:, s_, 128 + 64 * g:192 + 64 * g] for s_ in range(4)],
                                  PS[:, OB[i], 64 * (4 * g + n):64 * (4 * g + n) + 64])])
                if n == 3 and g == 1:
                    def done(tok, i=i):
                        t1 = dve.do(lambda e: e.reciprocal(ri1[:, 8 * i:8 * i + 8], sm1[:, 8 * i:8 * i + 8]), tok)
                        t1 = dve.do(lambda e: e.tensor_tensor(
                            MIX[:, i, 0:512].rearrange("p (h d) -> p h d", h=8),
                            PS[:, OB[i], :].rearrange("p (h d) -> p h d", h=8),
                            bc(ri1[:, 8 * i:8 * i + 8], [P, 8, 64], 2), ALU.mult), t1, t_vn)
                        free[OB[i]] = [t1]
                        t_mixa.append(t1)
                    ld["done"] = done
                two.append(ld)
            pairs.append(two)

    WST = reg(15360, 8, 128)
    t_wst = []

    def turn_ws(hlf):
        b, tok = transposes(ALL6, [WS[:, 4 * hlf + i, :] for i in range(4)], t_ws)
        t = evac(WST[:, 4 * hlf:4 * hlf + 4, :], PS[:, b, :].rearrange("p (g i) -> p g i", g=4), tok)
        free[b] = [t]
        t_wst.append(t)

    t_mixg = []

    def mixed(i):
        b, fr = bank(ALL6)
        pe.wait(fr, t_wst, t_vn)
        for g in range(8):
            tok = pe.do(lambda e, b=b, g=g, i=i: e.matmul(PS[:, b, 64 * g:64 * g + 64], WST[:, g, :],
                                                          VV[:, i, 64 * g:64 * g + 64], start=True, stop=True),
                        mark=g == 7)
        mg = MIX[:, i, 512:1024].rearrange("p (g d) -> p g d", g=8)
        t1 = dve.do(lambda e, b=b, mg=mg: e.tensor_tensor(mg, PS[:, b, :].rearrange("p (g d) -> p g d", g=8),
                                                          bc(c_bs, [P, 8, 64], 2), ALU.add), tok, t_vn, t_QT, t_KT)
        free[b] = [t1]
        t_mixg.append(dve.do(lambda e, i=i: e.tensor_tensor(MIX[:, i, 512:1024], MIX[:, i, 512:1024], U[:, i, :],
                                                            ALU.mult), t1, t_u))

    fillers = [lambda: gelu_part("u", U, t_u, 0), lambda: gelu_part("u", U, t_u, 1),
               lambda: turn_ws(0), lambda: turn_ws(1), lambda: mixed(0), lambda: mixed(1)]
    for G in (1, 2):
        fillers += modulation_steps(G)
    attention(pairs, PB, PT, [t_QT, t_KT, t_kr], fillers)
    t_gf = load(pool, gfb, A["g_final"].partition_broadcast(P), t_vn)

    modulation_cols(1)
    modulation_cols(2)
    t_ab2 = [dve.do(lambda e: e.scalar_tensor_tensor(
        out=ab8(4), in0=mvec(2, 0, 0), scalar=1.0, in1=c_gffn.rearrange("p (j s) -> p j s", j=2),
        op0=ALU.add, op1=ALU.mult), t_mcol[2]),
        dve.do(lambda e: e.tensor_copy(ab8(5), mvec(1, 2, 0)), t_mcol[1])]
    t_gt1 = []
    for j in range(2):
        b, fr = bank(ALL6)
        tok = pe.do(lambda e, b=b, j=j: e.matmul(PS[:, b, :], ident[:, 32 * j:32 * j + 1].to_broadcast([P, 128]),
                                                 mrow[:, 1, :], start=True, stop=True), fr, t_mrow[1])
        t_gt1.append(act.do(lambda e, b=b, j=j: e.activation(gtb[:, 512 * j:512 * j + 512], PS[:, b, :], ACT.Copy), tok))
        free[b] = [t_gt1[-1]]

    def back(off, src, after):
        dst = reg(off, 8, 256)
        toks = []
        for m in range(4):
            b, tok = transposes(ALL6, [src[:, i, 128 * (2 * m + kk):128 * (2 * m + kk) + 128]
                                       for kk in range(2) for i in range(2)], after)
            t = evac(dst[:, 2 * m:2 * m + 2, :], PS[:, b, :].rearrange("p (k t) -> p k t", k=2), tok)
            free[b] = [t]
            toks.append(t)
        return dst, toks

    t_mix = t_mixa + t_mixg
    MT, t_MT = back(2048 + 2048, MIX, t_mix)
    G2 = reg(10240, 512)
    b, fr = bank(ALL6)
    pe.wait(fr, t_mrow[2])
    for j in range(2):
        tok = pe.do(lambda e, b=b, j=j: e.matmul(
            PS[64 * j:64 * j + 64, b, :], ident[:, 64 + 32 * j:65 + 32 * j].to_broadcast([P, 64]), mrow[:, 2, :],
            start=True, stop=True))
    t_g2 = act.do(lambda e, b=b: e.activation(G2, PS[:, b, :], ACT.Copy), tok, t_MT)
    free[b] = [t_g2]
    YT = reg(2048, 2, D)
    t_x1 = []
    for h in range(2):
        for i in range(2):
            b, tok = project(("out1", h), MT, i, 512, ALL6, after=[t_MT])
            c = slice(512 * h, 512 * h + 512)
            t1 = dve.do(lambda e, b=b, i=i, c=c: e.tensor_tensor(YT[:, i, c], PS[:, b, :], gtb[:, c], ALU.mult),
                        tok, t_gt1)
            free[b] = [t1]
            t_x1.append(dve.do(lambda e, i=i, c=c: e.tensor_tensor(X[:, i, c], X[:, i, c], YT[:, i, c], ALU.add), t1))
    t_mt_used = t_used[("out1", 1)]

    def quarter_squares(src, after, junk_off, jafter):
        ss_ = col(4)
        tok = None
        for h in range(2):
            for i in range(2):
                n = 2 * h + i
                tok = act.do(lambda e, h=h, i=i, n=n: e.activation(
                    reg(junk_off, 512), src[:, i, 512 * h:512 * h + 512], ACT.Square, scale=float(D) ** -0.5,
                    accum_out=ss_[:, n:n + 1]), after[n], jafter, tok)
        return ss_, tok

    def quarter_rstd(outc, ss_, tok):
        t1 = pool.do(lambda e: e.tensor_tensor(outc, ss_[:, 0:2], ss_[:, 2:4], ALU.add), tok)
        return rstd(outc, outc, t1)

    def normalise(dst, src, after, junk_off, jafter, dafter=None):
        ss_, tok = quarter_squares(src, after, junk_off, jafter)
        rs_ = col(2)
        t1 = quarter_rstd(rs_, ss_, tok)
        return [dve.do(lambda e: e.tensor_scalar(dst[:, 0, :], src[:, 0, :], rs_[:, 0:1], None, ALU.mult), t1, dafter),
                act.do(lambda e: e.activation(dst[:, 1, :], src[:, 1, :], ACT.Copy, scale=rs_[:, 1:2]), t1, dafter)]

    XN2 = reg(8192, 2, D)
    t_xn2 = normalise(XN2, X, t_x1, 6144, [t_mix])
    H2T = reg(4096, 8, 256)

    def turned(dst, src, a_col, b_col, after):
        toks = []
        for m in range(4):
            b, tok = transposes(ALL6, [src[:, i, 128 * (2 * m + kk):128 * (2 * m + kk) + 128]
                                       for kk in range(2) for i in range(2)], after)
            for kk in range(2):
                k = 2 * m + kk
                s_, d_ = PS[:, b, 256 * kk:256 * kk + 256], dst[:, k, :]
                eng = dve if m % 2 else act
                if eng is dve:
                    if b_col is None:
                        t = dve.do(lambda e, s_=s_, d_=d_, k=k: e.tensor_scalar(d_, s_, a_col[:, k:k + 1], None,
                                                                                ALU.mult), tok)
                    else:
                        t = dve.do(lambda e, s_=s_, d_=d_, k=k: e.tensor_scalar(
                            d_, s_, a_col[:, k:k + 1], b_col[:, k:k + 1], ALU.mult, ALU.add), tok)
                else:
                    bias = 0.0 if b_col is None else b_col[:, k:k + 1]
                    t = act.do(lambda e, s_=s_, d_=d_, k=k, bias=bias: e.activation(
                        d_, s_, ACT.Identity, bias=bias, scale=a_col[:, k:k + 1]), tok)
                toks.append(t)
            free[b] = [t]
        return toks

    act.wait(t_ab2)
    dve.wait(t_ab2)
    t_h2 = turned(H2T, XN2, ab[:, 4, :], ab[:, 5, :], t_xn2 + [t_mt_used])

    b, fr = bank(ALL6)
    pe.wait(fr, t_h2, t_wr)
    for i in range(2):
        for k in range(8):
            tok = pe.do(lambda e, b=b, i=i, k=k: e.matmul(PS[:, b, 16 * i:16 * i + 16], H2T[:, k, 128 * i:128 * i + 128],
                                                          wr[:, k, :], start=(k == 0), stop=(k == 7)),
                        mark=(i == 1 and k == 7))
    mxr, smr, rir = col(2), col(2), col(2)
    aff = col(32).rearrange("p (t e) -> p t e", t=2)
    lg = PS[:, b, 0:32].rearrange("p (t e) -> p t e", t=2)
    t1 = dve.do(lambda e: e.tensor_reduce(mxr, lg, AX.X, ALU.max), tok)
    t1 = dve.do(lambda e: e.tensor_scalar(mxr, mxr, -1.0, None, ALU.mult), t1)
    for i in range(2):
        t1 = act.do(lambda e, i=i, b=b: e.activation(aff[:, i, :], PS[:, b, 16 * i:16 * i + 16], ACT.Exp,
                                                bias=mxr[:, i:i + 1], accum_out=smr[:, i:i + 1]), t1)
    free[b] = [t1]
    t1 = dve.do(lambda e: e.reciprocal(rir, smr), t1)
    t_aff = dve.do(lambda e: e.tensor_tensor(aff, aff, bc(rir, [P, 2, 16], 2), ALU.mult), t1)
    b, fr = bank(ALL6)
    pe.wait(fr, t_aff)
    for i in range(2):
        tok = pe.do(lambda e, i=i, b=b: e.transpose(PS[0:16, b, 128 * i:128 * i + 128], aff[:, i, :], ident), mark=i == 1)
    o0 = 12288
    affT = reg(o0, 256)[0:16]
    wk = [reg(o0 + 256 + 256 * i, 256)[0:16] for i in range(2)]
    cum = reg(o0 + 768, 256)[0:16]
    pg = reg(o0 + 1024, 2, 256)[0:16]
    m8 = reg(o0 + 1536, 8)[0:16]
    t1 = dve.do(lambda e, b=b: e.tensor_copy(affT, PS[0:16, b, 0:256]), tok, t_mixa, t_mixg)
    free[b] = [t1]
    cur = affT
    for r in range(4):
        t1 = dve.do(lambda e, cur=cur: e.max(m8, cur), t1)
        t1 = dve.do(lambda e, cur=cur, r=r: e.match_replace(wk[r % 2], m8, cur, -1.0), t1)
        cur = wk[r % 2]
    sel = wk[0]
    t1 = dve.do(lambda e: e.tensor_scalar(sel, wk[1], -1.0, None, ALU.is_equal), t1)
    t_pgg = dve.do(lambda e: e.tensor_tensor(pg[:, 1, :], affT, sel, ALU.mult), t1)
    t1 = dve.do(lambda e: e.tensor_tensor_scan(cum, sel, sel, 0.0, ALU.add, ALU.bypass), t1)
    t1 = dve.do(lambda e: e.tensor_tensor(pg[:, 0, :], cum, sel, ALU.mult), t1)
    t_pg = dve.do(lambda e: e.tensor_scalar(pg[:, 0, :], pg[:, 0, :], -1.0, None, ALU.add), t1)
    b, fr = bank(ALL6)
    pe.wait(fr, t_pg)
    for i in range(2):
        tok = pe.do(lambda e, i=i, b=b: e.transpose(PS[:, b, 16 * i:16 * i + 16], pg[:, 0, 128 * i:128 * i + 128],
                                                    ident[0:16, 0:16]), mark=i == 1)
    SEL = reg(11264, 2, E, 32)
    post = col(32).rearrange("p (t e) -> p t e", t=2)
    t1 = dve.do(lambda e, b=b: e.tensor_copy(post, PS[:, b, 0:32].rearrange("p (t e) -> p t e", t=2)), tok)
    free[b] = [t1]
    t_sel = []
    for i in range(2):
        t_sel.append(dve.do(lambda e, i=i: e.tensor_tensor(
            SEL[:, i, :, :], bc(post[:, i, :], [P, E, 32], 2), bc(iota, [P, E, 32], 1), ALU.is_equal), t1))

    XE = reg(0, 8, 512)

    def gather(q, group):
        toks = []
        for kh in range(2):
            b, fr = bank(group)
            pe.wait(fr, t_sel)
            for kk in range(4):
                for i in range(2):
                    k = 4 * kh + kk
                    tok = pe.do(lambda e, b=b, i=i, k=k, kk=kk: e.matmul(
                        PS[:, b, 128 * kk:128 * kk + 128], XN2[:, i, 128 * k:128 * k + 128],
                        SEL[:, i, 4 * q:4 * q + 4, :].rearrange("p e s -> p (e s)"),
                        start=(i == 0), stop=(i == 1)), mark=(kk == 3 and i == 1))
            for kk in range(4):
                k = 4 * kh + kk
                s_, d_ = PS[:, b, 128 * kk:128 * kk + 128], XE[:, k, 128 * q:128 * q + 128]
                if kh:
                    t = dve.do(lambda e, s_=s_, d_=d_, k=k: e.tensor_scalar(d_, s_, ab[:, 4, k:k + 1], ab[:, 5, k:k + 1],
                                                                            ALU.mult, ALU.add), tok)
                else:
                    t = act.do(lambda e, s_=s_, d_=d_, k=k: e.activation(d_, s_, ACT.Identity, bias=ab[:, 5, k:k + 1],
                                                                         scale=ab[:, 4, k:k + 1]), tok)
            free[b] = [t]
            toks.append(t)
        return toks

    t_xe = gather(0, ALL6)
    t_xes = {0: t_xe}

    BIA = reg(14336, 8, 256)

    def tables(t_xe):
        t_bia = []
        for h in range(8):
            t_bia.append(pool.do(lambda e, h=h: e.tensor_scalar(BIA[:, h, :], dist, -8.0 * 2.0 ** -(h + 1), None, ALU.mult),
                                 t_wst, t_xe, t_mixg))
        posf = col(2)
        ang = col(32).rearrange("p (t f) -> p t f", t=2)
        nrd = col(32).rearrange("p (t f) -> p t f", t=2)
        C1 = 6.28125
        C2 = float(np.float32(np.float32((2 * np.pi - C1) * 2 ** 20).round() / 2 ** 20))
        C3 = float(np.float32(2 * np.pi - C1 - C2))
        MAG = 12582912.0
        prow = reg(13824, 128)[0:2]
        pflt = reg(13952, 128)[0:2]
        t_pos = load(pool, prow.bitcast(I32), A["positions_2"].rearrange("(t p) -> t p", p=P), t_xe)
        t1 = dve.do(lambda e: e.tensor_copy(pflt, prow.bitcast(I32)), t_pos)
        bp, fr = bank(B4)
        tok = pe.do(lambda e: e.transpose(PS[:, bp, 0:2], pflt, ident[0:2, 0:2]), fr, t1)
        t1 = dve.do(lambda e: e.tensor_copy(posf, PS[:, bp, 0:2]), tok)
        free[bp] = [t1]
        t_ang = None
        for i in range(2):
            t_ang = dve.do(lambda e, i=i: e.tensor_scalar(ang[:, i, :], invf, posf[:, i:i + 1], None, ALU.mult), t1)
        PI_ = 3.1415925
        t_rcs = []
        for n, (quarter, shift) in enumerate(((0.25, float(np.pi / 2)), (0.0, 0.0))):
            r_ = rcs[:, n, :, :]
            t1 = dve.do(lambda e, quarter=quarter: e.tensor_scalar(nrd, ang, float(1 / (2 * np.pi)), quarter,
                                                                   ALU.mult, ALU.add), t_ang, t_rcs)
            t1 = dve.do(lambda e: e.tensor_scalar(nrd, nrd, MAG, None, ALU.add), t1)
            t1 = dve.do(lambda e: e.tensor_scalar(nrd, nrd, MAG, None, ALU.subtract), t1)
            t1 = dve.do(lambda e, r_=r_: e.scalar_tensor_tensor(out=r_, in0=nrd, scalar=-C1, in1=ang,
                                                                op0=ALU.mult, op1=ALU.add), t1)
            for cc in (C2, C3):
                t1 = dve.do(lambda e, r_=r_, cc=cc: e.scalar_tensor_tensor(out=r_, in0=nrd, scalar=-cc, in1=r_,
                                                                           op0=ALU.mult, op1=ALU.add), t1)
            if shift:
                t1 = dve.do(lambda e, r_=r_, shift=shift: e.tensor_scalar(r_, r_, shift, None, ALU.add), t1)
            t1 = dve.do(lambda e, r_=r_: e.tensor_scalar(r_, r_, PI_, -PI_, ALU.min, ALU.max), t1)
            t_rcs.append(act.do(lambda e, r_=r_: e.activation(r_, r_, ACT.Sin), t1))

        return t_bia, t_rcs

    HB = [reg(4096 + 512 * i, 512) for i in range(2)]
    HT = [reg(5120 + 512 * i, 512) for i in range(2)]
    YE = [reg(6144 + 512 * i, 512) for i in range(2)]
    EQ = [reg(7168 + 256 * i, 256) for i in range(2)]
    GT = [reg(7680 + 256 * i, 256) for i in range(2)]
    t_hb, t_ht, t_ye, t_gt = [t_xe] * 2, [t_xe] * 2, [t_xe] * 2, [t_xe] * 2
    t_eq = [t_xe] * 2
    acc_free = [free[b] for b in (4, 5, 6, 7)]
    for b in (4, 5, 6, 7):
        free[b] = None
    gt_tok, ye_tok = {}, {}

    def scatter(e_):
        m = e_ % 2
        pe.wait(gt_tok[e_], ye_tok[e_])
        if e_ == 0:
            pe.wait(acc_free)
        for i in range(2):
            for dh in range(2):
                tok = pe.do(lambda e, i=i, dh=dh, m=m: e.matmul(
                    PS[:, 4 + 2 * i + dh, :], GT[m][64 * dh:64 * dh + 64, 128 * i:128 * i + 128],
                    YE[m][64 * dh:64 * dh + 64, :], start=(e_ == 0), stop=(e_ == E - 1)), mark=(i == 1 and dh == 1))
        t_ye[m] = t_gt[m] = tok
        return tok

    def up(name, e_, b):
        for k in range(4):
            w = weight((name, e_, k))
            for kk in range(2):
                for j in range(4):
                    tok = pe.do(lambda e, w=w, k=k, kk=kk, j=j: e.matmul(
                        PS[32 * j:32 * j + 32, b, :], XE[:, 2 * k + kk, 32 * e_:32 * e_ + 32],
                        w[:, kk, 512 * j:512 * j + 512],
                        start=(k == 0 and kk == 0), stop=(k == 3 and kk == 1)), mark=(kk == 1 and j == 3))
            t_used[(name, e_, k)] = tok
        return tok

    pe.wait(t_xe)
    for e_ in range(E):
        m = e_ % 2
        b, fr = bank(B4)
        tok = pe.do(lambda e, b=b, e_=e_: e.matmul(PS[:, b, :], ident[0:16, e_:e_ + 1].to_broadcast([16, 128]),
                                                   pg.rearrange("p a t -> p (a t)"), start=True, stop=True),
                    fr, t_pg, t_pgg)
        t1 = dve.do(lambda e, b=b, m=m: e.tensor_scalar(EQ[m], PS[:, b, 0:256], slotc, None, ALU.is_equal), tok, t_eq[m])
        t1 = dve.do(lambda e, b=b, m=m: e.tensor_tensor(GT[m], PS[:, b, 256:512], EQ[m], ALU.mult), t1, t_gt[m])
        t_eq[m] = gt_tok[e_] = t1
        free[b] = [t1]
        if e_ == 0:
            for q in range(1, 4):
                t_xes[q] = gather(q, B4)
        if e_ == 1:
            t_bia, t_rcs = tables(t_xes[3])
        pe.wait(t_xes[e_ // 4])
        b1, fr = bank(B4)
        pe.wait(fr)
        tok = up("w1", e_, b1)
        t_s = act.do(lambda e, b1=b1, m=m: e.activation(HB[m], PS[:, b1, :], ACT.Silu), tok, t_hb[m])
        free[b1] = [t_s]
        b3, fr = bank(B4)
        pe.wait(fr)
        if e_:
            scatter(e_ - 1)
        tok = up("w3", e_, b3)
        t_h = dve.do(lambda e, b3=b3, m=m: e.tensor_tensor(HB[m], PS[:, b3, :], HB[m], ALU.mult), tok, t_s)
        free[b3] = [t_h]
        b, tok = transposes(B4, [HB[m][:, 128 * s:128 * s + 128] for s in range(4)], t_h)
        t_hb[m] = tok
        t_t = act.do(lambda e, b=b, m=m: e.activation(HT[m], PS[:, b, :], ACT.Copy), tok, t_ht[m])
        free[b] = [t_t]
        b, fr = bank(B4)
        pe.wait(fr, t_t)
        for j in range(4):
            w = weight(("w2", e_, j))
            for s in range(4):
                for dh in range(2):
                    q = 64 * dh + 32 * (s % 2)
                    tok = pe.do(lambda e, b=b, w=w, j=j, s=s, dh=dh, q=q, m=m: e.matmul(
                        PS[q:q + 32, b, :], HT[m][:, 128 * s + 32 * j:128 * s + 32 * j + 32],
                        w[:, s, 512 * dh:512 * dh + 512], start=(j == 0 and s < 2), stop=(j == 3 and s >= 2)),
                        mark=(s == 3 and dh == 1))
            t_used[("w2", e_, j)] = tok
        t_ht[m] = tok
        ye_tok[e_] = dve.do(lambda e, b=b, m=m: e.tensor_tensor(YE[m], PS[:, b, :], G2, ALU.mult), tok, t_ye[m], t_g2)
        free[b] = [ye_tok[e_]]

    t_acc = scatter(E - 1)

    XN3 = reg(2048, 2, D)
    ssx, ssy = col(4), col(4)
    rs_, ra_ = col(2), col(2)
    tok, t_y = None, []
    for dh in range(2):
        for i in range(2):
            n = 2 * dh + i
            c = slice(512 * dh, 512 * dh + 512)
            t1 = dve.do(lambda e, i=i, dh=dh, c=c: e.tensor_tensor(X[:, i, c], PS[:, 4 + 2 * i + dh, :], X[:, i, c],
                                                                   ALU.add), t_acc)
            free[4 + 2 * i + dh] = [t1]
            tok = act.do(lambda e, i=i, c=c, n=n: e.activation(reg(0, 512), X[:, i, c], ACT.Square,
                                                               scale=float(D) ** -0.5, accum_out=ssx[:, n:n + 1]),
                         t1, tok)
            t2 = dve.do(lambda e, i=i, c=c: e.tensor_tensor(XN3[:, i, c], X[:, i, c], gfb[:, c], ALU.mult), t1, t_gf)
            t_y.append(t2)
            tok = act.do(lambda e, i=i, c=c, n=n: e.activation(reg(0, 512), XN3[:, i, c], ACT.Square,
                                                               scale=float(D) ** -0.5, accum_out=ssy[:, n:n + 1]),
                         t2, tok)
    t1 = quarter_rstd(rs_, ssx, tok)
    t2 = pool.do(lambda e: e.tensor_tensor(ra_, ssy[:, 0:2], ssy[:, 2:4], ALU.add), t1)
    t2 = pool.do(lambda e: e.tensor_tensor(ra_, ra_, rs_, ALU.mult), t2)
    t2 = pool.do(lambda e: e.tensor_tensor(ra_, ra_, rs_, ALU.mult), t2)
    t2 = rstd(ra_, ra_, t2)
    t2 = pool.do(lambda e: e.tensor_tensor(ra_, ra_, rs_, ALU.mult), t2)
    XF = reg(6144, 2, D)
    t_n = [dve.do(lambda e: e.tensor_scalar(XF[:, 0, :], XN3[:, 0, :], ra_[:, 0:1], None, ALU.mult), t2, t_y),
           act.do(lambda e: e.activation(XF[:, 1, :], XN3[:, 1, :], ACT.Copy, scale=ra_[:, 1:2]), t2, t_y)]
    t_xf = [pool.do(lambda e, i=i: e.tensor_scalar(X[:, i, :], XN3[:, i, :], rs_[:, i:i + 1], None, ALU.mult), t2, t_y)
            for i in range(2)]

    HE = reg(4096, 8, 256)
    t_HE = turned(HE, XF, c_ge, None, t_n + [t_acc])

    ZA = reg(0, 2, 416)
    t_za = []
    ssa, rsa = col(4), col(4)
    jk = reg(1024, 256)
    tj = None
    for i in range(2):
        b, tok = project(("e", "a"), HE, i, 416, ALL6, after=[t_HE])
        tz = dve.do(lambda e, b=b, i=i: e.tensor_copy(ZA[:, i, :], PS[:, b, 0:416]), tok, t_n)
        free[b] = [tz]
        tj = act.do(lambda e, i=i: e.activation(jk, ZA[:, i, 0:256], ACT.Square, scale=1.0 / 16,
                                                accum_out=ssa[:, 2 * i:2 * i + 1]), tz, tj, t_n)
        tj = act.do(lambda e, i=i: e.activation(jk[:, 0:128], ZA[:, i, 256:384], ACT.Square, scale=128.0 ** -0.5,
                                                accum_out=ssa[:, 2 * i + 1:2 * i + 2]), tj)
    t1 = rstd(rsa, ssa, tj)
    for i in range(2):
        t_za.append(dve.do(lambda e, i=i: e.tensor_scalar(ZA[:, i, 0:256], ZA[:, i, 0:256], rsa[:, 2 * i:2 * i + 1],
                                                          None, ALU.mult), t1))
        t_za.append(dve.do(lambda e, i=i: e.tensor_scalar(ZA[:, i, 256:384], ZA[:, i, 256:384],
                                                          rsa[:, 2 * i + 1:2 * i + 2], None, ALU.mult), t1))
    QST = reg(12800, 4, 256)
    KST = reg(3584, 2, 256)
    w = weight(("e", "qs"))
    t_qst = []
    for n2 in range(2):
        b, fr = bank(ALL6)
        pe.wait(fr)
        for nn in range(2):
            n = 2 * n2 + nn
            for k in range(8):
                tok = pe.do(lambda e, b=b, n=n, nn=nn, k=k, w=w: e.matmul(
                    PS[:, b, 256 * nn:256 * nn + 256],
                    w[:, k, 128 * n:128 * n + 128], HE[:, k, :],
                    start=(k == 0), stop=(k == 7)), mark=(nn == 1 and k == 7))
        t = evac(QST[:, 2 * n2:2 * n2 + 2, :], PS[:, b, :].rearrange("p (n t) -> p n t", n=2), tok, t_acc)
        free[b] = [t]
        t_qst.append(t)
    t_used[("e", "qs")] = tok
    w = weight(("e", "kvs"))
    b, fr = bank(ALL6)
    pe.wait(fr)
    for k in range(8):
        tok = pe.do(lambda e, b=b, k=k, w=w: e.matmul(PS[:, b, 0:256], w[:, k, 0:128], HE[:, k, :],
                                                      start=(k == 0), stop=(k == 7)), mark=k == 7)
    t_kst = None
    for g in range(2):
        for r in range(2):
            t_kst = dve.do(lambda e, b=b, g=g, r=r: e.tensor_copy(KST[64 * r:64 * r + 64, g, :],
                                                                  PS[64 * g:64 * g + 64, b, 0:256]), tok, t_HE, t_xf)
    free[b] = [t_kst]
    VS = reg(14080, 2, 128)
    t_vs = []
    for i in range(2):
        b, tok = project(("e", "kvs"), HE, i, 128, ALL6, o=128)
        t_vs.append(act.do(lambda e, b=b, i=i: e.activation(VS[:, i, :], PS[:, b, 0:128], ACT.Copy), tok, t_rcs))
        free[b] = [t_vs[-1]]
    CT = reg(1024 + 256, 3, 256)
    t_ct = []
    for kk in range(3):
        b, tok = transposes(ALL6, [ZA[:, i, 128 * kk:128 * kk + 128] for i in range(2)], t_za)
        g_ = c_qa[:, kk:kk + 1] if kk < 2 else c_kva
        t_ct.append(dve.do(lambda e, b=b, kk=kk, g_=g_: e.tensor_scalar(CT[:, kk, :], PS[:, b, 0:256], g_, None,
                                                                        ALU.mult), tok, t_n))
        free[b] = [t_ct[-1]]
    KP = col(64).rearrange("p (t f) -> p t f", t=2)
    rtmp = reg(13824, 2, 8, 16)
    kt2 = [rtmp[:, a, 0:2, :] for a in range(2)]
    cs, sn = rcs[:, 0, :, :], rcs[:, 1, :, :]
    t_kp = rope(KP[:, :, 0:16], KP[:, :, 16:32], ZA[:, :, 384:400], ZA[:, :, 400:416], cs, sn, sn, cs, kt2,
                t_rcs, t_za, t_acc)
    QK = reg(2048, 2, 8, 96)
    KM = reg(8192, 2, 8, 96)
    VM = reg(9728, 2, 8, 64)
    QMT = reg(10752, 8, 256)
    t_qk, t_km, t_vm = [], [], []
    for i in range(2):
        for o, w, h0, hn in ((0, 480, 0, 5), (480, 288, 5, 3)):
            b, tok = project(("qup",), CT, i, w, ALL6, k8=2, o=o, after=[t_ct])
            v = PS[:, b, 0:w].rearrange("p (h d) -> p h d", d=96)
            ta = act.do(lambda e, v=v, i=i, h0=h0, hn=hn: e.activation(QK[:, i, h0:h0 + hn, 0:64], v[:, :, 0:64], ACT.Copy),
                        tok, t_HE, t_xf)
            tm = [rtmp[:, a, 0:hn, :] for a in range(2)]
            tr_ = rope(QK[:, i, h0:h0 + hn, 64:80], QK[:, i, h0:h0 + hn, 80:96], v[:, :, 64:80], v[:, :, 80:96],
                       bc(cs[:, i, :], [P, hn, 16], 1), bc(sn[:, i, :], [P, hn, 16], 1),
                       bc(sn[:, i, :], [P, hn, 16], 1), bc(cs[:, i, :], [P, hn, 16], 1), tm, ta, t_kp)
            free[b] = tr_
            t_qk += [ta] + tr_
            t_kp = tr_ + t_kp
    for i in range(2):
        for o in range(2):
            b, tok = project(("kvup",), CT[:, 2:3, :], i, 512, ALL6, k8=1, o=512 * o)
            v = PS[:, b, :].rearrange("p (h d) -> p h d", d=128)
            ta = act.do(lambda e, v=v, i=i, o=o: e.activation(KM[:, i, 4 * o:4 * o + 4, 0:64], v[:, :, 0:64], ACT.Copy),
                        tok, t_acc)
            tb = act.do(lambda e, v=v, i=i, o=o: e.activation(VM[:, i, 4 * o:4 * o + 4, :], v[:, :, 64:128], ACT.Copy))
            free[b] = [tb]
            t_km.append(ta)
            t_vm.append(tb)
        t_km.append(dve.do(lambda e, i=i: e.tensor_copy(KM[:, i, :, 64:96], bc(KP[:, i, :], [P, 8, 32], 1)),
                           t_kp, t_acc))
    def gate_steps(key, h, i, lst, after):
        held = []

        def step(n):
            if n == 0:
                b, fr = bank(ALL6)
                held.append(b)
                pe.wait(fr)
            b = held[0]
            w = weight(key)
            for k in (2 * n, 2 * n + 1):
                tok = pe.do(lambda e, k=k: e.matmul(PS[:, b, :], h_src[:, k, 128 * i:128 * i + 128], w[:, k, :],
                                                    start=(k == 0), stop=(k == 7)), mark=k % 2 == 1)
            t_used[key] = tok
            if n == 3:
                t = act.do(lambda e: e.activation(SG[:, i, 512 * h:512 * h + 512], PS[:, b, :], ACT.Silu), tok, after)
                free[b] = [t]
                lst[(h, i)] = t

        h_src = HE if key[0] == "e" else HO
        return [lambda n=n: step(n) for n in range(4)]

    t_sg = {}
    gates = [g for h, i in ((1, 0), (1, 1), (0, 1), (0, 0)) for g in gate_steps(("e", f"g{h}"), h, i, t_sg, t_xf)]
    gates.pop(0)()
    gates.pop(0)()
    KMT = reg(0, 8, 256)
    t_qmt, t_kmt = [], []
    for src, dst, lst, aft in ((QK, QMT, t_qmt, t_qk), (KM, KMT, t_kmt, t_km)):
        for hp in range(4):
            b, tok = transposes(ALL6, [src[:, i, 2 * hp + hh, :] for hh in range(2) for i in range(2)], aft, parts=96)
            t = evac(dst[0:96, 2 * hp:2 * hp + 2, :], PS[0:96, b, :].rearrange("p (h t) -> p h t", h=2), tok,
                     t_acc, t_qk, t_km, t_vm)
            free[b] = [t]
            lst.append(t)

    def masked(hs, nk, cols, bias, scale, mx, nm, sm, lower=None, shift=None, first=None):

        def soft(b, p, tok, before):
            for q, h in enumerate(hs):
                c = slice(q * nk, q * nk + nk)
                i_ = cols.start + q * cols.step
                t1 = dve.do(lambda e, c=c, h=h, i_=i_: e.tensor_tensor_reduce(
                    p[:, c], PS[:, b, c], bias(h), scale, -3.0e38, ALU.add, ALU.max, mx[:, i_:i_ + 1]),
                            tok, before, first)
            t_fr = t1
            if lower is not None:
                t1 = dve.do(lambda e: e.tensor_tensor(nm[:, cols], mx[:, cols], lower, ALU.max), t1)
                t1 = dve.do(lambda e: e.tensor_scalar(nm[:, cols], nm[:, cols], -1.0, None, ALU.mult), t1)
            elif shift is not None:
                t1 = dve.do(lambda e: e.tensor_tensor(nm[:, cols], mx[:, cols], shift, ALU.add), t1)
                t1 = dve.do(lambda e: e.scalar_tensor_tensor(out=nm[:, cols], in0=nm[:, cols], scalar=-1.0, in1=shift,
                                                             op0=ALU.mult, op1=ALU.add), t1)
            else:
                t1 = dve.do(lambda e: e.tensor_scalar(nm[:, cols], mx[:, cols], -1.0, None, ALU.mult), t1)
            for q, h in enumerate(hs):
                c = slice(q * nk, q * nk + nk)
                i_ = cols.start + q * cols.step
                t_e = act.do(lambda e, c=c, i_=i_: e.activation(p[:, c], p[:, c], ACT.Exp, bias=nm[:, i_:i_ + 1],
                                                                accum_out=sm[:, i_:i_ + 1]), t1)
            return t_e, t_fr

        return soft

    def outputs(dst, i, half, ob, c, sm, ri, gate, lst, add=None):

        def done(tok):
            t1 = None
            if add is not None:
                t1 = dve.do(lambda e: e.tensor_tensor(sm[:, c], sm[:, c], esk[:, c], ALU.add), add(), tok)
            t1 = dve.do(lambda e: e.reciprocal(ri[:, c], sm[:, c]), tok, t1)
            d = dst[:, i, 512 * half:512 * half + 512]
            t1 = dve.do(lambda e: e.tensor_tensor(d.rearrange("p (h d) -> p h d", h=8),
                                                  PS[:, ob, :].rearrange("p (h d) -> p h d", h=8),
                                                  bc(ri[:, c], [P, 8, 64], 2), ALU.mult), t1)
            free[ob] = [t1]
            lst.append(dve.do(lambda e: e.tensor_tensor(d, d, SG[:, i, 512 * half:512 * half + 512], ALU.mult), t1,
                              gate[(half, i)]))

        return done

    O2 = reg(6144, 2, D)
    mx2, nm2, sm2, ri2 = [col(16) for _ in range(4)]
    mx3, nm3, sm3, ri3 = mx1, nm1, sm1, ri1
    esk = col(16)
    t_o2 = []
    t_c2 = [t_qk, t_km]
    pairs = []
    n_o = 0
    for part, i in (("swa", 0), ("swa", 1), ("mla", 1), ("mla", 0)):
        nk = 128 * (i + 1)
        per = 512 // nk
        ob = OB[n_o % 2]
        n_o += 1
        for h0 in range(0, 8, 2 * per):
            two = []
            for odd in range(2):
                hs = list(range(h0 + odd, h0 + odd + 2 * per, 2))
                cols = slice(8 * i + hs[0], 8 * i + hs[-1] + 1, 2)
                hd = []
                for h in hs:
                    if part == "mla":
                        def score(b, c, i=i, h=h, nk=nk):
                            pe.wait(t_qmt, t_kmt)
                            return pe.do(lambda e: e.matmul(PS[:, b, c:c + nk], QMT[0:96, h, 128 * i:128 * i + 128],
                                                            KMT[0:96, h, 0:nk], start=True, stop=True))
                        vals = [VM[:, s_, h, :] for s_ in range(i + 1)]
                    else:
                        def score(b, c, i=i, h=h, nk=nk, r=64 * (h % 2)):
                            pe.wait(t_qst, t_kst)
                            return pe.do(lambda e: e.matmul(
                                PS[:, b, c:c + nk], QST[r:r + 64, h // 2, 128 * i:128 * i + 128],
                                KST[r:r + 64, h // 4, 0:nk], start=True, stop=True))
                        vals = [VS[:, s_, 64 * (h // 4):64 * (h // 4) + 64] for s_ in range(i + 1)]
                    hd.append((score, vals, PS[:, ob, 64 * h:64 * h + 64]))
                if part == "mla":
                    soft = masked(hs, nk, cols, lambda h, nk=nk: cmask[:, 256 - nk:256], 96.0 ** -0.5, mx2, nm2, sm2,
                                  first=t_c2)
                else:
                    soft = masked(hs, nk, cols, lambda h, nk=nk: BIA[:, h, 256 - nk:256], 0.125, mx3, nm3, sm3,
                                  lower=sinkb[:, hs[0]:hs[-1] + 1:2], first=[t_bia, t_sk])
                ld = dict(nk=nk, heads=hd, soft=soft, wait=[t_vm, t_vs])
                if h0 == 0 and odd == 0:
                    ld["wait"] = [t_vm, t_vs, lambda ob=ob: free[ob]]
                if hs[-1] == 7:
                    c8 = slice(8 * i, 8 * i + 8)
                    if part == "mla":
                        ld["done"] = outputs(O2, i, 0, ob, c8, sm2, ri2, t_sg, t_o2)
                    else:
                        def sinks(c=c8):
                            t = dve.do(lambda e: e.tensor_tensor(esk[:, c], sinkb[:], nm3[:, c], ALU.add))
                            return act.do(lambda e: e.activation(esk[:, c], esk[:, c], ACT.Exp), t)
                        ld["done"] = outputs(O2, i, 1, ob, c8, sm3, ri3, t_sg, t_o2, add=sinks)
                two.append(ld)
            pairs.append(two)
    attention(pairs, [reg(o, 512) for o in (2048, 2560, 3072, 9216)], [reg(8192, 512), reg(8704, 512)],
              [t_qmt, t_kmt], gates)

    OT, t_OT = back(10752, O2, t_o2)

    def residual(name, src_t, after):
        toks = []
        for h in range(2):
            for i in range(2):
                b, tok = project((name, h), src_t, i, 512, ALL6, after=[after])
                c = slice(512 * h, 512 * h + 512)
                t1 = dve.do(lambda e, b=b, i=i, c=c: e.tensor_tensor(X[:, i, c], PS[:, b, :], X[:, i, c], ALU.add), tok)
                free[b] = [t1]
                toks.append(t1)
        return toks

    t_x3 = residual("out2", OT, t_OT)
    t_ot_used = t_used[("out2", 1)]

    XN4 = reg(8192, 2, D)
    t_n = normalise(XN4, X, t_x3, 12800, [t_o2])
    HO = reg(0, 8, 256)
    t_HO = turned(HO, XN4, c_go, None, t_n + [t_x3[-1]])
    fl = col(32).rearrange("p (t h) -> p t h", t=2)
    F1 = reg(14336, 2, 16)
    F2 = reg(14368, 2, 16)
    F3 = reg(14400, 2, 16)
    F4 = reg(14432, 2, 16)
    F5 = reg(14464, 2, 16)
    b, fr = bank(ALL6)
    pe.wait(fr, t_HO, t_wf)
    for i in range(2):
        for k in range(8):
            tok = pe.do(lambda e, b=b, i=i, k=k: e.matmul(PS[:, b, 16 * i:16 * i + 16], HO[:, k, 128 * i:128 * i + 128],
                                                          wf[:, k, :], start=(k == 0), stop=(k == 7)),
                        mark=(i == 1 and k == 7))
    t1 = dve.do(lambda e, b=b: e.tensor_tensor(F1, PS[:, b, 0:32].rearrange("p (t h) -> p t h", t=2),
                                          bc(bfb[:], [P, 2, 16], 1), ALU.add), tok, t_bf, t_x3, t_bia)
    free[b] = [t1]
    t1 = dve.do(lambda e: e.tensor_scalar(F2, F1, -1.0, None, ALU.mult), t1)
    t1 = dve.do(lambda e: e.tensor_tensor(F2, F1, F2, ALU.min), t1)
    t1 = act.do(lambda e: e.activation(F2, F2, ACT.Exp), t1)
    t_u1 = dve.do(lambda e: e.tensor_scalar(F3, F2, 1.0, None, ALU.add), t1)
    t_ln = act.do(lambda e: e.activation(F4, F3, ACT.Ln), t_u1)
    t1 = dve.do(lambda e: e.tensor_scalar(F3, F3, -1.0, None, ALU.add), t_ln)
    t1 = dve.do(lambda e: e.tensor_scalar(F5, F3, 0.0, None, ALU.is_equal), t1)
    t1 = dve.do(lambda e: e.tensor_tensor(F3, F3, F5, ALU.add), t1)
    t1 = dve.do(lambda e: e.tensor_tensor(F4, F4, F5, ALU.add), t1)
    t1 = dve.do(lambda e: e.reciprocal(F3, F3), t1)
    t1 = dve.do(lambda e: e.tensor_tensor(F4, F4, F3, ALU.mult), t1)
    t1 = dve.do(lambda e: e.tensor_tensor(F4, F4, F2, ALU.mult), t1)
    t1 = dve.do(lambda e: e.tensor_scalar(F1, F1, 0.0, None, ALU.min), t1)
    t_lf = dve.do(lambda e: e.tensor_tensor(F1, F1, F4, ALU.subtract), t1)

    def straight(names, dst, after):
        toks = []
        for hf, nm in enumerate(names):
            w = weight(("o", nm))
            for n2 in range(2):
                b, fr = bank(ALL6)
                pe.wait(fr)
                for nn in range(2):
                    n = 2 * n2 + nn
                    for k in range(8):
                        tok = pe.do(lambda e, b=b, n=n, nn=nn, k=k, w=w: e.matmul(
                            PS[:, b, 256 * nn:256 * nn + 256], w[:, k, 128 * n:128 * n + 128], HO[:, k, :],
                            start=(k == 0), stop=(k == 7)), mark=(nn == 1 and k == 7))
                t = evac(dst[:, 4 * hf + 2 * n2:4 * hf + 2 * n2 + 2, :],
                         PS[:, b, :].rearrange("p (n t) -> p n t", n=2), tok, after)
                free[b] = [t]
                toks.append(t)
            t_used[("o", nm)] = tok
        return toks

    QF = reg(2048, 8, 256)
    t_qf = straight(("q0", "q1"), QF, t_x3)
    b, fr = bank(ALL6)
    pe.wait(fr, t_lf)
    pe.do(lambda e, b=b: e.matmul(PS[:, b, 0:16], tri, F1[:, 0, :], start=True, stop=True), mark=False)
    pe.do(lambda e, b=b: e.matmul(PS[:, b, 16:32], tri, F1[:, 1, :], start=True, stop=False), mark=False)
    tok = pe.do(lambda e, b=b: e.matmul(PS[:, b, 16:32], ones, F1[:, 0, :], start=False, stop=True))
    t_cs = dve.do(lambda e, b=b: e.tensor_copy(fl, PS[:, b, 0:32].rearrange("p (t h) -> p t h", t=2)), tok)
    free[b] = [t_cs]
    b, fr = bank(ALL6)
    pe.wait(fr, t_cs)
    for i in range(2):
        tok = pe.do(lambda e, i=i, b=b: e.transpose(PS[0:16, b, 128 * i:128 * i + 128], fl[:, i, :], ident), mark=i == 1)
    NC_ = reg(14592, 256)
    t_nc = []
    for r in (0, 64):
        t_nc.append(dve.do(lambda e, b=b, r=r: e.tensor_scalar(NC_[r:r + 16], PS[0:16, b, 0:256], -8.0, None, ALU.mult),
                           tok, t_bia, t_o2))
    free[b] = [t_nc[-1]]
    KF = reg(4096, 8, 256)
    t_kf = straight(("k0", "k1"), KF, t_x3)
    VF = reg(6144, 2, D)
    t_vf = []
    for h in range(2):
        for i in range(2):
            b, tok = project(("o", f"v{h}"), HO, i, 512, ALL6)
            t_vf.append(evac(VF[:, i, 512 * h:512 * h + 512], PS[:, b, :], tok, t_x3, t_OT))
            free[b] = [t_vf[-1]]
    O3 = reg(10752, 2, D)
    t_sg2 = {}
    gates = [g for h in range(2) for i in range(2) for g in gate_steps(("o", f"g{h}"), h, i, t_sg2, t_o2)]
    gates.pop(0)()
    gates.pop(0)()
    mx4, nm4, sm4, ri4 = [reg(15360 + 32 * i, 32) for i in range(4)]
    t_o3 = []
    pairs = []
    n_o = 0
    for half, i in ((0, 0), (0, 1), (1, 0), (1, 1)):
        nk = 128 * (i + 1)
        per = 512 // nk
        ob = OB[n_o % 2]
        n_o += 1
        for h0 in range(8 * half, 8 * half + 8, 2 * per):
            two = []
            for odd in range(2):
                hs = list(range(h0 + odd, h0 + odd + 2 * per, 2))
                cols = slice(16 * i + hs[0], 16 * i + hs[-1] + 1, 2)
                hd = []
                for h in hs:
                    def score(b, c, i=i, h=h, nk=nk, r=64 * (h % 2)):
                        pe.wait(t_qf, t_kf, t_nc)
                        pe.do(lambda e: e.matmul(PS[:, b, c:c + nk], QF[r:r + 64, h // 2, 128 * i:128 * i + 128],
                                                 KF[r:r + 64, h // 2, 0:nk], start=True, stop=False), mark=False)
                        return pe.do(lambda e: e.matmul(PS[:, b, c:c + nk],
                                                        ident[r:r + 16, r + h:r + h + 1].to_broadcast([16, 128]),
                                                        NC_[r:r + 16, 0:nk], start=False, stop=True))
                    hd.append((score, [VF[:, s_, 64 * h:64 * h + 64] for s_ in range(i + 1)],
                               PS[:, ob, 64 * (h % 8):64 * (h % 8) + 64]))
                soft = masked(hs, nk, cols, lambda h, nk=nk: cmask[:, 256 - nk:256], 0.125, mx4, nm4, sm4,
                              shift=fl[:, i, hs[0]:hs[-1] + 1:2], first=[t_x3, t_HO, t_bia])
                ld = dict(nk=nk, heads=hd, soft=soft, wait=[t_vf])
                if h0 % 8 == 0 and odd == 0:
                    ld["wait"] = [t_vf, lambda ob=ob: free[ob]]
                if hs[-1] % 8 == 7:
                    ld["done"] = outputs(O3, i, half, ob, slice(16 * i + 8 * half, 16 * i + 8 * half + 8), sm4, ri4,
                                         t_sg2, t_o3)
                two.append(ld)
            pairs.append(two)
    attention(pairs, [reg(8192 + 512 * n, 512) for n in range(4)], [reg(12800, 512), reg(13312, 512)],
              [t_HO], gates)
    g2b = reg(4096, D)
    t_gf2 = load(pool, g2b, A["g_final_2"].partition_broadcast(P), t_o3)
    OT3, t_OT3 = back(2048, O3, t_o3)
    t_x4 = residual("out3", OT3, t_OT3)
    ssf, tok = quarter_squares(X, t_x4, 8192, [t_o3])
    rsf = col(2)
    t1 = quarter_rstd(rsf, ssf, tok)
    s_out = sem("s_out")
    for i in range(2):
        t = dve.do(lambda e, i=i: e.scalar_tensor_tensor(out=X[:, i, :], in0=X[:, i, :], scalar=rsf[:, i:i + 1],
                                                         in1=g2b, op0=ALU.mult, op1=ALU.mult), t1, t_gf2)
        act.dma(s_out, 0, lambda e, i=i: e.dma_start(out.rearrange("(t p) d -> p t d", p=P)[:, i, :], X[:, i, :]), t)
    act.wait((s_out, 32))

    ring_loads()

    block = ctx.enter_context(nc.Block())

    @block.sync
    def _(eng):
        sp.emit(eng)

    @block.tensor
    def _(eng):
        pe.emit(eng)

    @block.vector
    def _(eng):
        dve.emit(eng)

    @block.scalar
    def _(eng):
        act.emit(eng)

    @block.gpsimd
    def _(eng):
        pool.emit(eng)


DROP = {"c": 1, "b_mod": 1, "g_mix": 1, "g_ffn": 1, "w_mod": 1, "w_in": 1, "q_gain": 1, "k_gain": 1, "v_gain": 1,
        "w_s": 1, "b_s": 1, "w_out": 1, "w_router": 1, "w1": 1, "w3": 1, "w2": 1, "x": 1, "ctx": 1, "positions_2": 1,
        "e_g_in_2": 1, "e_w_in_2": 1, "e_g_q_a_2": 1, "e_w_q_up_2": 1, "e_g_kv_a_2": 1, "e_w_kv_up_2": 1,
        "e_sinks_2": 1, "e_w_out_2": 1, "o_g_in_2": 1, "o_w_in_2": 1, "o_b_f_2": 1, "o_w_out_2": 1}


def kernel(**inputs):
    import concourse.bacc as bacc
    from concourse.bass_utils import run_bass_kernel_spmd as run

    nc = bacc.Bacc("TRN2", target_bir_lowering=False, num_devices=1)
    arrays, aps = {}, {}
    for name in INS:
        a = np.ascontiguousarray(inputs[name])
        arrays["in_" + name] = a
        ap = nc.dram_tensor("in_" + name, a.shape, mybir.dt.from_np(a.dtype), kind="ExternalInput").ap()
        aps[name] = ap[0] if name in DROP else ap
    k = constants()
    arrays["in_consts"] = k
    kin = nc.dram_tensor("in_consts", k.shape, F32, kind="ExternalInput").ap()
    o = nc.dram_tensor("out_0", (1, T, D), F32, kind="ExternalOutput").ap()
    program(nc, aps, kin, o[0])
    r = run(nc, [arrays], core_ids=[0])
    return r.results[0]["out_0"]
```

```python
from contextlib import ExitStack

import numpy as np

import concourse.bass as bass
from concourse import mybir

F32 = mybir.dt.float32
I32 = mybir.dt.int32
F32R = mybir.dt.float32r
ACT = mybir.ActivationFunctionType
ALU = mybir.AluOpType
AX = mybir.AxisListType

P = 128
D = 1024
T = 256
E = 16
SLOT = 4096
NSLOT = 7
EPS = 1e-6
NEG = -1.0e30

INS = ["x", "c", "ctx", "c_ctx", "w_mod", "b_mod", "g_mix", "g_ffn", "w_in", "q_gain", "k_gain", "v_gain",
       "w_s", "b_s", "w_out", "w_router", "w1", "w3", "w2", "g_final", "positions_2", "e_g_in_2", "e_w_in_2",
       "e_g_q_a_2", "e_w_q_up_2", "e_g_kv_a_2", "e_w_kv_up_2", "e_sinks_2", "e_w_out_2", "o_g_in_2",
       "o_w_in_2", "o_b_f_2", "o_w_out_2", "g_final_2"]

K_ID, K_TRI, K_CM, K_DIST, K_ONE, K_COS, K_SIN, K_IOTA, K_SLOT, K_INV, K_HALF, K_Q, K_END = np.cumsum(
    [0, 128, 128, 256, 256, 128, 64, 64, 32, 1, 16, 16, 16]).tolist()


def constants():
    k = np.zeros((P, K_END), np.float32)
    r = np.arange(P)
    k[:, K_ID:K_ID + 128] = np.eye(P)
    k[:, K_TRI:K_TRI + 128] = r[:, None] <= r[None, :]
    k[:, K_CM + 128:K_CM + 256] = np.where(r[None, :] <= r[:, None], 0.0, NEG)
    dist = 128 + r[:, None] - np.arange(256)[None, :]
    k[:, K_DIST:K_DIST + 256] = np.where((dist >= 0) & (dist < 128), dist, -NEG)
    k[:, K_ONE:K_ONE + 128] = 1.0
    f = np.float32
    inv = (f(10000.0) ** (-np.arange(16, dtype=f) / f(16))).astype(f)
    tok = np.arange(T)
    ang = np.concatenate([(tok // 64).astype(f)[:, None] * inv, (tok % 64).astype(f)[:, None] * inv], axis=1)
    k[:, K_COS:K_COS + 64] = np.cos(ang).astype(f).reshape(2, P, 32).transpose(1, 0, 2).reshape(P, 64)
    k[:, K_SIN:K_SIN + 64] = np.sin(ang).astype(f).reshape(2, P, 32).transpose(1, 0, 2).reshape(P, 64)
    k[:, K_IOTA:K_IOTA + 32] = np.arange(32)[None, :]
    k[:, K_SLOT] = r % 32
    k[:, K_INV:K_INV + 16] = (f(1.0) / (f(10000.0) ** (np.arange(0, 32, 2, dtype=f) / f(32)))).astype(f)[None, :]
    k[:, K_HALF:K_HALF + 16] = -0.5
    k[:, K_Q:K_Q + 16] = r[:, None] % 32 == np.arange(16)[None, :]
    return k


class Queue:

    def __init__(self, name, sem):
        self.name, self.sem, self.ops, self.count, self.seen = name, sem, [], 0, {}

    def wait(self, *tokens):
        for t in tokens:
            if t is None:
                continue
            if isinstance(t, list):
                self.wait(*t)
                continue
            sem, value = t
            if self.seen.get(id(sem), 0) < value:
                self.seen[id(sem)] = value
                self.ops.append(lambda e, s=sem, v=value: e.wait_ge(s, v))

    def do(self, fn, *after, mark=True):
        self.wait(*after)
        if mark:
            self.count += 1
            self.ops.append(lambda e: fn(e).then_inc(self.sem, 1))
            return (self.sem, self.count)
        self.ops.append(fn)

    def dma(self, sem, level, fn, *after):
        self.wait(*after)
        self.ops.append(lambda e: fn(e).then_inc(sem, 16))
        return (sem, level)

    def emit(self, eng):
        for op in self.ops:
            op(eng)


def program(nc, ins, kin, out):
    with ExitStack() as ctx:
        body(ctx, nc, ins, kin, out)


def body(ctx, nc, A, kin, out):
    nsem = [0]

    def sem(name):
        nsem[0] += 1
        return ctx.enter_context(nc.semaphore(name))

    pe = Queue("pe", sem("s_pe"))
    dve = Queue("dve", sem("s_dve"))
    act = Queue("act", sem("s_act"))
    pool = Queue("pool", sem("s_pool"))
    sp = Queue("sp", sem("s_sp"))

    ring = ctx.enter_context(nc.sbuf_tensor("ring", [P, NSLOT, SLOT], F32))
    RR = [nc.alloc_sbuf_tensor_at(f"RR{i}", [P, SLOT], F32R, offset=nc.sbuf_base - 4 * (NSLOT - i) * SLOT)
          for i in range(NSLOT)]
    PS = ctx.enter_context(nc.psum_tensor("PS", [P, 8, 512], F32))

    def sb(name, *shape, dt=F32):
        return ctx.enter_context(nc.sbuf_tensor(name, [P, *shape], dt))

    KC = sb("KC", K_END)
    ident = KC[:, K_ID:K_ID + 128]
    tri = KC[:, K_TRI:K_TRI + 128]
    cmask = KC[:, K_CM:K_CM + 256]
    dist = KC[:, K_DIST:K_DIST + 256]
    ones = KC[:, K_ONE:K_ONE + 128]
    iota = KC[:, K_IOTA:K_IOTA + 32]
    slotc = KC[:, K_SLOT:K_SLOT + 1]
    invf = KC[:, K_INV:K_INV + 16]
    quarters = KC[:, K_Q:K_Q + 16]

    X = sb("X", 2, D)
    qgb = sb("qgb", 64)
    kgb = sb("kgb", 64)
    SG = sb("SG", 2, D)
    vgb = SG[:, 0, 0:512]
    sinkb = sb("sinkb", 8)
    bfb = sb("bfb", 16)
    gfb = SG[:, 0, :]
    gtb = SG[:, 1, :]

    RT = sb("RT", 59)
    bm = sb("bm", 3, 512)
    mrow = bm
    mcol = sb("mcol", 3, 4, 4, 2)
    ab = sb("ab", 6, 8)
    cvec = sb("cvec", 8, 32)
    wr = sb("wr", 8, E)
    wf = sb("wf", 8, 16)
    rcs = sb("rcs", 2, 2, 16)
    st = sb("st", 470)
    SC = 16384
    S = sb("S", SC)
    SR = nc.alloc_sbuf_tensor_at("SR", [P, SC], F32R, offset=nc.sbuf_base - 4 * SC)

    def regr(off, *shape):
        return reg(off, *shape, of=SR)

    def reg(off, *shape, of=S):
        n = int(np.prod(shape))
        assert off + n <= SC, (off, n)
        v = of[:, off:off + n]
        if len(shape) > 1:
            names = "abcd"[:len(shape)]
            v = v.rearrange("p (" + " ".join(names) + ") -> p " + " ".join(names),
                            **{k: s for k, s in zip(names, shape)})
        return v

    R = reg(12288, 128)
    stn = [0]

    def col(n=1):
        stn[0] += n
        assert stn[0] <= 470
        return st[:, stn[0] - n:stn[0]]

    def bc(ap, shape, *axes):
        for a in axes:
            ap = ap.unsqueeze(a)
        return ap.to_broadcast(shape)

    free = {b: [] for b in range(8)}
    turn = {}

    def bank(group):
        i = turn.get(group, 0)
        while free[group[i % len(group)]] is None and i < turn.get(group, 0) + len(group):
            i += 1
        turn[group] = i + 1
        b = group[i % len(group)]
        assert free[b] is not None, f"bank {b} still held"
        t, free[b] = free[b], None
        return b, t

    ALL6 = (0, 1, 2, 3, 4, 5)
    OB = (6, 7)
    B4 = (0, 1, 2, 3)

    def load(q, dst, src, *after):
        s = sem(f"s_l{nsem[0]}")
        return q.dma(s, 16, lambda e: e.dma_start(dst, src), *after)

    t_x0 = load(act, X[:], A["x"].rearrange("(t p) d -> p t d", p=P))
    t_k = load(sp, KC[:], kin)
    t_r = [load(sp, R[8 * i:8 * i + 8, :], A[n].rearrange("(j p) -> j p", p=P))
           for i, n in enumerate(["c", "c_ctx", "g_mix", "g_ffn", "e_g_in_2", "o_g_in_2"])]
    t_r.append(load(sp, R[48:56, :], A["b_s"]))
    t_r.append(load(sp, R[56:58, :], A["e_g_q_a_2"].rearrange("(j p) -> j p", p=P)))
    t_r.append(load(sp, R[58:59, :], A["e_g_kv_a_2"].rearrange("(j p) -> j p", p=P)))

    ring_sem = [sem(f"s_w{i}") for i in range(NSLOT)]
    n_load = [0] * NSLOT
    owner = [None] * NSLOT
    t_used = {}
    place, pending, second, ready = {}, [], {}, {}
    keys, behind = [], {}

    def view(t, off, k, w):
        return t[:, off:off + k * w].rearrange("p (k w) -> p k w", k=k)

    def unit(key, src, k, w, slot, hslot=None, off=0, hoff=0, share=None):
        if share is None:
            before = owner[slot]
            n_load[slot] += 1
            s, level = ring_sem[slot], 16 * n_load[slot]
        else:
            before = second_before[share][0]
            s, level = sem(f"s_u{len(pending)}"), 16
        hbefore = None
        if hslot is not None:
            hbefore = second_before[share][1] if share is not None else owner[hslot]
            second[key] = (view(RR[hslot], hoff, k, w), view(RR[slot], off, k, w))
            second_before[key] = (before, hbefore)
            owner[hslot] = key
        owner[slot] = key
        place[key] = (view(ring[:, slot, :], off, k, w), (s, level))
        pending.append((place[key][0], src, s, before))
        keys.append(key)

    second_before = {}

    def weight(key):
        dst, tok = place[key]
        pe.wait(tok)
        return dst

    def split_steps(key, eng):
        dst, tok = place[key]
        hi, lo = second[key]
        k = hi.shape[1]
        step = max(1, k // 4)
        hb = second_before[key][1]
        ready[key] = [None] * k

        def piece(c):
            t1 = act.do(lambda e: e.activation(hi[:, c:c + step, :], dst[:, c:c + step, :], ACT.Copy),
                        tok, t_used[hb] if hb is not None and hb != key else None)
            t2 = eng.do(lambda e: e.tensor_tensor(lo[:, c:c + step, :], dst[:, c:c + step, :],
                                                  hi[:, c:c + step, :].bitcast(F32), ALU.subtract), t1)
            for n in range(c, c + step):
                ready[key][n] = t2

        return [lambda c=c: piece(c) for c in range(0, k, step)]

    def split(key, eng):
        for piece in split_steps(key, eng):
            piece()

    def ahead(key, eng):
        n = order.index(key) + 2
        if n < len(order):
            split(order[n], eng)
            if order[n] == ("qup",):
                split(("kvup",), eng)

    def passes(key, h, kk, wc, hc, swap=False):
        wh, wl = [w[:, kk, wc] for w in second[key]]
        hh, hl = h[0][:, kk, hc], h[1][:, kk, hc]
        return [(wh, hh), (wl, hh), (wh, hl)] if swap else [(hh, wh), (hh, wl), (hl, wh)]

    def kview(ap):
        return ap.rearrange("(k p) n -> p k n", p=P)

    wm = kview(A["w_mod"])

    def mod_unit(G, k, slot):
        unit(("mod", G, k), wm[:, 2 * k:2 * k + 2, 2048 * G:2048 * G + 2048], 2, 2048, slot)

    wi = kview(A["w_in"])
    for k in range(4):
        mod_unit(0, k, k)
    for n, o, w, slot, hslot, hoff in [("kv", 512, 256, 4, 4, 2048), ("q", 0, 512, 5, 6, 0), ("vv", 1280, 512, 0, 1, 0),
                                       ("u", 768, 512, 2, 3, 0)]:
        unit(("in", n), wi[:, :, o:o + w], 8, w, slot, hslot, hoff=hoff)
    for n, slot in enumerate((4, 5, 6, 0, 1, 2, 3, 4)):
        mod_unit(1 + n // 4, n % 4, slot)
    for h in range(2):
        unit(("out1", h), kview(A["w_out"])[:, :, 512 * h:512 * h + 512], 8, 512, 2 * h, 2 * h + 1)
    n_u = 4
    for e in range(E):
        for n in ("w1", "w3"):
            for k in range(4):
                unit((n, e, k), kview(A[n][e])[:, 2 * k:2 * k + 2, :], 2, 2048, n_u % NSLOT)
                n_u += 1
        for j in range(4):
            unit(("w2", e, j), kview(A["w2"][e])[:, 4 * j:4 * j + 4, :], 4, 1024, n_u % NSLOT)
            n_u += 1
    EXTRA = RR[6]
    we = kview(A["e_w_in_2"])
    wo = kview(A["o_w_in_2"])
    later = [(("e", "a"), we[:, :, 0:416], 416), (("e", "qs"), we[:, :, 416:928], 512),
             (("e", "kvs"), we[:, :, 928:1184], 256), (("qup",), kview(A["e_w_q_up_2"]), 768),
             (("e", "g1"), we[:, :, 1696:2208], 512), (("e", "g0"), we[:, :, 1184:1696], 512)]
    later += [(("out2", h), kview(A["e_w_out_2"])[:, :, 512 * h:512 * h + 512], 512) for h in range(2)]
    later += [(("o", n), wo[:, :, o:o + 512], 512) for n, o in
              [("q0", 0), ("q1", 512), ("k0", 1024), ("k1", 1536), ("v0", 2048), ("v1", 2560), ("g0", 3088),
               ("g1", 3600)]]
    later += [(("out3", h), kview(A["o_w_out_2"])[:, :, 512 * h:512 * h + 512], 512) for h in range(2)]
    for n, (key, src, w) in enumerate(later):
        unit(key, src, 2 if key == ("qup",) else 8, w, 2 * (n % 3), 2 * (n % 3) + 1)
        if key == ("qup",):
            unit(("kvup",), kview(A["e_w_kv_up_2"]), 1, 1024, 2 * (n % 3), 2 * (n % 3) + 1, off=1536, hoff=1536,
                 share=key)
    order = [key for key, _, _ in later]

    def ring_loads():
        for n, (dst, src, s, before) in enumerate(pending):
            sp.wait(t_used[before] if before is not None else None)
            sp.dma(s, 0, lambda e, dst=dst, src=src: e.dma_start(dst, src))
            for dst2, src2, s2, after in behind.get(keys[n], []):
                sp.dma(s2, 0, lambda e, dst2=dst2, src2=src2: e.dma_start(dst2, src2), *after)

    def load_after(key, dst, src, *after):
        s = sem(f"s_l{nsem[0]}")
        behind.setdefault(key, []).append((dst, src, s, after))
        return (s, 16)

    XC = reg(6144, 2, D)
    t_x = t_x0
    t_c = load(act, XC, A["ctx"].rearrange("(t p) d -> p t d", p=P))
    t_bm0 = dve.do(lambda e: e.memset(bm[:], 0.0))
    t_bm = []
    for r in range(2):
        for j in range(4):
            t_bm.append(load_after(("mod", 0, 3), bm[32 * j + r:32 * j + r + 1, :, :],
                                   A["b_mod"].rearrange("(g j n) -> j g n", j=4, n=512)[j:j + 1], t_bm0))
    t_qg = load_after(("in", "q"), qgb[:], A["q_gain"].partition_broadcast(P))
    t_kg = load_after(("in", "q"), kgb[:], A["k_gain"].partition_broadcast(P))
    t_vg = load_after(("in", "vv"), vgb, A["v_gain"].partition_broadcast(P))
    WS = reg(14336, 8, 128)
    t_ws = load_after(("in", "vv"), WS, A["w_s"].rearrange("g i j -> i g j"))
    t_wr = load_after(("in", "u"), wr[:], kview(A["w_router"]))
    t_sk = load_after(("in", "u"), sinkb[:], A["e_sinks_2"].partition_broadcast(P))
    t_bf = load_after(("in", "u"), bfb[:], A["o_b_f_2"].partition_broadcast(P))
    t_wf = load_after(("in", "u"), wf[:], kview(A["o_w_in_2"])[:, :, 3072:3088])

    def rstd(outc, ssq, *after):
        n = ssq.shape[-1]
        t = pool.do(lambda e: e.tensor_scalar(outc, ssq, EPS, None, ALU.add), *after)
        return pool.do(lambda e: e.tensor_tensor(outc, outc, KC[:, K_HALF:K_HALF + n], ALU.pow), t)

    def square_sum(in_, outc, junk, width, *after):
        return act.do(lambda e: e.activation(junk, in_, ACT.Square, scale=float(width) ** -0.5, accum_out=outc),
                      *after)

    def transposes(group, pieces, after, parts=P):
        b, fr = bank(group)
        pe.wait(fr, after)
        for i, in_ in enumerate(pieces):
            tok = pe.do(lambda e, i=i, in_=in_, b=b: e.transpose(PS[0:parts, b, 128 * i:128 * i + 128], in_, ident),
                        mark=i == len(pieces) - 1)
        return b, tok

    ev = [0]

    def evac(dst, src, *after):
        ev[0] += 1
        if ev[0] % 2:
            return dve.do(lambda e: e.tensor_copy(dst, src), *after)
        return act.do(lambda e: e.activation(dst, src, ACT.Copy), *after)

    pe.wait(t_k)
    b, fr = bank(ALL6)
    tok = pe.do(lambda e: e.transpose(PS[:, 0, 0:59], R[0:59, :], ident[0:59, 0:59]), t_r)
    t_rt = dve.do(lambda e: e.tensor_copy(RT[:], PS[:, 0, 0:59]), tok)
    free[b] = [t_rt]
    t_cz = pool.do(lambda e: e.memset(cvec[:], 0.0))
    act.wait(t_rt, t_cz)
    t_cv = [act.do(lambda e, r=r: e.activation(cvec[:, :, r], RT[:, 8 * r:8 * r + 8], ACT.Silu)) for r in range(2)]

    c_gmix, c_gffn, c_ge, c_go = [RT[:, 8 * i:8 * i + 8] for i in (2, 3, 4, 5)]
    c_bs, c_qa, c_kva = RT[:, 48:56], RT[:, 56:58], RT[:, 58:59]

    t_mcol = {}
    t_mrow = {}

    def modulation_steps(G):
        held = []

        def step(k):
            if k == 0:
                b, fr = bank(ALL6)
                held.append(b)
                pe.wait(fr, t_cv)
            b = held[0]
            w = weight(("mod", G, k))
            for kk in range(2):
                for j in range(4):
                    tok = pe.do(lambda e, w=w, k=k, kk=kk, j=j, b=b: e.matmul(
                        PS[32 * j:32 * j + 32, b, :], cvec[:, 2 * k + kk, :], w[:, kk, 512 * j:512 * j + 512],
                        start=(k == 0 and kk == 0), stop=(k == 3 and kk == 1)), mark=(kk == 1 and j == 3))
            t_used[("mod", G, k)] = tok
            if k == 3:
                t = dve.do(lambda e: e.tensor_tensor(mrow[:, G, :], PS[:, b, :], bm[:, G, :], ALU.add), tok, t_bm, t_bm0)
                free[b] = [t]
                t_mrow[G] = t

        return [lambda k=k: step(k) for k in range(4)]

    def modulation(G):
        for step in modulation_steps(G):
            step()

    def modulation_cols(G):
        b, tok = transposes(ALL6, [mrow[:, G, 128 * s:128 * s + 128] for s in range(4)], t_mrow[G])
        t_mcol[G] = dve.do(lambda e: e.tensor_copy(
            mcol[:, G, :, :, :], PS[:, b, :].rearrange("p (s j r) -> p s j r", s=4, r=32)[:, :, :, 0:2]),
                           tok)
        free[b] = [t_mcol[G]]

    def mvec(G, unit0, r):
        return mcol[:, G, :, unit0:unit0 + 2, r].rearrange("p s j -> p j s")

    def ab8(i):
        return ab[:, i, :].rearrange("p (j s) -> p j s", j=2)

    XN = reg(4096, 2, D)
    junk = reg(12288, D)
    junk2 = reg(8192 + 2048, D)
    ss1 = col(4)
    rs1 = col(4)
    tok = t_cv[-1]
    tok2 = None
    for i in (0, 2):
        src, src2 = (X if i < 2 else XC)[:, 0, :], (X if i < 2 else XC)[:, 1, :]
        tok = square_sum(src, ss1[:, i:i + 1], junk, D, t_x if i < 2 else t_c, tok)
        tok2 = dve.do(lambda e, src2=src2, i=i: e.tensor_tensor_reduce(
            junk2, src2, src2, 1.0 / D, 0.0, ALU.mult, ALU.add, ss1[:, i + 1:i + 2]), t_x if i < 2 else t_c, tok2)
    t_rs1 = rstd(rs1, ss1, tok, tok2)
    t_xn = []
    for i in range(4):
        src = X[:, i, :] if i < 2 else XC[:, i - 2, :]
        dst = XN[:, i, :] if i < 2 else XC[:, i - 2, :]
        t_xn.append(dve.do(lambda e, src=src, dst=dst, i=i: e.tensor_scalar(dst, src, rs1[:, i:i + 1], None, ALU.mult),
                           t_rs1))
    steps0 = modulation_steps(0)
    steps0[0]()
    steps0[1]()
    RAW = reg(0, 2, 8, 256)
    HI, LO = regr(4096, 2, 8, 256), regr(0, 2, 8, 256)
    HL = (HI[:, 0], LO[:, 0])
    t_raw = []
    for k in range(8):
        b, tok = transposes(ALL6, [(XN if i < 2 else XC)[:, i % 2, 128 * k:128 * k + 128] for i in range(4)], t_xn)
        t_raw.append(evac(RAW[:, :, k, :], PS[:, b, :].rearrange("p (r t) -> p r t", r=2), tok))
        free[b] = [t_raw[-1]]
    kv_pieces = split_steps(("in", "kv"), pool)
    steps0[2]()
    steps0[3]()
    modulation_cols(0)
    t_ab = []
    for r in range(2):
        t_ab.append(dve.do(lambda e, r=r: e.scalar_tensor_tensor(
            out=ab8(2 * r), in0=mvec(0, 2, r), scalar=1.0, in1=c_gmix.rearrange("p (j s) -> p j s", j=2),
            op0=ALU.add, op1=ALU.mult), t_mcol[0]))
        t_ab.append(dve.do(lambda e, r=r: e.tensor_copy(ab8(2 * r + 1), mvec(0, 0, r))))
    t_hk = [[] for _ in range(8)]
    t_m = {}
    for k in range(9):
        if k % 2 == 0 and k < 8:
            kv_pieces[k // 2]()
        for r in range(2 if k < 8 else 0):
            v, a_, b_ = RAW[:, r, k, :], ab[:, 2 * r, k:k + 1], ab[:, 2 * r + 1, k:k + 1]
            if r == 0:
                t_m[k, r] = dve.do(lambda e, v=v, a_=a_, b_=b_: e.tensor_scalar(v, v, a_, b_, ALU.mult, ALU.add),
                                   t_raw, t_ab)
            else:
                t_m[k, r] = act.do(lambda e, v=v, a_=a_, b_=b_: e.activation(v, v, ACT.Identity, bias=b_, scale=a_),
                                   t_raw, t_ab)
        for r in range(2 if k else 0):
            v, hi_, lo_ = RAW[:, r, k - 1, :], HI[:, r, k - 1, :], LO[:, r, k - 1, :]
            if r == 0:
                t1 = dve.do(lambda e, v=v, hi_=hi_: e.tensor_copy(hi_, v), t_m[k - 1, r], t_raw)
            else:
                t1 = act.do(lambda e, v=v, hi_=hi_: e.activation(hi_, v, ACT.Copy), t_m[k - 1, r], t_raw)
            t_hk[k - 1].append(dve.do(lambda e, v=v, hi_=hi_, lo_=lo_: e.tensor_tensor(lo_, v, hi_.bitcast(F32),
                                                                                       ALU.subtract), t1))
    split(("in", "q"), dve)

    def project(key, h, tile, width, group, k8=8, o=0, after=()):
        b, fr = bank(group)
        pe.wait(fr, *after)
        for k in range(k8):
            pe.wait(ready[key][k])
            for n, (l_, r_) in enumerate(passes(key, h, k, slice(o, o + width), slice(128 * tile, 128 * tile + 128))):
                tok = pe.do(lambda e, l_=l_, r_=r_, st=(k == 0 and n == 0), sp_=(k == k8 - 1 and n == 2): e.matmul(
                    PS[:, b, 0:width], l_, r_, start=st, stop=sp_), mark=(k == k8 - 1 and n == 2))
        t_used[key] = tok
        return b, tok

    KV = reg(9216, 4, 256)
    KR = reg(10240, 4, 128)
    sqk = reg(10752, 4, 128)
    ssk, rsk = col(8), col(8)
    t_kvp = []
    kv_banks = [bank(ALL6) for i in range(4)]
    pe.wait([fr for _, fr in kv_banks])
    for k in range(8):
        pe.wait(t_hk[k], ready[("in", "kv")][k])
        for i in range(4):
            for n, (l_, r_) in enumerate(passes(("in", "kv"), (HI[:, i // 2], LO[:, i // 2]), k, slice(0, 256),
                                                slice(128 * (i % 2), 128 * (i % 2) + 128))):
                tok = pe.do(lambda e, l_=l_, r_=r_, b=kv_banks[i][0], st=(k == 0 and n == 0), sp_=(k == 7 and n == 2):
                            e.matmul(PS[:, b, 0:256], l_, r_, start=st, stop=sp_), mark=(k == 7 and n == 2))
        if k == 7:
            t_used[("in", "kv")] = tok
    for i in range(4):
        b = kv_banks[i][0]
        t1 = act.do(lambda e, b=b, i=i: e.activation(KV[:, i, :], PS[:, b, 0:256], ACT.Copy), tok)
        t_kvp.append(t1)
        free[b] = [t1]
    t_kvev = t_kvp[-1]
    tabq = reg(11264, 4, 2, 32)
    tabk = reg(11520, 4, 2, 32)
    cosT = KC[:, K_COS:K_COS + 64].rearrange("p (t f) -> p t f", t=2)
    sinT = KC[:, K_SIN:K_SIN + 64].rearrange("p (t f) -> p t f", t=2)
    t_tab = []
    for tab, g in ((tabq, qgb), (tabk, kgb)):
        for i, (tr, half) in enumerate(((cosT, 0), (sinT, 1), (sinT, 0), (cosT, 1))):
            t_tab.append(pool.do(lambda e, tab=tab, i=i, tr=tr, half=half, g=g: e.tensor_tensor(
                tab[:, i, :, :], tr, bc(g[:, 32 * half:32 * half + 32], [P, 2, 32], 1), ALU.mult), t_qg, t_kg, t_k))
    kh = KV[:, :, 0:128].rearrange("p t (g d) -> p t g d", g=2)
    t1 = dve.do(lambda e: e.tensor_tensor(sqk, KV[:, :, 0:128], KV[:, :, 0:128], ALU.mult), t_kvev)
    t1 = dve.do(lambda e: e.tensor_reduce(ssk, sqk.rearrange("p t (g d) -> p (t g) d", g=2), AX.X, ALU.add), t1)
    t1 = dve.do(lambda e: e.tensor_scalar(ssk, ssk, 1.0 / 64, None, ALU.mult), t1)
    t1 = rstd(rsk, ssk, t1)
    t_kn = dve.do(lambda e: e.tensor_tensor(kh, kh, bc(rsk.rearrange("p (t g) -> p t g", g=2), [P, 4, 2, 64], 3),
                                            ALU.mult), t1)
    rt = reg(11776, 2, 2, 2, 32)

    def rope(dst1, dst2, x1, x2, c1, s2, s1, c2, tmp, *after):
        ta = dve.do(lambda e: e.tensor_tensor(dst1, x1, c1, ALU.mult), *after)
        tb = dve.do(lambda e: e.tensor_tensor(tmp[0], x2, s2, ALU.mult))
        tc = dve.do(lambda e: e.tensor_tensor(dst2, x1, s1, ALU.mult))
        td = dve.do(lambda e: e.tensor_tensor(tmp[1], x2, c2, ALU.mult))
        te = dve.do(lambda e: e.tensor_tensor(dst1, dst1, tmp[0], ALU.subtract), tb)
        return [te, dve.do(lambda e: e.tensor_tensor(dst2, dst2, tmp[1], ALU.add), td)]

    krh = KR.rearrange("p t (g d) -> p t g d", g=2)

    def kt_(i):
        return bc(tabk[:, i, :, :], [P, 2, 2, 32], 2)

    t_kr = rope(krh[:, 0:2, :, 0:32], krh[:, 0:2, :, 32:64], kh[:, 0:2, :, 0:32], kh[:, 0:2, :, 32:64],
                kt_(0), kt_(1), kt_(2), kt_(3), (rt[:, 0], rt[:, 1]), t_kn, t_tab)
    t_kr.append(dve.do(lambda e: e.tensor_tensor(krh[:, 2:4, :, :], kh[:, 2:4, :, :],
                                                 bc(kgb[:], [P, 2, 2, 64], 1, 1), ALU.mult), t_kn))
    split(("in", "vv"), dve)
    QN = reg(6144, 2, 512)
    QR = reg(7168, 2, 512)
    sqq = reg(12288, 2, 512)
    ssq, rsq = col(16), col(16)
    t_qr = []
    for i in range(2):
        b, tok = project(("in", "q"), HL, i, 512, ALL6)
        qv = QN[:, i, :].rearrange("p (h d) -> p h d", h=8)
        t1 = act.do(lambda e, b=b, i=i: e.activation(sqq[:, i, :], PS[:, b, :], ACT.Square, scale=0.125), tok)
        t1 = dve.do(lambda e, i=i: e.tensor_reduce(ssq[:, 8 * i:8 * i + 8],
                                                   sqq[:, i, :].rearrange("p (h d) -> p h d", h=8), AX.X, ALU.add), t1)
        t1 = rstd(rsq[:, 8 * i:8 * i + 8], ssq[:, 8 * i:8 * i + 8], t1)
        t1 = dve.do(lambda e, b=b, i=i, qv=qv: e.tensor_tensor(
            qv, PS[:, b, :].rearrange("p (h d) -> p h d", h=8), bc(rsq[:, 8 * i:8 * i + 8], [P, 8, 64], 2), ALU.mult), t1)
        free[b] = [t1]
        src = QN[:, i, :].rearrange("p (g n d) -> p g n d", g=2, n=4)
        dst = QR[:, i, :].rearrange("p (n g d) -> p g n d", g=2, n=4)

        tmpv = S[:, 13312:13312 + 512].rearrange("p (a g n d) -> p a g n d", a=2, g=2, n=4)

        def qt_(n, i=i):
            return bc(tabq[:, n, i, :], [P, 2, 4, 32], 1, 1)

        t_qr += rope(dst[:, :, :, 0:32], dst[:, :, :, 32:64], src[:, :, :, 0:32], src[:, :, :, 32:64],
                     qt_(0), qt_(1), qt_(2), qt_(3), (tmpv[:, 0], tmpv[:, 1]), t1, t_tab, t_qr)
    VV = reg(2048, 2, 512)
    U = reg(3072, 2, 512)
    t_vv, t_u = [], []

    def gelu_part(n, dst, lst, i):
        b, tok = project(("in", n), HL, i, 512, ALL6)
        tok = act.do(lambda e, b=b, i=i, dst=dst: e.activation(dst[:, i, :], PS[:, b, :], ACT.Gelu), tok)
        free[b] = [tok]
        lst.append(tok)

    split(("in", "u"), pool)
    for i in range(2):
        gelu_part("vv", VV, t_vv, i)
    KT = reg(8192, 512)
    b, tok = transposes(ALL6, [KR[:, i, :] for i in range(4)], t_kr)
    t_KT = evac(KT, PS[:, b, :], tok)
    free[b] = [t_KT]

    QT = reg(12288, 2, 512)
    t_QT = []
    for i in range(2):
        b, tok = transposes(ALL6, [QR[:, i, 128 * n:128 * n + 128] for n in range(4)], t_qr)
        t = evac(QT[:, i, :], PS[:, b, :], tok)
        free[b] = [t]
        t_QT.append(t)

    ssv, rsv = col(2), col(2)
    jv = reg(10752, 512)
    tok = None
    for i in range(2):
        tok = act.do(lambda e, i=i: e.activation(jv, VV[:, i, :], ACT.Square, scale=512.0 ** -0.5,
                                                 accum_out=ssv[:, i:i + 1]), t_vv, t_kn, tok)
    t1 = rstd(rsv, ssv, tok)
    t_vn = []
    for i in range(2):
        t_vn.append(dve.do(lambda e, i=i: e.scalar_tensor_tensor(
            out=VV[:, i, :], in0=VV[:, i, :], scalar=rsv[:, i:i + 1], in1=vgb, op0=ALU.mult, op1=ALU.mult),
            t1, t_vg))

    def interleaved(a, b_):
        return [h for two in zip(a, b_) for h in two]

    def attention(pairs, pbuf, ptbuf, before, fillers=()):
        fillers = list(fillers)
        pfree = [[before] for _ in pbuf]
        ptfree = [[before] for _ in ptbuf]
        n_p = n_pt = 0
        live = []

        def fill():
            if fillers:
                fillers.pop(0)()

        for n in range(len(pairs) + 1):
            now = []
            if n < len(pairs):
                two = pairs[n]
                for ld in two:
                    b, fr = bank(ALL6)
                    pe.wait(fr)
                    now.append([ld, b, None])
                for hh in range(len(two[0]["heads"])):
                    for it in now:
                        it[2] = it[0]["heads"][hh][0](it[1], hh * it[0]["nk"])
                for it in now:
                    ld, b, tok = it
                    m = n_p % len(pbuf)
                    n_p += 1
                    t_e, t_fr = ld["soft"](b, pbuf[m], tok, pfree[m])
                    free[b] = [t_fr]
                    it[1:] = [m, t_e]
            fill()
            stage = []
            for ld, m, t_e in live:
                m2 = n_pt % len(ptbuf)
                n_pt += 1
                b, tok = transposes(ALL6, [pbuf[m][:, 128 * i:128 * i + 128] for i in range(4)], t_e)
                pfree[m] = [tok]
                t = evac(ptbuf[m2], PS[:, b, :], tok, ptfree[m2])
                free[b] = [t]
                stage.append((ld, m2, t))
            for it in now:
                if "scale" in it[0]:
                    it[2] = it[0]["scale"](pbuf[it[1]], it[2])
            fill()
            for group in ([stage] if stage and "flip" in stage[0][0] else [[one] for one in stage]):
                for ld, m2, t in group:
                    pe.wait(t, *[w() if callable(w) else w for w in ld["wait"]])
                nt = group[0][0]["nk"] // 128
                n_h = len(group[0][0]["heads"])
                for hh in range(n_h):
                    for i in range(nt):
                        c = 128 * (nt * hh + i)
                        last = hh == n_h - 1 and i == nt - 1
                        for ld, m2, t in group:
                            _, values, o = ld["heads"][hh]
                            l_, r_ = ptbuf[m2][:, c:c + 128], values[i]
                            if "flip" in ld:
                                l_, r_ = r_, l_
                            tok = pe.do(lambda e, o=o, l_=l_, r_=r_, i=i, nt=nt: e.matmul(
                                o, l_, r_, start=(i == 0), stop=(i == nt - 1)), mark=last)
                            if last:
                                ptfree[m2] = [tok]
                for ld, m2, t in group:
                    if "done" in ld:
                        ld["done"](tok)
            live = now
        while fillers:
            fill()

    MIX = reg(10240, 2, D)
    PB = [reg(6144 + 512 * i, 512) for i in range(4)]
    PT = [reg(13312, 512), reg(13824, 512), reg(8704, 512)]
    mx1, nm1, sm1, ri1 = col(16), col(16), col(16), col(16)
    t_mixa = []
    pairs = []
    for i in range(2):
        for n in range(4):
            two = []
            for g in range(2):
                idx = 8 * i + 4 * g + n

                def score(b, c, i=i, n=n, g=g):
                    pe.wait(t_QT, t_KT)
                    return pe.do(lambda e: e.matmul(PS[:, b, :], QT[64 * g:64 * g + 64, i, 128 * n:128 * n + 128],
                                                    KT[64 * g:64 * g + 64, :], start=True, stop=True))

                def soft(b, p, tok, before, c=slice(idx, idx + 1)):
                    t1 = dve.do(lambda e: e.tensor_reduce(mx1[:, c], PS[:, b, :], AX.X, ALU.max), tok)
                    t1 = dve.do(lambda e: e.tensor_scalar(nm1[:, c], mx1[:, c], -0.125, None, ALU.mult), t1)
                    t1 = act.do(lambda e: e.activation(p, PS[:, b, :], ACT.Exp, bias=nm1[:, c], scale=0.125,
                                                       accum_out=sm1[:, c]), t1, before)
                    return t1, t1

                ld = dict(nk=512, soft=soft, wait=[t_kvp] + ([free[OB[i]]] if n == 0 and g == 0 else []),
                          heads=[(score, [KV[:, s_, 128 + 64 * g:192 + 64 * g] for s_ in range(4)],
                                  PS[:, OB[i], 64 * (4 * g + n):64 * (4 * g + n) + 64])])
                if n == 3 and g == 1:
                    def done(tok, i=i):
                        t1 = dve.do(lambda e: e.reciprocal(ri1[:, 8 * i:8 * i + 8], sm1[:, 8 * i:8 * i + 8]), tok)
                        t1 = dve.do(lambda e: e.tensor_tensor(
                            MIX[:, i, 0:512].rearrange("p (h d) -> p h d", h=8),
                            PS[:, OB[i], :].rearrange("p (h d) -> p h d", h=8),
                            bc(ri1[:, 8 * i:8 * i + 8], [P, 8, 64], 2), ALU.mult), t1, t_vn)
                        free[OB[i]] = [t1]
                        t_mixa.append(t1)
                    ld["done"] = done
                two.append(ld)
            pairs.append(two)

    WST = reg(15360, 8, 128)
    t_wst = []

    def turn_ws(hlf):
        b, tok = transposes(ALL6, [WS[:, 4 * hlf + i, :] for i in range(4)], t_ws)
        t = evac(WST[:, 4 * hlf:4 * hlf + 4, :], PS[:, b, :].rearrange("p (g i) -> p g i", g=4), tok)
        free[b] = [t]
        t_wst.append(t)

    t_mixg = []

    def mixed(i):
        b, fr = bank(ALL6)
        pe.wait(fr, t_wst, t_vn)
        for g in range(8):
            tok = pe.do(lambda e, b=b, g=g, i=i: e.matmul(PS[:, b, 64 * g:64 * g + 64], WST[:, g, :],
                                                          VV[:, i, 64 * g:64 * g + 64], start=True, stop=True),
                        mark=g == 7)
        mg = MIX[:, i, 512:1024].rearrange("p (g d) -> p g d", g=8)
        t1 = dve.do(lambda e, b=b, mg=mg: e.tensor_tensor(mg, PS[:, b, :].rearrange("p (g d) -> p g d", g=8),
                                                          bc(c_bs, [P, 8, 64], 2), ALU.add), tok, t_vn, t_QT, t_KT)
        free[b] = [t1]
        t_mixg.append(dve.do(lambda e, i=i: e.tensor_tensor(MIX[:, i, 512:1024], MIX[:, i, 512:1024], U[:, i, :],
                                                            ALU.mult), t1, t_u))

    fillers = [lambda: gelu_part("u", U, t_u, 0), lambda: gelu_part("u", U, t_u, 1),
               lambda: turn_ws(0), lambda: turn_ws(1), lambda: mixed(0), lambda: mixed(1)]
    for G in (1, 2):
        fillers += modulation_steps(G)
    attention(pairs, PB, PT, [t_QT, t_KT, t_kr], fillers)
    split(("out1", 0), pool)
    split(("out1", 1), dve)
    t_gf = load(pool, gfb, A["g_final"].partition_broadcast(P), t_vn)

    modulation_cols(1)
    modulation_cols(2)
    t_ab2 = [dve.do(lambda e: e.scalar_tensor_tensor(
        out=ab8(4), in0=mvec(2, 0, 0), scalar=1.0, in1=c_gffn.rearrange("p (j s) -> p j s", j=2),
        op0=ALU.add, op1=ALU.mult), t_mcol[2]),
        dve.do(lambda e: e.tensor_copy(ab8(5), mvec(1, 2, 0)), t_mcol[1])]
    t_gt1 = []
    for j in range(2):
        b, fr = bank(ALL6)
        tok = pe.do(lambda e, b=b, j=j: e.matmul(PS[:, b, :], ident[:, 32 * j:32 * j + 1].to_broadcast([P, 128]),
                                                 mrow[:, 1, :], start=True, stop=True), fr, t_mrow[1])
        t_gt1.append(act.do(lambda e, b=b, j=j: e.activation(gtb[:, 512 * j:512 * j + 512], PS[:, b, :], ACT.Copy), tok))
        free[b] = [t_gt1[-1]]

    def back(hi, lo, src, after):
        toks = []
        for m in range(4):
            b, tok = transposes(ALL6, [src[:, i, 128 * (2 * m + kk):128 * (2 * m + kk) + 128]
                                       for kk in range(2) for i in range(2)], after)
            src_ = PS[:, b, :].rearrange("p (k t) -> p k t", k=2)
            h_, l_ = hi[:, 2 * m:2 * m + 2, :], lo[:, 2 * m:2 * m + 2, :]
            t = act.do(lambda e, h_=h_, src_=src_: e.activation(h_, src_, ACT.Copy), tok)
            t = dve.do(lambda e, h_=h_, l_=l_, src_=src_: e.tensor_tensor(l_, src_, h_.bitcast(F32), ALU.subtract), t)
            free[b] = [t]
            toks.append(t)
        return toks

    t_mix = t_mixa + t_mixg
    WRZ = reg(10752, 8, 32)
    MT = (regr(4096, 8, 256), regr(6144, 8, 256))
    t_MT = back(*MT, MIX, t_mix)
    t_wrz = pool.do(lambda e: e.memset(WRZ, 0.0), t_MT)
    t_wrz = pool.do(lambda e: e.tensor_copy(WRZ[:, :, 0:16], wr[:]), t_wrz, t_wr)
    G2 = reg(10240, 512)
    b, fr = bank(ALL6)
    pe.wait(fr, t_mrow[2])
    for j in range(2):
        tok = pe.do(lambda e, b=b, j=j: e.matmul(
            PS[64 * j:64 * j + 64, b, :], ident[:, 64 + 32 * j:65 + 32 * j].to_broadcast([P, 64]), mrow[:, 2, :],
            start=True, stop=True))
    t_g2 = act.do(lambda e, b=b: e.activation(G2, PS[:, b, :], ACT.Copy), tok, t_MT)
    free[b] = [t_g2]
    YT = reg(2048, 2, D)
    t_x1 = []
    for h in range(2):
        for i in range(2):
            b, tok = project(("out1", h), MT, i, 512, ALL6, after=[t_MT])
            c = slice(512 * h, 512 * h + 512)
            t1 = dve.do(lambda e, b=b, i=i, c=c: e.tensor_tensor(YT[:, i, c], PS[:, b, :], gtb[:, c], ALU.mult),
                        tok, t_gt1)
            free[b] = [t1]
            t_x1.append(dve.do(lambda e, i=i, c=c: e.tensor_tensor(X[:, i, c], X[:, i, c], YT[:, i, c], ALU.add), t1))
    t_mt_used = t_used[("out1", 1)]

    def quarter_squares(src, after, junk_off, jafter):
        ss_ = col(4)
        tok = None
        for h in range(2):
            for i in range(2):
                n = 2 * h + i
                tok = act.do(lambda e, h=h, i=i, n=n: e.activation(
                    reg(junk_off, 512), src[:, i, 512 * h:512 * h + 512], ACT.Square, scale=float(D) ** -0.5,
                    accum_out=ss_[:, n:n + 1]), after[n], jafter, tok)
        return ss_, tok

    def quarter_rstd(outc, ss_, tok):
        t1 = pool.do(lambda e: e.tensor_tensor(outc, ss_[:, 0:2], ss_[:, 2:4], ALU.add), tok)
        return rstd(outc, outc, t1)

    def normalise(dst, src, after, junk_off, jafter, dafter=None):
        ss_, tok = quarter_squares(src, after, junk_off, jafter)
        rs_ = col(2)
        t1 = quarter_rstd(rs_, ss_, tok)
        return [dve.do(lambda e: e.tensor_scalar(dst[:, 0, :], src[:, 0, :], rs_[:, 0:1], None, ALU.mult), t1, dafter),
                act.do(lambda e: e.activation(dst[:, 1, :], src[:, 1, :], ACT.Copy, scale=rs_[:, 1:2]), t1, dafter)]

    XN2 = reg(8192, 2, D)
    t_xn2 = normalise(XN2, X, t_x1, 13312, [t_mix])
    H2T = reg(4096, 8, 256)

    def turned(dst, src, a_col, b_col, after):
        toks = []
        for m in range(4):
            b, tok = transposes(ALL6, [src[:, i, 128 * (2 * m + kk):128 * (2 * m + kk) + 128]
                                       for kk in range(2) for i in range(2)], after)
            for kk in range(2):
                k = 2 * m + kk
                s_, d_ = PS[:, b, 256 * kk:256 * kk + 256], dst[:, k, :]
                eng = dve if m % 2 else act
                if eng is dve:
                    if b_col is None:
                        t = dve.do(lambda e, s_=s_, d_=d_, k=k: e.tensor_scalar(d_, s_, a_col[:, k:k + 1], None,
                                                                                ALU.mult), tok)
                    else:
                        t = dve.do(lambda e, s_=s_, d_=d_, k=k: e.tensor_scalar(
                            d_, s_, a_col[:, k:k + 1], b_col[:, k:k + 1], ALU.mult, ALU.add), tok)
                else:
                    bias = 0.0 if b_col is None else b_col[:, k:k + 1]
                    t = act.do(lambda e, s_=s_, d_=d_, k=k, bias=bias: e.activation(
                        d_, s_, ACT.Identity, bias=bias, scale=a_col[:, k:k + 1]), tok)
                toks.append(t)
            free[b] = [t]
        return toks

    def turned_split(hi, lo, src, a_col, after):
        toks = []
        for m in range(4):
            b, tok = transposes(ALL6, [src[:, i, 128 * (2 * m + kk):128 * (2 * m + kk) + 128]
                                       for kk in range(2) for i in range(2)], after)
            for kk in range(2):
                k = 2 * m + kk
                t1 = act.do(lambda e, k=k, kk=kk, b=b: e.activation(hi[:, k, :], PS[:, b, 256 * kk:256 * kk + 256],
                                                                    ACT.Identity, bias=0.0, scale=a_col[:, k:k + 1]), tok)
            for kk in range(2):
                k = 2 * m + kk
                t = dve.do(lambda e, k=k, kk=kk, b=b: e.scalar_tensor_tensor(
                    out=lo[:, k, :], in0=PS[:, b, 256 * kk:256 * kk + 256], scalar=a_col[:, k:k + 1],
                    in1=hi[:, k, :].bitcast(F32), op0=ALU.mult, op1=ALU.subtract), t1)
                toks.append(t)
            free[b] = [t]
        return toks

    act.wait(t_ab2)
    dve.wait(t_ab2)
    t_h2 = turned(H2T, XN2, ab[:, 4, :], ab[:, 5, :], t_xn2 + [t_mt_used])

    def by_quarters(lr, r_width, after):
        b, fr = bank(ALL6)
        pe.wait(fr, after)
        for m in range(2):
            for q in range(4):
                prods = lr(2 * q + m)
                for n, (l_, r_) in enumerate(prods):
                    tok = pe.do(lambda e, b=b, q=q, l_=l_, r_=r_, st=(m == 0 and n == 0),
                                sp_=(m == 1 and n == len(prods) - 1): e.matmul(
                        PS[32 * q:32 * q + 32, b, 0:r_width], l_, r_, start=st, stop=sp_), mark=(m == 1 and q == 3))
        part = reg(13832 + 0, 256)
        t = dve.do(lambda e, b=b: e.tensor_copy(part, PS[:, b, 0:256]), tok)
        free[b] = [t]
        b2, fr = bank(ALL6)
        pe.wait(fr, t)
        for i in range(2):
            tok = pe.do(lambda e, i=i: e.matmul(PS[:, b2, 16 * i:16 * i + 16], part[:, 128 * i:128 * i + 128], quarters,
                                                start=True, stop=True), mark=i == 1)
        return b2, tok

    b, tok = by_quarters(lambda k: [(WRZ[:, k, :], H2T[:, k, :])], 256, [t_h2, t_wrz])
    mxr, smr, rir = col(2), col(2), col(2)
    aff = col(32).rearrange("p (t e) -> p t e", t=2)
    lg = PS[:, b, 0:32].rearrange("p (t e) -> p t e", t=2)
    t1 = dve.do(lambda e: e.tensor_reduce(mxr, lg, AX.X, ALU.max), tok)
    t1 = dve.do(lambda e: e.tensor_scalar(mxr, mxr, -1.0, None, ALU.mult), t1)
    for i in range(2):
        t1 = act.do(lambda e, i=i, b=b: e.activation(aff[:, i, :], PS[:, b, 16 * i:16 * i + 16], ACT.Exp,
                                                bias=mxr[:, i:i + 1], accum_out=smr[:, i:i + 1]), t1)
    free[b] = [t1]
    t1 = dve.do(lambda e: e.reciprocal(rir, smr), t1)
    t_aff = dve.do(lambda e: e.tensor_tensor(aff, aff, bc(rir, [P, 2, 16], 2), ALU.mult), t1)
    b, fr = bank(ALL6)
    pe.wait(fr, t_aff)
    for i in range(2):
        tok = pe.do(lambda e, i=i, b=b: e.transpose(PS[0:16, b, 128 * i:128 * i + 128], aff[:, i, :], ident), mark=i == 1)
    o0 = 12288
    affT = reg(o0, 256)[0:16]
    wk = [reg(o0 + 256 + 256 * i, 256)[0:16] for i in range(2)]
    cum = reg(o0 + 768, 256)[0:16]
    pg = reg(o0 + 1024, 2, 256)[0:16]
    m8 = reg(o0 + 1536, 8)[0:16]
    t1 = dve.do(lambda e, b=b: e.tensor_copy(affT, PS[0:16, b, 0:256]), tok, t_mixa, t_mixg)
    free[b] = [t1]
    cur = affT
    for r in range(4):
        t1 = dve.do(lambda e, cur=cur: e.max(m8, cur), t1)
        t1 = dve.do(lambda e, cur=cur, r=r: e.match_replace(wk[r % 2], m8, cur, -1.0), t1)
        cur = wk[r % 2]
    sel = wk[0]
    t1 = dve.do(lambda e: e.tensor_scalar(sel, wk[1], -1.0, None, ALU.is_equal), t1)
    t_pgg = dve.do(lambda e: e.tensor_tensor(pg[:, 1, :], affT, sel, ALU.mult), t1)
    t1 = dve.do(lambda e: e.tensor_tensor_scan(cum, sel, sel, 0.0, ALU.add, ALU.bypass), t1)
    t1 = dve.do(lambda e: e.tensor_tensor(pg[:, 0, :], cum, sel, ALU.mult), t1)
    t_pg = dve.do(lambda e: e.tensor_scalar(pg[:, 0, :], pg[:, 0, :], -1.0, None, ALU.add), t1)
    b, fr = bank(ALL6)
    pe.wait(fr, t_pg)
    for i in range(2):
        tok = pe.do(lambda e, i=i, b=b: e.transpose(PS[:, b, 16 * i:16 * i + 16], pg[:, 0, 128 * i:128 * i + 128],
                                                    ident[0:16, 0:16]), mark=i == 1)
    SEL = reg(11264, 2, E, 32)
    post = col(32).rearrange("p (t e) -> p t e", t=2)
    t1 = dve.do(lambda e, b=b: e.tensor_copy(post, PS[:, b, 0:32].rearrange("p (t e) -> p t e", t=2)), tok)
    free[b] = [t1]
    t_sel = []
    for i in range(2):
        t_sel.append(dve.do(lambda e, i=i: e.tensor_tensor(
            SEL[:, i, :, :], bc(post[:, i, :], [P, E, 32], 2), bc(iota, [P, E, 32], 1), ALU.is_equal), t1))

    XE = reg(0, 8, 512)

    def gather(q, group):
        toks = []
        for kh in range(2):
            b, fr = bank(group)
            pe.wait(fr, t_sel)
            for kk in range(4):
                for i in range(2):
                    k = 4 * kh + kk
                    tok = pe.do(lambda e, b=b, i=i, k=k, kk=kk: e.matmul(
                        PS[:, b, 128 * kk:128 * kk + 128], XN2[:, i, 128 * k:128 * k + 128],
                        SEL[:, i, 4 * q:4 * q + 4, :].rearrange("p e s -> p (e s)"),
                        start=(i == 0), stop=(i == 1)), mark=(kk == 3 and i == 1))
            for kk in range(4):
                k = 4 * kh + kk
                s_, d_ = PS[:, b, 128 * kk:128 * kk + 128], XE[:, k, 128 * q:128 * q + 128]
                if kh:
                    t = dve.do(lambda e, s_=s_, d_=d_, k=k: e.tensor_scalar(d_, s_, ab[:, 4, k:k + 1], ab[:, 5, k:k + 1],
                                                                            ALU.mult, ALU.add), tok)
                else:
                    t = act.do(lambda e, s_=s_, d_=d_, k=k: e.activation(d_, s_, ACT.Identity, bias=ab[:, 5, k:k + 1],
                                                                         scale=ab[:, 4, k:k + 1]), tok)
            free[b] = [t]
            toks.append(t)
        return toks

    t_xe = gather(0, ALL6)
    t_xes = {0: t_xe}

    BIA = reg(14336, 8, 256)

    def tables(t_xe):
        t_bia = []
        for h in range(8):
            t_bia.append(pool.do(lambda e, h=h: e.tensor_scalar(BIA[:, h, :], dist, -8.0 * 2.0 ** -(h + 1), None, ALU.mult),
                                 t_wst, t_xe, t_mixg))
        posf = col(2)
        ang = col(32).rearrange("p (t f) -> p t f", t=2)
        nrd = col(32).rearrange("p (t f) -> p t f", t=2)
        C1 = 6.28125
        C2 = float(np.float32(np.float32((2 * np.pi - C1) * 2 ** 20).round() / 2 ** 20))
        C3 = float(np.float32(2 * np.pi - C1 - C2))
        MAG = 12582912.0
        prow = reg(13824, 128)[0:2]
        pflt = reg(13952, 128)[0:2]
        t_pos = load(pool, prow.bitcast(I32), A["positions_2"].rearrange("(t p) -> t p", p=P), t_xe)
        t1 = dve.do(lambda e: e.tensor_copy(pflt, prow.bitcast(I32)), t_pos)
        bp, fr = bank(B4)
        tok = pe.do(lambda e: e.transpose(PS[:, bp, 0:2], pflt, ident[0:2, 0:2]), fr, t1)
        t1 = dve.do(lambda e: e.tensor_copy(posf, PS[:, bp, 0:2]), tok)
        free[bp] = [t1]
        t_ang = None
        for i in range(2):
            t_ang = dve.do(lambda e, i=i: e.tensor_scalar(ang[:, i, :], invf, posf[:, i:i + 1], None, ALU.mult), t1)
        PI_ = 3.1415925
        t_rcs = []
        for n, (quarter, shift) in enumerate(((0.25, float(np.pi / 2)), (0.0, 0.0))):
            r_ = rcs[:, n, :, :]
            t1 = dve.do(lambda e, quarter=quarter: e.tensor_scalar(nrd, ang, float(1 / (2 * np.pi)), quarter,
                                                                   ALU.mult, ALU.add), t_ang, t_rcs)
            t1 = dve.do(lambda e: e.tensor_scalar(nrd, nrd, MAG, None, ALU.add), t1)
            t1 = dve.do(lambda e: e.tensor_scalar(nrd, nrd, MAG, None, ALU.subtract), t1)
            t1 = dve.do(lambda e, r_=r_: e.scalar_tensor_tensor(out=r_, in0=nrd, scalar=-C1, in1=ang,
                                                                op0=ALU.mult, op1=ALU.add), t1)
            for cc in (C2, C3):
                t1 = dve.do(lambda e, r_=r_, cc=cc: e.scalar_tensor_tensor(out=r_, in0=nrd, scalar=-cc, in1=r_,
                                                                           op0=ALU.mult, op1=ALU.add), t1)
            if shift:
                t1 = dve.do(lambda e, r_=r_, shift=shift: e.tensor_scalar(r_, r_, shift, None, ALU.add), t1)
            t1 = dve.do(lambda e, r_=r_: e.tensor_scalar(r_, r_, PI_, -PI_, ALU.min, ALU.max), t1)
            t_rcs.append(act.do(lambda e, r_=r_: e.activation(r_, r_, ACT.Sin), t1))

        return t_bia, t_rcs

    HB = [reg(4096 + 512 * i, 512) for i in range(2)]
    HT = [reg(5120 + 512 * i, 512) for i in range(2)]
    YE = [reg(6144 + 512 * i, 512) for i in range(2)]
    EQ = [reg(7168 + 256 * i, 256) for i in range(2)]
    GT = [reg(7680 + 256 * i, 256) for i in range(2)]
    t_hb, t_ht, t_ye, t_gt = [t_xe] * 2, [t_xe] * 2, [t_xe] * 2, [t_xe] * 2
    t_eq = [t_xe] * 2
    acc_free = [free[b] for b in (4, 5, 6, 7)]
    for b in (4, 5, 6, 7):
        free[b] = None
    gt_tok, ye_tok, t_bank = {}, {}, {}

    def scatter(e_):
        m = e_ % 2
        pe.wait(gt_tok[e_], ye_tok[e_])
        if e_ == 0:
            pe.wait(acc_free)
        for i in range(2):
            for dh in range(2):
                tok = pe.do(lambda e, i=i, dh=dh, m=m: e.matmul(
                    PS[:, 4 + 2 * i + dh, :], GT[m][64 * dh:64 * dh + 64, 128 * i:128 * i + 128],
                    YE[m][64 * dh:64 * dh + 64, :], start=(e_ == 0), stop=(e_ == E - 1)),
                            mark=(e_ == E - 1 or (i == 1 and dh == 1)))
                if e_ == E - 1:
                    t_bank[i, dh] = tok
        t_ye[m] = t_gt[m] = tok
        return tok

    def up(name, e_, b):
        for k in range(4):
            w = weight((name, e_, k))
            for kk in range(2):
                for j in range(4):
                    tok = pe.do(lambda e, w=w, k=k, kk=kk, j=j: e.matmul(
                        PS[32 * j:32 * j + 32, b, :], XE[:, 2 * k + kk, 32 * e_:32 * e_ + 32],
                        w[:, kk, 512 * j:512 * j + 512],
                        start=(k == 0 and kk == 0), stop=(k == 3 and kk == 1)), mark=(kk == 1 and j == 3))
            t_used[(name, e_, k)] = tok
        return tok

    pe.wait(t_xe)
    for e_ in range(E):
        m = e_ % 2
        if e_ == 4:
            t_bia, t_rcs = tables(t_xes[3])
        pe.wait(t_xes[e_ // 4])
        b1, fr = bank(B4)
        pe.wait(fr)
        tok = up("w1", e_, b1)
        t_s = act.do(lambda e, b1=b1, m=m: e.activation(HB[m], PS[:, b1, :], ACT.Silu), tok, t_hb[m])
        free[b1] = [t_s]
        b, fr = bank(B4)
        tok = pe.do(lambda e, b=b, e_=e_: e.matmul(PS[:, b, :], ident[0:16, e_:e_ + 1].to_broadcast([16, 128]),
                                                   pg.rearrange("p a t -> p (a t)"), start=True, stop=True),
                    fr, t_pg, t_pgg)
        t1 = dve.do(lambda e, b=b, m=m: e.tensor_scalar(EQ[m], PS[:, b, 0:256], slotc, None, ALU.is_equal), tok, t_eq[m])
        t1 = dve.do(lambda e, b=b, m=m: e.tensor_tensor(GT[m], PS[:, b, 256:512], EQ[m], ALU.mult), t1, t_gt[m])
        t_eq[m] = gt_tok[e_] = t1
        free[b] = [t1]
        b3, fr = bank(B4)
        pe.wait(fr)
        if e_:
            scatter(e_ - 1)
        tok = up("w3", e_, b3)
        t_h = dve.do(lambda e, b3=b3, m=m: e.tensor_tensor(HB[m], PS[:, b3, :], HB[m], ALU.mult), tok, t_s)
        free[b3] = [t_h]
        b, tok = transposes(B4, [HB[m][:, 128 * s:128 * s + 128] for s in range(4)], t_h)
        t_hb[m] = tok
        t_t = act.do(lambda e, b=b, m=m: e.activation(HT[m], PS[:, b, :], ACT.Copy), tok, t_ht[m])
        free[b] = [t_t]
        b, fr = bank(B4)
        pe.wait(fr, t_t)
        for j in range(4):
            w = weight(("w2", e_, j))
            for s in range(4):
                for dh in range(2):
                    q = 64 * dh + 32 * (s % 2)
                    tok = pe.do(lambda e, b=b, w=w, j=j, s=s, dh=dh, q=q, m=m: e.matmul(
                        PS[q:q + 32, b, :], HT[m][:, 128 * s + 32 * j:128 * s + 32 * j + 32],
                        w[:, s, 512 * dh:512 * dh + 512], start=(j == 0 and s < 2), stop=(j == 3 and s >= 2)),
                        mark=(s == 3 and dh == 1))
            t_used[("w2", e_, j)] = tok
        t_ht[m] = tok
        ye_tok[e_] = dve.do(lambda e, b=b, m=m: e.tensor_tensor(YE[m], PS[:, b, :], G2, ALU.mult), tok, t_ye[m], t_g2)
        free[b] = [ye_tok[e_]]
        if e_ < 3:
            t_xes[e_ + 1] = gather(e_ + 1, B4)

    t_acc = scatter(E - 1)

    XN3 = reg(2048, 2, D)
    ssx, ssy = col(4), col(4)
    rs_, ra_ = col(2), col(2)
    tok, t_y = None, []
    e_pieces = split_steps(("e", "a"), dve)
    for i in range(2):
        for dh in range(2):
            n = 2 * dh + i
            c = slice(512 * dh, 512 * dh + 512)
            t1 = dve.do(lambda e, i=i, dh=dh, c=c: e.tensor_tensor(X[:, i, c], PS[:, 4 + 2 * i + dh, :], X[:, i, c],
                                                                   ALU.add), t_bank[i, dh])
            free[4 + 2 * i + dh] = [t1]
            tok = act.do(lambda e, i=i, c=c, n=n: e.activation(reg(0, 512), X[:, i, c], ACT.Square,
                                                               scale=float(D) ** -0.5, accum_out=ssx[:, n:n + 1]),
                         t1, tok)
            t_sx = tok
            t2 = dve.do(lambda e, i=i, c=c: e.tensor_tensor(XN3[:, i, c], X[:, i, c], gfb[:, c], ALU.mult), t1, t_gf)
            t_y.append(t2)
            tok = act.do(lambda e, i=i, c=c, n=n: e.activation(reg(0, 512), XN3[:, i, c], ACT.Square,
                                                               scale=float(D) ** -0.5, accum_out=ssy[:, n:n + 1]),
                         t2, tok)
    t2 = pool.do(lambda e: e.tensor_tensor(rs_, ssx[:, 0:2], ssx[:, 2:4], ALU.add), t_sx)
    t2 = pool.do(lambda e: e.tensor_scalar(rs_, rs_, EPS, None, ALU.add), t2)
    t1 = pool.do(lambda e: e.tensor_scalar(ra_, rs_, EPS, None, ALU.mult), t2)
    t1 = pool.do(lambda e: e.tensor_tensor(ra_, ra_, ssy[:, 0:2], ALU.add), t1, tok)
    t1 = pool.do(lambda e: e.tensor_tensor(ra_, ra_, ssy[:, 2:4], ALU.add), t1)
    t2 = pool.do(lambda e: e.tensor_tensor(ra_, ra_, KC[:, K_HALF:K_HALF + 2], ALU.pow), t1)
    t1 = pool.do(lambda e: e.tensor_tensor(rs_, rs_, KC[:, K_HALF:K_HALF + 2], ALU.pow), t2)
    XF = reg(6144, 2, D)
    e_pieces.pop(0)()
    t_n = [dve.do(lambda e: e.tensor_scalar(XF[:, 0, :], XN3[:, 0, :], ra_[:, 0:1], None, ALU.mult), t2, t_y),
           act.do(lambda e: e.activation(XF[:, 1, :], XN3[:, 1, :], ACT.Copy, scale=ra_[:, 1:2]), t2, t_y)]
    t_xf = [pool.do(lambda e, i=i: e.tensor_scalar(X[:, i, :], XN3[:, i, :], rs_[:, i:i + 1], None, ALU.mult), t1, t_y)
            for i in range(2)]

    def extra(off, k):
        return EXTRA[:, off:off + 256 * k].rearrange("p (k t) -> p k t", k=k)

    for piece in e_pieces:
        piece()
    HE = (regr(4096, 8, 256), extra(0, 8))
    t_HE = turned_split(*HE, XF, c_ge, t_n + [t_acc])
    split(("e", "qs"), dve)

    ZA = reg(0, 2, 416)
    t_za = []
    ssa, rsa = col(4), col(4)
    jk = reg(1024, 256)
    tj = None
    for i in range(2):
        b, tok = project(("e", "a"), HE, i, 416, ALL6, after=[t_HE])
        tz = dve.do(lambda e, b=b, i=i: e.tensor_copy(ZA[:, i, :], PS[:, b, 0:416]), tok, t_n)
        free[b] = [tz]
        tj = act.do(lambda e, i=i: e.activation(jk, ZA[:, i, 0:256], ACT.Square, scale=1.0 / 16,
                                                accum_out=ssa[:, 2 * i:2 * i + 1]), tz, tj, t_n)
        tj = act.do(lambda e, i=i: e.activation(jk[:, 0:128], ZA[:, i, 256:384], ACT.Square, scale=128.0 ** -0.5,
                                                accum_out=ssa[:, 2 * i + 1:2 * i + 2]), tj)
    t1 = rstd(rsa, ssa, tj)
    ahead(("e", "a"), pool)
    for i in range(2):
        t_za.append(dve.do(lambda e, i=i: e.tensor_scalar(ZA[:, i, 0:256], ZA[:, i, 0:256], rsa[:, 2 * i:2 * i + 1],
                                                          None, ALU.mult), t1))
        t_za.append(dve.do(lambda e, i=i: e.tensor_scalar(ZA[:, i, 256:384], ZA[:, i, 256:384],
                                                          rsa[:, 2 * i + 1:2 * i + 2], None, ALU.mult), t1))
    QST = reg(12800, 4, 256)
    KST = reg(3584, 2, 256)
    t_qst = []

    def straight_bank(key, h, n2):
        b, fr = bank(ALL6)
        pe.wait(fr)
        for nn in range(2):
            n = 2 * n2 + nn
            for k in range(8):
                pe.wait(ready[key][k])
                for m, (l_, r_) in enumerate(passes(key, h, k, slice(128 * n, 128 * n + 128), slice(0, 256), swap=True)):
                    tok = pe.do(lambda e, l_=l_, r_=r_, nn=nn, st=(k == 0 and m == 0), sp_=(k == 7 and m == 2): e.matmul(
                        PS[:, b, 256 * nn:256 * nn + 256], l_, r_, start=st, stop=sp_),
                                mark=(nn == 1 and k == 7 and m == 2))
        t_used[key] = tok
        return b, tok

    for n2 in range(2):
        b, tok = straight_bank(("e", "qs"), HE, n2)
        t = evac(QST[:, 2 * n2:2 * n2 + 2, :], PS[:, b, :].rearrange("p (n t) -> p n t", n=2), tok, t_acc)
        free[b] = [t]
        t_qst.append(t)
    ahead(("e", "qs"), pool)
    b, fr = bank(ALL6)
    pe.wait(fr)
    for k in range(8):
        pe.wait(ready[("e", "kvs")][k])
        for m, (l_, r_) in enumerate(passes(("e", "kvs"), HE, k, slice(0, 128), slice(0, 256), swap=True)):
            tok = pe.do(lambda e, b=b, l_=l_, r_=r_, st=(k == 0 and m == 0), sp_=(k == 7 and m == 2): e.matmul(
                PS[:, b, 0:256], l_, r_, start=st, stop=sp_), mark=(k == 7 and m == 2))
    t_kst = None
    for g in range(2):
        for r in range(2):
            t_kst = dve.do(lambda e, b=b, g=g, r=r: e.tensor_copy(KST[64 * r:64 * r + 64, g, :],
                                                                  PS[64 * g:64 * g + 64, b, 0:256]), tok, t_HE, t_xf)
    free[b] = [t_kst]
    VS = reg(14080, 2, 128)
    t_vs = []
    for i in range(2):
        b, tok = project(("e", "kvs"), HE, i, 128, ALL6, o=128)
        t_vs.append(act.do(lambda e, b=b, i=i: e.activation(VS[:, i, :], PS[:, b, 0:128], ACT.Copy), tok, t_rcs))
        free[b] = [t_vs[-1]]
    CT = (regr(1024 + 256, 3, 256), extra(2048, 3))
    t_ct = []
    for kk in range(3):
        b, tok = transposes(ALL6, [ZA[:, i, 128 * kk:128 * kk + 128] for i in range(2)], t_za)
        g_ = c_qa[:, kk:kk + 1] if kk < 2 else c_kva
        t1 = act.do(lambda e, b=b, kk=kk, g_=g_: e.activation(CT[0][:, kk, :], PS[:, b, 0:256],
                                                              ACT.Identity, bias=0.0, scale=g_), tok, t_n)
        t_ct.append(dve.do(lambda e, b=b, kk=kk, g_=g_: e.scalar_tensor_tensor(
            out=CT[1][:, kk, :], in0=PS[:, b, 0:256], scalar=g_, in1=CT[0][:, kk, :].bitcast(F32),
            op0=ALU.mult, op1=ALU.subtract), t1, t_acc))
        free[b] = [t_ct[-1]]
    ahead(("e", "kvs"), pool)
    KP = col(64).rearrange("p (t f) -> p t f", t=2)
    rtmp = reg(13824, 2, 8, 16)
    kt2 = [rtmp[:, a, 0:2, :] for a in range(2)]
    cs, sn = rcs[:, 0, :, :], rcs[:, 1, :, :]
    t_kp = rope(KP[:, :, 0:16], KP[:, :, 16:32], ZA[:, :, 384:400], ZA[:, :, 400:416], cs, sn, sn, cs, kt2,
                t_rcs, t_za, t_acc)
    QK = reg(2048, 2, 8, 96)
    KM = reg(8192, 2, 8, 96)
    VM = reg(9728, 2, 8, 64)
    QMT = reg(10752, 8, 256)
    t_qk, t_km, t_vm = [], [], []
    for i in range(2):
        for o, w, h0, hn in ((0, 480, 0, 5), (480, 288, 5, 3)):
            b, tok = project(("qup",), CT, i, w, ALL6, k8=2, o=o, after=[t_ct])
            v = PS[:, b, 0:w].rearrange("p (h d) -> p h d", d=96)
            ta = act.do(lambda e, v=v, i=i, h0=h0, hn=hn: e.activation(QK[:, i, h0:h0 + hn, 0:64], v[:, :, 0:64], ACT.Copy),
                        tok, t_HE, t_xf)
            tm = [rtmp[:, a, 0:hn, :] for a in range(2)]
            tr_ = rope(QK[:, i, h0:h0 + hn, 64:80], QK[:, i, h0:h0 + hn, 80:96], v[:, :, 64:80], v[:, :, 80:96],
                       bc(cs[:, i, :], [P, hn, 16], 1), bc(sn[:, i, :], [P, hn, 16], 1),
                       bc(sn[:, i, :], [P, hn, 16], 1), bc(cs[:, i, :], [P, hn, 16], 1), tm, ta, t_kp)
            free[b] = tr_
            t_qk += [ta] + tr_
            t_kp = tr_ + t_kp
    for i in range(2):
        for o in range(2):
            b, tok = project(("kvup",), (CT[0][:, 2:3, :], CT[1][:, 2:3, :]), i, 512, ALL6, k8=1, o=512 * o)
            v = PS[:, b, :].rearrange("p (h d) -> p h d", d=128)
            ta = act.do(lambda e, v=v, i=i, o=o: e.activation(KM[:, i, 4 * o:4 * o + 4, 0:64], v[:, :, 0:64], ACT.Copy),
                        tok, t_acc)
            tb = act.do(lambda e, v=v, i=i, o=o: e.activation(VM[:, i, 4 * o:4 * o + 4, :], v[:, :, 64:128], ACT.Copy))
            free[b] = [tb]
            t_km.append(ta)
            t_vm.append(tb)
        t_km.append(dve.do(lambda e, i=i: e.tensor_copy(KM[:, i, :, 64:96], bc(KP[:, i, :], [P, 8, 32], 1)),
                           t_kp, t_acc))
    ahead(("qup",), pool)
    SGT = SG[:].rearrange("p t (a b) -> p (t a) b", a=4)

    def gate_steps(key, h, lst, after):
        held = []

        def step(n2, q):
            if q == 0:
                b, fr = bank(ALL6)
                held.append(b)
                pe.wait(fr)
            b = held[n2]
            nn = q // 2
            n = 2 * n2 + nn
            for k in range(4 * (q % 2), 4 * (q % 2) + 4):
                pe.wait(ready[key][k])
                for m, (l_, r_) in enumerate(passes(key, h_src, k, slice(128 * n, 128 * n + 128), slice(0, 256),
                                                    swap=True)):
                    tok = pe.do(lambda e, l_=l_, r_=r_, st=(k == 0 and m == 0), sp_=(k == 7 and m == 2): e.matmul(
                        PS[:, b, 256 * nn:256 * nn + 256], l_, r_, start=st, stop=sp_), mark=(k % 4 == 3 and m == 2))
            t_used[key] = tok
            if q == 3:
                d = SGT[:, 4 * h + 2 * n2:4 * h + 2 * n2 + 2, :]
                v = PS[:, b, :].rearrange("p (n t) -> p n t", n=2)
                t = act.do(lambda e: e.activation(d, v, ACT.Tanh, scale=0.5), tok, after)
                t = dve.do(lambda e: e.scalar_tensor_tensor(out=d, in0=d, scalar=1.0, in1=v, op0=ALU.add, op1=ALU.mult), t)
                free[b] = [t]
                lst[(h, n2)] = t

        h_src = HE if key[0] == "e" else HO
        return [lambda n2=n2, q=q: step(n2, q) for n2 in range(2) for q in range(4)]

    def with_splits(steps, first, second_):

        def both(a, b_):
            def run():
                a()
                b_()

            return run

        more = split_steps(first, pool)
        return steps[:8] + [both(a, b_) for a, b_ in zip(steps[8:12], more)] + steps[12:] + split_steps(second_, pool)

    t_sg = {}
    gates = [g for h in (1, 0) for g in gate_steps(("e", f"g{h}"), h, t_sg, t_xf)]
    gates = with_splits(gates, ("out2", 0), ("out2", 1))
    for _ in range(4):
        gates.pop(0)()
    KMT = reg(0, 8, 256)
    t_qmt, t_kmt = [], []
    for src, dst, lst, aft in ((QK, QMT, t_qmt, t_qk), (KM, KMT, t_kmt, t_km)):
        for hp in range(4):
            b, tok = transposes(ALL6, [src[:, i, 2 * hp + hh, :] for hh in range(2) for i in range(2)], aft, parts=96)
            t = evac(dst[0:96, 2 * hp:2 * hp + 2, :], PS[0:96, b, :].rearrange("p (h t) -> p h t", h=2), tok,
                     t_acc, t_qk, t_km, t_vm)
            free[b] = [t]
            lst.append(t)

    def masked(hs, nk, cols, bias, scale, mx, nm, sm, lower=None, shift=None, first=None):

        def soft(b, p, tok, before):
            for q, h in enumerate(hs):
                c = slice(q * nk, q * nk + nk)
                i_ = cols.start + q * cols.step
                t1 = dve.do(lambda e, c=c, h=h, i_=i_: e.tensor_tensor_reduce(
                    p[:, c], PS[:, b, c], bias(h), scale, -3.0e38, ALU.add, ALU.max, mx[:, i_:i_ + 1]),
                            tok, before, first)
            t_fr = t1
            if lower is not None:
                t1 = dve.do(lambda e: e.tensor_tensor(nm[:, cols], mx[:, cols], lower, ALU.max), t1)
                t1 = dve.do(lambda e: e.tensor_scalar(nm[:, cols], nm[:, cols], -1.0, None, ALU.mult), t1)
            elif shift is not None:
                t1 = dve.do(lambda e: e.tensor_tensor(nm[:, cols], mx[:, cols], shift, ALU.add), t1)
                t1 = dve.do(lambda e: e.scalar_tensor_tensor(out=nm[:, cols], in0=nm[:, cols], scalar=-1.0, in1=shift,
                                                             op0=ALU.mult, op1=ALU.add), t1)
            else:
                t1 = dve.do(lambda e: e.tensor_scalar(nm[:, cols], mx[:, cols], -1.0, None, ALU.mult), t1)
            for q, h in enumerate(hs):
                c = slice(q * nk, q * nk + nk)
                i_ = cols.start + q * cols.step
                t_e = act.do(lambda e, c=c, i_=i_: e.activation(p[:, c], p[:, c], ACT.Exp, bias=nm[:, i_:i_ + 1],
                                                                accum_out=sm[:, i_:i_ + 1]), t1)
            if lower is not None:
                t1 = dve.do(lambda e: e.tensor_tensor(esk[:, cols], lower, nm[:, cols], ALU.add), t1)
                t_e = act.do(lambda e: e.activation(esk[:, cols], esk[:, cols], ACT.Exp), t1)
            return t_e, t_fr

        def scale_(p, t_e):
            t1 = None
            if lower is not None:
                t1 = dve.do(lambda e: e.tensor_tensor(sm[:, cols], sm[:, cols], esk[:, cols], ALU.add), t_e)
            t1 = dve.do(lambda e: e.reciprocal(sm[:, cols], sm[:, cols]), t_e, t1)
            for q in range(len(hs)):
                c = slice(q * nk, q * nk + nk)
                i_ = cols.start + q * cols.step
                t = dve.do(lambda e, c=c, i_=i_: e.tensor_scalar(p[:, c], p[:, c], sm[:, i_:i_ + 1], None, ALU.mult), t1)
            return t

        return soft, scale_

    n_tmp = [0]

    def outputs(dst, i, half, ob, gate, lst, after=None):

        def done(tok):
            tmp = bm[:, n_tmp[0] % 2, :].rearrange("p (n t) -> p n t", n=4)
            n_tmp[0] += 1
            c = slice(128 * i, 128 * i + 128)
            hi, lo = [d[:, 4 * half:4 * half + 4, c] for d in dst]
            t1 = dve.do(lambda e: e.tensor_tensor(tmp, PS[:, ob, :].rearrange("p (n t) -> p n t", n=4),
                                                  SGT[:, 4 * half:4 * half + 4, c], ALU.mult), tok, gate[(half, 0)],
                        gate[(half, 1)], lst, t_g2)
            free[ob] = [t1]
            t1 = act.do(lambda e: e.activation(hi, tmp, ACT.Copy, scale=0.5), t1, after)
            lst.append(dve.do(lambda e: e.scalar_tensor_tensor(out=lo, in0=tmp, scalar=0.5, in1=hi.bitcast(F32),
                                                               op0=ALU.mult, op1=ALU.subtract), t1, after))

        return done

    OT = (regr(6144, 8, 256), extra(2048, 8))
    mx2, nm2, sm2 = [col(16) for _ in range(3)]
    mx3, nm3, sm3 = mx1, nm1, sm1
    esk = col(16)
    t_o2 = []
    t_c2 = [t_qk, t_km]
    pairs = []
    n_o = 0
    for part, i in (("swa", 0), ("swa", 1), ("mla", 1), ("mla", 0)):
        nk = 128 * (i + 1)
        per = 512 // nk
        ob = OB[n_o % 2]
        n_o += 1
        for h0 in range(0, 8, 2 * per):
            two = []
            for odd in range(2):
                hs = list(range(h0 + odd, h0 + odd + 2 * per, 2))
                cols = slice(8 * i + hs[0], 8 * i + hs[-1] + 1, 2)
                hd = []
                for h in hs:
                    if part == "mla":
                        def score(b, c, i=i, h=h, nk=nk):
                            pe.wait(t_qmt, t_kmt)
                            return pe.do(lambda e: e.matmul(PS[:, b, c:c + nk], QMT[0:96, h, 128 * i:128 * i + 128],
                                                            KMT[0:96, h, 0:nk], start=True, stop=True))
                        vals = [VM[:, s_, h, :] for s_ in range(i + 1)]
                    else:
                        def score(b, c, i=i, h=h, nk=nk, r=64 * (h % 2)):
                            pe.wait(t_qst, t_kst)
                            return pe.do(lambda e: e.matmul(
                                PS[:, b, c:c + nk], QST[r:r + 64, h // 2, 128 * i:128 * i + 128],
                                KST[r:r + 64, h // 4, 0:nk], start=True, stop=True))
                        vals = [VS[:, s_, 64 * (h // 4):64 * (h // 4) + 64] for s_ in range(i + 1)]
                    hd.append((score, vals, PS[64 * (h % 2):64 * (h % 2) + 64, ob, 128 * (h // 2):128 * (h // 2) + 128]))
                if part == "mla":
                    soft, scale_ = masked(hs, nk, cols, lambda h, nk=nk: cmask[:, 256 - nk:256], 96.0 ** -0.5, mx2, nm2, sm2,
                                  first=t_c2)
                else:
                    soft, scale_ = masked(hs, nk, cols, lambda h, nk=nk: BIA[:, h, 256 - nk:256], 0.125, mx3, nm3, sm3,
                                  lower=sinkb[:, hs[0]:hs[-1] + 1:2], first=[t_bia, t_sk])
                ld = dict(nk=nk, heads=hd, soft=soft, scale=scale_, flip=True, wait=[t_vm, t_vs])
                if h0 == 0 and odd == 0:
                    ld["wait"] = [t_vm, t_vs, lambda ob=ob: free[ob]]
                if hs[-1] == 7:
                    ld["done"] = outputs(OT, i, 0 if part == "mla" else 1, ob, t_sg, t_o2, [t_ct, t_qk, t_km])
                two.append(ld)
            pairs.append(two)
    attention(pairs, [reg(o, 512) for o in (2048, 2560, 3072, 9216)], [reg(8192, 512), reg(8704, 512)],
              [t_qmt, t_kmt], gates)

    t_OT = t_o2

    def residual(name, src_t, after):
        toks = []
        for h in range(2):
            for i in range(2):
                b, tok = project((name, h), src_t, i, 512, ALL6, after=[after])
                c = slice(512 * h, 512 * h + 512)
                t1 = dve.do(lambda e, b=b, i=i, c=c: e.tensor_tensor(X[:, i, c], PS[:, b, :], X[:, i, c], ALU.add), tok)
                free[b] = [t1]
                toks.append(t1)
            if h == 0:
                ahead((name, 0), dve)
        return toks

    t_x3 = residual("out2", OT, t_OT)
    t_ot_used = t_used[("out2", 1)]

    NC_ = regr(14592, 256)
    WFZ = reg(14848, 8, 32)
    KQR = regr(15488, 16)
    t_zero = pool.do(lambda e: e.tensor_scalar(NC_, cmask, 0.0, None, ALU.mult), t_o2, t_bia)
    t_wfz = pool.do(lambda e: e.memset(WFZ, 0.0), t_o2, t_bia)
    t_wfz = pool.do(lambda e: e.tensor_copy(WFZ[:, :, 0:16], wf[:]), t_wfz, t_wf)
    t_kq = act.do(lambda e: e.activation(KQR, quarters, ACT.Copy), t_zero)
    XN4 = reg(8192, 2, D)
    t_n = normalise(XN4, X, t_x3, 12800, [t_o2])
    HO = (regr(0, 8, 256), extra(0, 8))
    t_HO = turned_split(*HO, XN4, c_go, t_n + [t_x3])
    fl = col(32).rearrange("p (t h) -> p t h", t=2)
    F1 = reg(14336, 2, 16)
    F2 = reg(14368, 2, 16)
    F3 = reg(14400, 2, 16)
    F4 = reg(14432, 2, 16)
    F5 = reg(14464, 2, 16)
    def straight(nm, dst, after):
        toks = []
        for n2 in range(2):
            b, tok = straight_bank(("o", nm), HO, n2)
            t = evac(dst[:, 2 * n2:2 * n2 + 2, :], PS[:, b, :].rearrange("p (n t) -> p n t", n=2), tok, after)
            free[b] = [t]
            toks.append(t)
        return toks

    ahead(("out2", 1), dve)
    QF = reg(2048, 8, 256)
    pe.wait(t_HO)
    t_qf = straight("q0", QF[:, 0:4, :], t_x3)
    b, tok = by_quarters(lambda k: [(WFZ[:, k, :], h_[:, k, :].bitcast(F32)) for h_ in HO], 256, [t_HO, t_wfz])
    ahead(("o", "q0"), dve)
    t1 = dve.do(lambda e, b=b: e.tensor_tensor(F1, PS[:, b, 0:32].rearrange("p (t h) -> p t h", t=2),
                                          bc(bfb[:], [P, 2, 16], 1), ALU.add), tok, t_bf, t_x3, t_bia)
    free[b] = [t1]
    t1 = dve.do(lambda e: e.tensor_scalar(F2, F1, -1.0, None, ALU.mult), t1)
    t1 = dve.do(lambda e: e.tensor_tensor(F2, F1, F2, ALU.min), t1)
    t1 = act.do(lambda e: e.activation(F2, F2, ACT.Exp), t1)
    t_u1 = dve.do(lambda e: e.tensor_scalar(F3, F2, 1.0, None, ALU.add), t1)
    t_ln = act.do(lambda e: e.activation(F4, F3, ACT.Ln), t_u1)
    t1 = dve.do(lambda e: e.tensor_scalar(F3, F3, -1.0, None, ALU.add), t_ln)
    t1 = dve.do(lambda e: e.tensor_scalar(F5, F3, 0.0, None, ALU.is_equal), t1)
    t1 = dve.do(lambda e: e.tensor_tensor(F3, F3, F5, ALU.add), t1)
    t1 = dve.do(lambda e: e.tensor_tensor(F4, F4, F5, ALU.add), t1)
    t1 = dve.do(lambda e: e.reciprocal(F3, F3), t1)
    t1 = dve.do(lambda e: e.tensor_tensor(F4, F4, F3, ALU.mult), t1)
    t1 = dve.do(lambda e: e.tensor_tensor(F4, F4, F2, ALU.mult), t1)
    t1 = dve.do(lambda e: e.tensor_scalar(F1, F1, 0.0, None, ALU.min), t1)
    t_lf = dve.do(lambda e: e.tensor_tensor(F1, F1, F4, ALU.subtract), t1)

    t_qf += straight("q1", QF[:, 4:8, :], t_x3)
    ahead(("o", "q1"), dve)
    KF = reg(4096, 8, 256)
    t_kf = straight("k0", KF[:, 0:4, :], t_x3)
    b, fr = bank(ALL6)
    pe.wait(fr, t_lf)
    pe.do(lambda e, b=b: e.matmul(PS[:, b, 0:16], tri, F1[:, 0, :], start=True, stop=True), mark=False)
    pe.do(lambda e, b=b: e.matmul(PS[:, b, 16:32], tri, F1[:, 1, :], start=True, stop=False), mark=False)
    tok = pe.do(lambda e, b=b: e.matmul(PS[:, b, 16:32], ones, F1[:, 0, :], start=False, stop=True))
    t_cs = dve.do(lambda e, b=b: e.tensor_copy(fl, PS[:, b, 0:32].rearrange("p (t h) -> p t h", t=2)), tok)
    free[b] = [t_cs]
    b, fr = bank(ALL6)
    pe.wait(fr, t_cs)
    for i in range(2):
        tok = pe.do(lambda e, i=i, b=b: e.transpose(PS[0:16, b, 128 * i:128 * i + 128], fl[:, i, :], ident), mark=i == 1)
    for r in (0, 64):
        t1 = dve.do(lambda e, b=b, r=r: e.tensor_scalar(NC_[r:r + 16], PS[0:16, b, 0:256], -8.0, None, ALU.mult),
                    tok, t_zero)
        t_nc = dve.do(lambda e, b=b, r=r: e.scalar_tensor_tensor(
            out=NC_[r + 32:r + 48], in0=PS[0:16, b, 0:256], scalar=-8.0, in1=NC_[0:16].bitcast(F32),
            op0=ALU.mult, op1=ALU.subtract), t1)
    free[b] = [t_nc]
    ahead(("o", "k0"), dve)
    t_kf += straight("k1", KF[:, 4:8, :], t_x3)
    ahead(("o", "k1"), dve)
    VF = reg(6144, 2, D)
    t_vf = []
    for h in range(2):
        for i in range(2):
            b, tok = project(("o", f"v{h}"), HO, i, 512, ALL6)
            t_vf.append(evac(VF[:, i, 512 * h:512 * h + 512], PS[:, b, :], tok, t_x3, t_OT))
            free[b] = [t_vf[-1]]
        ahead(("o", f"v{h}"), dve)
    OT3 = (regr(10752, 8, 256), extra(2048, 8))
    t_sg2 = {}
    gates = [g for h in range(2) for g in gate_steps(("o", f"g{h}"), h, t_sg2, t_o2)]
    gates = with_splits(gates, ("out3", 0), ("out3", 1))
    for _ in range(4):
        gates.pop(0)()
    mx4, nm4, sm4 = [reg(15360 + 32 * i, 32) for i in range(3)]
    t_o3 = []
    pairs = []
    n_o = 0
    for half, i in ((0, 0), (0, 1), (1, 1), (1, 0)):
        nk = 128 * (i + 1)
        per = 512 // nk
        ob = OB[n_o % 2]
        n_o += 1
        for h0 in range(8 * half, 8 * half + 8, 2 * per):
            two = []
            for odd in range(2):
                hs = list(range(h0 + odd, h0 + odd + 2 * per, 2))
                cols = slice(16 * i + hs[0], 16 * i + hs[-1] + 1, 2)
                hd = []
                for h in hs:
                    def score(b, c, i=i, h=h, nk=nk, r=64 * (h % 2)):
                        pe.wait(t_qf, t_kf, t_nc, t_kq)
                        pe.do(lambda e: e.matmul(PS[:, b, c:c + nk], QF[r:r + 64, h // 2, 128 * i:128 * i + 128],
                                                 KF[r:r + 64, h // 2, 0:nk], start=True, stop=False), mark=False)
                        return pe.do(lambda e: e.matmul(PS[:, b, c:c + nk], KQR[r:r + 48, h:h + 1].to_broadcast([48, 128]),
                                                        NC_[r:r + 48, 0:nk], start=False, stop=True))
                    hd.append((score, [VF[:, s_, 64 * h:64 * h + 64] for s_ in range(i + 1)],
                               PS[64 * (h % 2):64 * (h % 2) + 64, ob, 128 * (h % 8 // 2):128 * (h % 8 // 2) + 128]))
                soft, scale_ = masked(hs, nk, cols, lambda h, nk=nk: cmask[:, 256 - nk:256], 0.125, mx4, nm4, sm4,
                              shift=fl[:, i, hs[0]:hs[-1] + 1:2], first=[t_x3, t_HO, t_bia])
                ld = dict(nk=nk, heads=hd, soft=soft, scale=scale_, flip=True, wait=[t_vf])
                if h0 % 8 == 0 and odd == 0:
                    ld["wait"] = [t_vf, lambda ob=ob: free[ob]]
                if hs[-1] % 8 == 7:
                    ld["done"] = outputs(OT3, i, half, ob, t_sg2, t_o3, [t_x3])
                two.append(ld)
            pairs.append(two)
    attention(pairs, [reg(8192 + 512 * n, 512) for n in range(4)], [reg(12800, 512), reg(13312, 512)],
              [t_HO], gates)
    g2b = reg(4096, D)
    t_gf2 = load(pool, g2b, A["g_final_2"].partition_broadcast(P), t_o3)
    t_OT3 = t_o3
    t_x4 = residual("out3", OT3, t_OT3)
    ssf, tok = quarter_squares(X, t_x4, 8192, [t_o3])
    rsf = col(2)
    t1 = quarter_rstd(rsf, ssf, tok)
    s_out = sem("s_out")
    for i in range(2):
        t = dve.do(lambda e, i=i: e.scalar_tensor_tensor(out=X[:, i, :], in0=X[:, i, :], scalar=rsf[:, i:i + 1],
                                                         in1=g2b, op0=ALU.mult, op1=ALU.mult), t1, t_gf2)
        act.dma(s_out, 0, lambda e, i=i: e.dma_start(out.rearrange("(t p) d -> p t d", p=P)[:, i, :], X[:, i, :]), t)
    act.wait((s_out, 32))

    ring_loads()

    block = ctx.enter_context(nc.Block())

    @block.sync
    def _(eng):
        sp.emit(eng)

    @block.tensor
    def _(eng):
        pe.emit(eng)

    @block.vector
    def _(eng):
        dve.emit(eng)

    @block.scalar
    def _(eng):
        act.emit(eng)

    @block.gpsimd
    def _(eng):
        pool.emit(eng)


DROP = {"c": 1, "b_mod": 1, "g_mix": 1, "g_ffn": 1, "w_mod": 1, "w_in": 1, "q_gain": 1, "k_gain": 1, "v_gain": 1,
        "w_s": 1, "b_s": 1, "w_out": 1, "w_router": 1, "w1": 1, "w3": 1, "w2": 1, "x": 1, "ctx": 1, "positions_2": 1,
        "e_g_in_2": 1, "e_w_in_2": 1, "e_g_q_a_2": 1, "e_w_q_up_2": 1, "e_g_kv_a_2": 1, "e_w_kv_up_2": 1,
        "e_sinks_2": 1, "e_w_out_2": 1, "o_g_in_2": 1, "o_w_in_2": 1, "o_b_f_2": 1, "o_w_out_2": 1}


def kernel(**inputs):
    import concourse.bacc as bacc
    from concourse.bass_utils import run_bass_kernel_spmd as run

    nc = bacc.Bacc("TRN2", target_bir_lowering=False, num_devices=1)
    arrays, aps = {}, {}
    for name in INS:
        a = np.ascontiguousarray(inputs[name])
        arrays["in_" + name] = a
        ap = nc.dram_tensor("in_" + name, a.shape, mybir.dt.from_np(a.dtype), kind="ExternalInput").ap()
        aps[name] = ap[0] if name in DROP else ap
    k = constants()
    arrays["in_consts"] = k
    kin = nc.dram_tensor("in_consts", k.shape, F32, kind="ExternalInput").ap()
    o = nc.dram_tensor("out_0", (1, T, D), F32, kind="ExternalOutput").ap()
    program(nc, aps, kin, o[0])
    r = run(nc, [arrays], core_ids=[0])
    return r.results[0]["out_0"]
```
